# Optimizing a Trainium2 kernel written in Bass

```python
import math
import jax
import jax.numpy as jnp
from jax import lax
import numpy as np
import jax, jax.numpy as jnp

D_MODEL = 1024
BATCH = 1
SEQ = 256
DEPTH = 2

GRID_W = 64
CTX_LEN = 256
BLOCK = 128
WINDOW = 128
ROPE_THETA = 10000.0
A_HQ = 8
A_HKV = 2
A_HD = 64
B_H = 4
B_HD = 64
B_VD = 2 * B_HD
C_HQ = 8
C_HKV = 2
C_HD = 128
N_EXPERTS = 16
N_GROUPS = 4
EXPERTS_PER_GROUP = N_EXPERTS // N_GROUPS
TOP_K = 2
D_EXPERT = 512
N_EVEN = (DEPTH + 1) // 2
N_ODD = DEPTH // 2
ALPHA = (2 * DEPTH) ** 0.25
BETA = (8 * DEPTH) ** -0.25
LN_EPS = 1e-5
QK_EPS = 1e-6
SUBLN_EPS = 1e-5
EVEN_SPLITS = (A_HQ * A_HD, A_HKV * A_HD, A_HKV * A_HD, B_H * 2 * B_HD, B_H * 2 * B_HD, B_H * B_VD)
EVEN_IN = sum(EVEN_SPLITS)
EVEN_OUT = A_HQ * A_HD + B_H * B_VD
ODD_SPLITS = (C_HQ * C_HD, C_HKV * C_HD, C_HKV * C_HD)
ODD_IN = sum(ODD_SPLITS)
ODD_OUT = C_HQ * C_HD


def _split(z, sizes):
    idx, acc = [], 0
    for s in sizes[:-1]:
        acc += s
        idx.append(acc)
    return jnp.split(z, idx, axis=-1)

def layer_norm(x, g, b):
    xf = x.astype(jnp.float32)
    mu = jnp.mean(xf, -1, keepdims=True)
    var = jnp.mean(jnp.square(xf - mu), -1, keepdims=True)
    y = (xf - mu) * lax.rsqrt(var + LN_EPS)
    return (y * g.astype(jnp.float32) + b.astype(jnp.float32)).astype(x.dtype)

def rms_norm(x, g, eps):
    xf = x.astype(jnp.float32)
    y = xf * lax.rsqrt(jnp.mean(jnp.square(xf), -1, keepdims=True) + eps)
    return (y * g.astype(jnp.float32)).astype(x.dtype)

def axial_rope_tables(n_tokens, head_dim):
    rows = n_tokens // GRID_W
    rr, cc = jnp.meshgrid(jnp.arange(rows), jnp.arange(GRID_W), indexing='ij')
    quarter = head_dim // 4
    inv_freq = ROPE_THETA ** (-jnp.arange(quarter, dtype=jnp.float32) / quarter)
    ang_r = rr.reshape(-1)[:, None].astype(jnp.float32) * inv_freq
    ang_c = cc.reshape(-1)[:, None].astype(jnp.float32) * inv_freq
    return jnp.cos(ang_r), jnp.sin(ang_r), jnp.cos(ang_c), jnp.sin(ang_c)

def _rotate(x, cos, sin):
    x1, x2 = jnp.split(x, 2, axis=-1)
    return jnp.concatenate([x1 * cos - x2 * sin, x1 * sin + x2 * cos], axis=-1)

def apply_axial_rope(x, tabs):
    cr, sr, cc, sc = [t[:, None, :].astype(x.dtype) for t in tabs]
    xr, xc = jnp.split(x, 2, axis=-1)
    return jnp.concatenate([_rotate(xr, cr, sr), _rotate(xc, cc, sc)], axis=-1)

def gqa_softmax(q, k, v, sink=None):
    hkv, grp = q.shape[2], q.shape[3]
    s = jnp.einsum('bqhgd,bkhd->bhgqk', q, k).astype(jnp.float32) * (q.shape[-1] ** -0.5)
    if sink is not None:
        s_sink = jnp.broadcast_to(sink.astype(jnp.float32).reshape(1, hkv, grp, 1, 1), s.shape[:-1] + (1,))
        p = jax.nn.softmax(jnp.concatenate([s_sink, s], axis=-1), axis=-1)[..., 1:]
    else:
        p = jax.nn.softmax(s, axis=-1)
    return jnp.einsum('bhgqk,bkhd->bqhgd', p.astype(v.dtype), v)

def window_attention_sink(q, k, v, kc, vc, sink):
    bsz, seq = q.shape[0], q.shape[1]
    nb = seq // BLOCK
    grp = A_HQ // A_HKV
    n_ctx = kc.shape[1]
    scale = A_HD ** -0.5
    qb = q.reshape(bsz, nb, BLOCK, A_HKV, grp, A_HD)

    def band(t):
        tp = jnp.pad(t, ((0, 0), (BLOCK, BLOCK), (0, 0), (0, 0))).reshape(bsz, nb + 2, BLOCK, A_HKV, A_HD)
        return jnp.concatenate([tp[:, :-2], tp[:, 1:-1], tp[:, 2:]], axis=2)

    kb, vb = band(k), band(v)
    blk = jnp.arange(nb)[:, None, None] * BLOCK
    qpos = blk + jnp.arange(BLOCK)[None, :, None]
    kpos = blk - BLOCK + jnp.arange(3 * BLOCK)[None, None, :]
    ok = (jnp.abs(qpos - kpos) <= WINDOW) & (kpos >= 0) & (kpos < seq)
    s_loc = jnp.einsum('bnqhgd,bnkhd->bnhgqk', qb, kb).astype(jnp.float32) * scale
    s_loc = jnp.where(ok[None, :, None, None], s_loc, -jnp.inf)
    s_ctx = jnp.einsum('bnqhgd,bchd->bnhgqc', qb, kc).astype(jnp.float32) * scale
    s_sink = jnp.broadcast_to(sink.astype(jnp.float32).reshape(1, 1, A_HKV, grp, 1, 1), s_ctx.shape[:-1] + (1,))
    p = jax.nn.softmax(jnp.concatenate([s_sink, s_ctx, s_loc], axis=-1), axis=-1)
    p_ctx = p[..., 1:1 + n_ctx].astype(v.dtype)
    p_loc = p[..., 1 + n_ctx:].astype(v.dtype)
    o = jnp.einsum('bnhgqc,bchd->bnqhgd', p_ctx, vc) + jnp.einsum('bnhgqk,bnkhd->bnqhgd', p_loc, vb)
    return o.reshape(bsz, seq, A_HQ * A_HD)

def diff_core(q, k, v, lam):
    s = jnp.einsum('bqhmd,bkhmd->bhmqk', q, k).astype(jnp.float32) * (B_HD ** -0.5)
    p = jax.nn.softmax(s, axis=-1)
    a = p[:, :, 0] - lam * p[:, :, 1]
    return jnp.einsum('bhqk,bkhe->bqhe', a.astype(v.dtype), v)

def diff_post(o, subln_g, lam_init):
    o = rms_norm(o, subln_g, SUBLN_EPS) * (1.0 - lam_init)
    return o.reshape(o.shape[0], o.shape[1], B_H * B_VD)

def even_mixer(h, hc, w_in, w_out, sink, lq1, lk1, lq2, lk2, subln_g, lam_init, ctx_out):
    bsz, seq = h.shape[0], h.shape[1]
    n_ctx = hc.shape[1]
    nb = seq // BLOCK
    grp = A_HQ // A_HKV
    tabs = axial_rope_tables(seq, A_HD)

    def proj(t):
        aq, ak, av, bq, bk, bv = _split(t @ w_in, EVEN_SPLITS)
        lead = t.shape[:2]
        return (aq.reshape(lead + (A_HQ, A_HD)), ak.reshape(lead + (A_HKV, A_HD)),
                av.reshape(lead + (A_HKV, A_HD)), bq.reshape(lead + (B_H * 2, B_HD)),
                bk.reshape(lead + (B_H * 2, B_HD)), bv.reshape(lead + (B_H, B_VD)))

    aq, ak, av, bq, bk, bv = proj(h)
    aq, ak, bq, bk = [apply_axial_rope(t, tabs) for t in (aq, ak, bq, bk)]
    aqc, akc, avc, bqc, bkc, bvc = proj(hc)
    lam = (jnp.exp(jnp.sum(lq1 * lk1)) - jnp.exp(jnp.sum(lq2 * lk2))).astype(jnp.float32) + lam_init

    oa = window_attention_sink(aq, ak, av, akc, avc, sink)
    kb_all = jnp.concatenate([bkc, bk], axis=1).reshape(bsz, n_ctx + seq, B_H, 2, B_HD)
    vb_all = jnp.concatenate([bvc, bv], axis=1)
    qblocks = bq.reshape(bsz, nb, BLOCK, B_H, 2, B_HD).swapaxes(0, 1)
    ob = lax.map(lambda qblk: diff_core(qblk, kb_all, vb_all, lam), qblocks)
    ob = diff_post(ob.swapaxes(0, 1).reshape(bsz, seq, B_H, B_VD), subln_g, lam_init)
    y = jnp.concatenate([oa, ob], axis=-1) @ w_out
    if not ctx_out:
        return y, None
    oac = gqa_softmax(aqc.reshape(bsz, n_ctx, A_HKV, grp, A_HD), akc, avc, sink).reshape(bsz, n_ctx, A_HQ * A_HD)
    obc = diff_post(diff_core(bqc.reshape(bsz, n_ctx, B_H, 2, B_HD), bkc.reshape(bsz, n_ctx, B_H, 2, B_HD), bvc, lam), subln_g, lam_init)
    yc = jnp.concatenate([oac, obc], axis=-1) @ w_out
    return y, yc

def odd_mixer(h, hc, w_in, w_out, qn_g, kn_g, ctx_out):
    bsz, seq = h.shape[0], h.shape[1]
    n_ctx = hc.shape[1]
    nb = seq // BLOCK
    grp = C_HQ // C_HKV
    tabs = axial_rope_tables(seq, C_HD)

    def proj(t):
        q, k, v = _split(t @ w_in, ODD_SPLITS)
        lead = t.shape[:2]
        q = rms_norm(q.reshape(lead + (C_HQ, C_HD)), qn_g, QK_EPS)
        k = rms_norm(k.reshape(lead + (C_HKV, C_HD)), kn_g, QK_EPS)
        return q, k, v.reshape(lead + (C_HKV, C_HD))

    q, k, v = proj(h)
    q, k = apply_axial_rope(q, tabs), apply_axial_rope(k, tabs)
    qc, kc, vc = proj(hc)
    k_all = jnp.concatenate([kc, k], axis=1)
    v_all = jnp.concatenate([vc, v], axis=1)
    qblocks = q.reshape(bsz, nb, BLOCK, C_HKV, grp, C_HD).swapaxes(0, 1)
    o = lax.map(lambda qblk: gqa_softmax(qblk, k_all, v_all), qblocks)
    y = o.swapaxes(0, 1).reshape(bsz, seq, C_HQ * C_HD) @ w_out
    if not ctx_out:
        return y, None
    oc = gqa_softmax(qc.reshape(bsz, n_ctx, C_HKV, grp, C_HD), kc, vc).reshape(bsz, n_ctx, C_HQ * C_HD)
    return y, oc @ w_out

def moe(h, w_router, b_router, w_gate, w_up, w_down):
    logits = jnp.einsum('...d,de->...e', h, w_router).astype(jnp.float32)
    scores = jax.nn.sigmoid(logits)
    sel = scores + b_router.astype(jnp.float32)
    grouped = sel.reshape(sel.shape[:-1] + (N_GROUPS, EXPERTS_PER_GROUP))
    group_score = jnp.sum(lax.top_k(grouped, TOP_K)[0], axis=-1)
    best = jnp.argmax(group_score, axis=-1)
    in_group = (jnp.arange(N_EXPERTS) // EXPERTS_PER_GROUP) == best[..., None]
    _, idx = lax.top_k(jnp.where(in_group, sel, -jnp.inf), TOP_K)
    wts = jnp.take_along_axis(scores, idx, axis=-1)
    wts = wts / jnp.sum(wts, axis=-1, keepdims=True)
    gates = jnp.sum(jax.nn.one_hot(idx, N_EXPERTS, dtype=jnp.float32) * wts[..., None], axis=-2)
    g = jnp.einsum('...d,edf->...ef', h, w_gate)
    u = jnp.einsum('...d,edf->...ef', h, w_up)
    a = jax.nn.silu(g) * u * gates[..., None].astype(h.dtype)
    return jnp.einsum('...ef,efd->...d', a, w_down)

def first_inputs(seed: int = 0) -> dict:
    key = jax.random.key(seed)
    ks = jax.random.split(key, 25)

    def nrm(k, shape, s):
        return jax.random.normal(k, shape, jnp.float32) * s

    return {
        'x': nrm(ks[0], (BATCH, SEQ, D_MODEL), 1.0),
        'c': nrm(ks[1], (BATCH, D_MODEL), 1.0),
        'ctx': nrm(ks[2], (BATCH, CTX_LEN, D_MODEL), 1.0),
        'c_ctx': nrm(ks[3], (D_MODEL,), 1.0),
        'w_mod': nrm(ks[4], (DEPTH, D_MODEL, 6 * D_MODEL), 0.5 * D_MODEL ** -0.5),
        'b_mod': nrm(ks[5], (DEPTH, 6 * D_MODEL), 0.02),
        'ln_g': 1.0 + nrm(ks[6], (DEPTH, 2, D_MODEL), 0.02),
        'ln_b': nrm(ks[7], (DEPTH, 2, D_MODEL), 0.02),
        'w_in_even': nrm(ks[8], (N_EVEN, D_MODEL, EVEN_IN), D_MODEL ** -0.5),
        'w_out_even': nrm(ks[9], (N_EVEN, EVEN_OUT, D_MODEL), BETA * EVEN_OUT ** -0.5),
        'sink_logits': nrm(ks[10], (N_EVEN, A_HQ), 0.5),
        'lam_q1': nrm(ks[11], (N_EVEN, B_HD), 0.1),
        'lam_k1': nrm(ks[12], (N_EVEN, B_HD), 0.1),
        'lam_q2': nrm(ks[13], (N_EVEN, B_HD), 0.1),
        'lam_k2': nrm(ks[14], (N_EVEN, B_HD), 0.1),
        'subln_g': 1.0 + nrm(ks[15], (N_EVEN, B_VD), 0.02),
        'w_in_odd': nrm(ks[16], (N_ODD, D_MODEL, ODD_IN), D_MODEL ** -0.5),
        'w_out_odd': nrm(ks[17], (N_ODD, ODD_OUT, D_MODEL), BETA * ODD_OUT ** -0.5),
        'q_norm_g': 1.0 + nrm(ks[18], (N_ODD, C_HD), 0.02),
        'k_norm_g': 1.0 + nrm(ks[19], (N_ODD, C_HD), 0.02),
        'w_router': nrm(ks[20], (D_MODEL, N_EXPERTS), D_MODEL ** -0.5),
        'b_router': nrm(ks[21], (N_EXPERTS,), 0.01),
        'w_gate': nrm(ks[22], (DEPTH, N_EXPERTS, D_MODEL, D_EXPERT), D_MODEL ** -0.5),
        'w_up': nrm(ks[23], (DEPTH, N_EXPERTS, D_MODEL, D_EXPERT), D_MODEL ** -0.5),
        'w_down': nrm(ks[24], (DEPTH, N_EXPERTS, D_EXPERT, D_MODEL), BETA * D_EXPERT ** -0.5),
    }

def first_block(x, c, ctx, c_ctx, w_mod, b_mod, ln_g, ln_b, w_in_even, w_out_even, sink_logits,
              lam_q1, lam_k1, lam_q2, lam_k2, subln_g, w_in_odd, w_out_odd, q_norm_g, k_norm_g,
              w_router, b_router, w_gate, w_up, w_down):
    xc = ctx
    cond = jax.nn.silu(c)
    cond_ctx = jax.nn.silu(c_ctx)
    for l in range(DEPTH):
        ctx_out = l < DEPTH - 1
        sh1, sc1, g1, sh2, sc2, g2 = [m[:, None, :] for m in jnp.split(cond @ w_mod[l] + b_mod[l], 6, axis=-1)]
        shc1, scc1, gc1, shc2, scc2, gc2 = jnp.split(cond_ctx @ w_mod[l] + b_mod[l], 6, axis=-1)
        h = x * (1.0 + sc1) + sh1
        hc = xc * (1.0 + scc1) + shc1
        i = l // 2
        if l % 2 == 0:
            lam_init = 0.8 - 0.6 * math.exp(-0.3 * l)
            y, yc = even_mixer(h, hc, w_in_even[i], w_out_even[i], sink_logits[i], lam_q1[i], lam_k1[i],
                               lam_q2[i], lam_k2[i], subln_g[i], lam_init, ctx_out)
        else:
            y, yc = odd_mixer(h, hc, w_in_odd[i], w_out_odd[i], q_norm_g[i], k_norm_g[i], ctx_out)
        x = layer_norm(ALPHA * x + g1 * y, ln_g[l, 0], ln_b[l, 0])
        h2 = x * (1.0 + sc2) + sh2
        x = layer_norm(ALPHA * x + g2 * moe(h2, w_router, b_router, w_gate[l], w_up[l], w_down[l]), ln_g[l, 1], ln_b[l, 1])
        if ctx_out:
            xc = layer_norm(ALPHA * xc + gc1 * yc, ln_g[l, 0], ln_b[l, 0])
            hc2 = xc * (1.0 + scc2) + shc2
            xc = layer_norm(ALPHA * xc + gc2 * moe(hc2, w_router, b_router, w_gate[l], w_up[l], w_down[l]), ln_g[l, 1], ln_b[l, 1])
    return x


DEPTH_2 = 4

N_MIXERS = 3
N_META = 16
NORM_EPS = 1e-6

FOX_HEADS = 16
FOX_HEAD_DIM = D_MODEL // FOX_HEADS
FOX_Q_BLOCK = 128
FOX_IN = 4 * D_MODEL + FOX_HEADS

GLA_HEADS = 4
GLA_DK = D_MODEL // 2 // GLA_HEADS
GLA_DV = D_MODEL // GLA_HEADS
GLA_GATE_RANK = 16
GLA_GATE_NORMALIZER = 16.0
GLA_CHUNK = 64
GLA_QK = GLA_HEADS * GLA_DK
GLA_V = GLA_HEADS * GLA_DV
GLA_IN = 2 * GLA_QK + 2 * GLA_V + GLA_GATE_RANK

GDN_HEADS = 8
GDN_DK = 128
GDN_DV = 128
GDN_CONV = 4
GDN_CHUNK = 64
GDN_CONV_DIM = 2 * GDN_HEADS * GDN_DK + GDN_HEADS * GDN_DV
GDN_IN = GDN_CONV_DIM + GDN_HEADS * GDN_DV + 2 * GDN_HEADS

D_FF = ((-(-8 * D_MODEL // 3) + 255) // 256) * 256

N_FOX = (DEPTH_2 + 2) // 3
N_GLA = (DEPTH_2 + 1) // 3
N_GDN = DEPTH_2 // 3


def rmsnorm(x, g):
    xf = x.astype(jnp.float32)
    y = xf * lax.rsqrt(jnp.mean(xf * xf, axis=-1, keepdims=True) + NORM_EPS)
    return (y * g.astype(jnp.float32)).astype(x.dtype)

def l2norm(x):
    xf = x.astype(jnp.float32)
    return (xf * lax.rsqrt(jnp.sum(xf * xf, axis=-1, keepdims=True) + NORM_EPS)).astype(x.dtype)

def to_chunks(a, chunk):
    b, t = a.shape[0], a.shape[1]
    return jnp.moveaxis(a.reshape((b, t // chunk, chunk) + a.shape[2:]), 1, 0)

def from_chunks(a):
    a = jnp.moveaxis(a, 0, 1)
    return a.reshape((a.shape[0], a.shape[1] * a.shape[2]) + a.shape[3:])

def chunked_scan(chunk_fn, state0, seqs, chunk):
    state, o_meta = chunk_fn(state0, tuple(a[:, :N_META] for a in seqs))
    real = tuple(to_chunks(a[:, N_META:], chunk) for a in seqs)
    _, o_real = lax.scan(chunk_fn, state, real)
    return jnp.concatenate([o_meta, from_chunks(o_real)], axis=1)

def fox_attend(q, cq, qpos, k, v, ck, kpos):
    s = jnp.einsum('bqhd,bkhd->bhqk', q, k).astype(jnp.float32)
    bias = cq[..., :, None] - ck[..., None, :]
    mask = kpos[None, :] <= qpos[:, None]
    s = jnp.where(mask, s + bias, -jnp.inf)
    p = jax.nn.softmax(s, axis=-1)
    return jnp.einsum('bhqk,bkhd->bqhd', p.astype(v.dtype), v)

def fox_mixer(h, w_in, b_f, q_gain, k_gain, w_out):
    B, L, _ = h.shape
    H, Dh = FOX_HEADS, FOX_HEAD_DIM
    proj = h @ w_in
    q, k, v, gate, f = jnp.split(proj, [D_MODEL, 2 * D_MODEL, 3 * D_MODEL, 4 * D_MODEL], axis=-1)
    q = rmsnorm(q.reshape(B, L, H, Dh), q_gain) * (Dh ** -0.5)
    k = rmsnorm(k.reshape(B, L, H, Dh), k_gain)
    v = v.reshape(B, L, H, Dh)
    log_f = jax.nn.log_sigmoid((f + b_f).astype(jnp.float32))
    c = jnp.cumsum(log_f, axis=1).transpose(0, 2, 1)
    kpos = jnp.arange(L)

    o_meta = fox_attend(q[:, :N_META], c[:, :, :N_META], kpos[:N_META],
                        k[:, :N_META], v[:, :N_META], c[:, :, :N_META], kpos[:N_META])

    n_blk = (L - N_META) // FOX_Q_BLOCK
    q_blocks = q[:, N_META:].reshape(B, n_blk, FOX_Q_BLOCK, H, Dh).swapaxes(0, 1)
    cq_blocks = c[:, :, N_META:].reshape(B, H, n_blk, FOX_Q_BLOCK).transpose(2, 0, 1, 3)
    qpos_blocks = (N_META + jnp.arange(n_blk * FOX_Q_BLOCK)).reshape(n_blk, FOX_Q_BLOCK)

    def block(args):
        qb, cqb, qp = args
        return fox_attend(qb, cqb, qp, k, v, c, kpos)

    o_real = from_chunks(lax.map(block, (q_blocks, cq_blocks, qpos_blocks)))
    o = jnp.concatenate([o_meta, o_real], axis=1).reshape(B, L, H * Dh)
    o = o * jax.nn.sigmoid(gate)
    return (o @ w_out).astype(h.dtype)

def gla_chunk(state, inputs):
    q, k, v, g = inputs
    C = q.shape[1]
    b = jnp.cumsum(g, axis=1)
    causal = jnp.tril(jnp.ones((C, C), dtype=bool))
    diff = b[:, :, None] - b[:, None, :]
    decay = jnp.exp(jnp.where(causal[None, :, :, None, None], diff, -jnp.inf))
    A = jnp.einsum('bthd,bshd,btshd->bhts', q, k, decay)
    o_intra = jnp.einsum('bhts,bshv->bthv', A, v)
    o_inter = jnp.einsum('bthd,bhdv->bthv', q * jnp.exp(b), state)
    b_last = b[:, -1]
    k_dec = k * jnp.exp(b_last[:, None] - b)
    new_state = state * jnp.exp(b_last)[..., None] + jnp.einsum('bshd,bshv->bhdv', k_dec, v)
    return new_state, (o_intra + o_inter).astype(v.dtype)

def gla_mixer(h, w_in, w_alpha2, b_alpha, o_gain, w_out):
    B, L, _ = h.shape
    H = GLA_HEADS
    proj = h @ w_in
    q, k, v, r, a_lr = jnp.split(proj, [GLA_QK, 2 * GLA_QK, 2 * GLA_QK + GLA_V, 2 * GLA_QK + 2 * GLA_V], axis=-1)
    q = q.reshape(B, L, H, GLA_DK) * (GLA_DK ** -0.5)
    k = k.reshape(B, L, H, GLA_DK)
    v = v.reshape(B, L, H, GLA_DV)
    g = jax.nn.log_sigmoid((a_lr @ w_alpha2 + b_alpha).astype(jnp.float32)) / GLA_GATE_NORMALIZER
    g = g.reshape(B, L, H, GLA_DK)
    state0 = jnp.zeros((B, H, GLA_DK, GLA_DV), jnp.float32)
    o = chunked_scan(gla_chunk, state0, (q, k, v, g), GLA_CHUNK)
    o = rmsnorm(o, o_gain) * jax.nn.silu(r.reshape(B, L, H, GLA_DV))
    return (o.reshape(B, L, GLA_V) @ w_out).astype(h.dtype)

def causal_depthwise_conv(x, w):
    return lax.conv_general_dilated(
        x, w.astype(x.dtype), window_strides=(1,), padding=[(GDN_CONV - 1, 0)],
        dimension_numbers=('NWC', 'WIO', 'NWC'), feature_group_count=x.shape[-1])

def gdn_chunk(state, inputs):
    q, k, v, g, beta = inputs
    C = q.shape[1]
    qh = q.transpose(0, 2, 1, 3)
    kh = k.transpose(0, 2, 1, 3)
    vh = v.transpose(0, 2, 1, 3)
    bt = beta.transpose(0, 2, 1).astype(jnp.float32)[..., None]
    b = jnp.cumsum(g, axis=1).transpose(0, 2, 1)
    diff = b[..., :, None] - b[..., None, :]
    incl = jnp.tril(jnp.ones((C, C), dtype=bool))
    strict = jnp.tril(jnp.ones((C, C), dtype=bool), k=-1)
    kb = kh.astype(jnp.float32) * bt
    vb = vh.astype(jnp.float32) * bt
    lower = jnp.einsum('bhtd,bhsd->bhts', kb, kh) * jnp.exp(jnp.where(strict, diff, -jnp.inf))
    t_mat = jnp.eye(C, dtype=jnp.float32) + lower
    rhs = jnp.concatenate([vb, kb * jnp.exp(b)[..., None]], axis=-1)
    sol = lax.linalg.triangular_solve(t_mat, rhs, left_side=True, lower=True, unit_diagonal=True)
    u, w = sol[..., :GDN_DV], sol[..., GDN_DV:]
    v_new = u - jnp.einsum('bhcd,bhdv->bhcv', w, state)
    attn = jnp.einsum('bhtd,bhsd->bhts', qh, kh) * jnp.exp(jnp.where(incl, diff, -jnp.inf))
    o = jnp.einsum('bhts,bhsv->bhtv', attn, v_new) + \
        jnp.einsum('bhtd,bhdv->bhtv', qh * jnp.exp(b)[..., None], state)
    b_last = b[..., -1]
    k_dec = kh * jnp.exp(b_last[..., None] - b)[..., None]
    new_state = state * jnp.exp(b_last)[..., None, None] + jnp.einsum('bhsd,bhsv->bhdv', k_dec, v_new)
    return new_state, o.transpose(0, 2, 1, 3).astype(v.dtype)

def gdn_mixer(h, w_in, conv_w, a_log, dt_bias, o_gain, w_out):
    B, L, _ = h.shape
    H = GDN_HEADS
    proj = h @ w_in
    qkv, gate, a, beta_logit = jnp.split(
        proj, [GDN_CONV_DIM, GDN_CONV_DIM + H * GDN_DV, GDN_CONV_DIM + H * GDN_DV + H], axis=-1)
    qkv = jax.nn.silu(causal_depthwise_conv(qkv, conv_w))
    q, k, v = jnp.split(qkv, [H * GDN_DK, 2 * H * GDN_DK], axis=-1)
    q = l2norm(q.reshape(B, L, H, GDN_DK)) * (GDN_DK ** -0.5)
    k = l2norm(k.reshape(B, L, H, GDN_DK))
    v = v.reshape(B, L, H, GDN_DV)
    beta = jax.nn.sigmoid(beta_logit)
    g = -jnp.exp(a_log.astype(jnp.float32)) * jax.nn.softplus((a + dt_bias).astype(jnp.float32))
    state0 = jnp.zeros((B, H, GDN_DK, GDN_DV), jnp.float32)
    o = chunked_scan(gdn_chunk, state0, (q, k, v, g, beta), GDN_CHUNK)
    o = rmsnorm(o, o_gain) * jax.nn.silu(gate.reshape(B, L, H, GDN_DV))
    return (o.reshape(B, L, H * GDN_DV) @ w_out).astype(h.dtype)

def swiglu(h, w_gate_up, w_down):
    gu = h @ w_gate_up
    gt, up = gu[..., :D_FF], gu[..., D_FF:]
    return ((jax.nn.silu(gt) * up) @ w_down).astype(h.dtype)

def second_inputs(seed: int = 0) -> dict:
    key = jax.random.key(seed)
    ks = jax.random.split(key, 24)

    def nrm(k, shape, fan_in):
        return jax.random.normal(k, shape, jnp.float32) * (fan_in ** -0.5)

    def gain(k, shape):
        return 1.0 + 0.02 * jax.random.normal(k, shape, jnp.float32)

    dt = jnp.exp(jax.random.uniform(ks[20], (N_GDN, GDN_HEADS), jnp.float32, np.log(1e-3), np.log(1e-1)))
    return {
        "x": jax.random.normal(ks[0], (BATCH, SEQ, D_MODEL), jnp.float32),
        "meta_tokens": jax.random.normal(ks[1], (N_META, D_MODEL), jnp.float32),
        "norm_mix": gain(ks[2], (DEPTH_2, D_MODEL)),
        "norm_ffn": gain(ks[3], (DEPTH_2, D_MODEL)),
        "w_gate_up": nrm(ks[4], (DEPTH_2, D_MODEL, 2 * D_FF), D_MODEL),
        "w_down": nrm(ks[5], (DEPTH_2, D_FF, D_MODEL), D_FF),
        "fox_w_in": nrm(ks[6], (N_FOX, D_MODEL, FOX_IN), D_MODEL),
        "fox_b_f": 2.0 + 0.5 * jax.random.normal(ks[7], (N_FOX, FOX_HEADS), jnp.float32),
        "fox_q_gain": gain(ks[8], (N_FOX, FOX_HEAD_DIM)),
        "fox_k_gain": gain(ks[9], (N_FOX, FOX_HEAD_DIM)),
        "fox_w_out": nrm(ks[10], (N_FOX, D_MODEL, D_MODEL), D_MODEL),
        "gla_w_in": nrm(ks[11], (N_GLA, D_MODEL, GLA_IN), D_MODEL),
        "gla_w_alpha2": nrm(ks[12], (N_GLA, GLA_GATE_RANK, GLA_QK), GLA_GATE_RANK),
        "gla_b_alpha": 0.1 * jax.random.normal(ks[13], (N_GLA, GLA_QK), jnp.float32),
        "gla_o_gain": gain(ks[14], (N_GLA, GLA_DV)),
        "gla_w_out": nrm(ks[15], (N_GLA, GLA_V, D_MODEL), GLA_V),
        "gdn_w_in": nrm(ks[16], (N_GDN, D_MODEL, GDN_IN), D_MODEL),
        "gdn_conv_w": nrm(ks[17], (N_GDN, GDN_CONV, 1, GDN_CONV_DIM), GDN_CONV),
        "gdn_a_log": jnp.log(jax.random.uniform(ks[18], (N_GDN, GDN_HEADS), jnp.float32, 1.0, 16.0)),
        "gdn_dt_bias": dt + jnp.log(-jnp.expm1(-dt)),
        "gdn_o_gain": gain(ks[19], (N_GDN, GDN_DV)),
        "gdn_w_out": nrm(ks[21], (N_GDN, GDN_HEADS * GDN_DV, D_MODEL), GDN_HEADS * GDN_DV),
    }

def second_block(x, meta_tokens, norm_mix, norm_ffn, w_gate_up, w_down,
              fox_w_in, fox_b_f, fox_q_gain, fox_k_gain, fox_w_out,
              gla_w_in, gla_w_alpha2, gla_b_alpha, gla_o_gain, gla_w_out,
              gdn_w_in, gdn_conv_w, gdn_a_log, gdn_dt_bias, gdn_o_gain, gdn_w_out):
    B = x.shape[0]
    meta = jnp.broadcast_to(meta_tokens[None].astype(x.dtype), (B, N_META, D_MODEL))
    h = jnp.concatenate([meta, x], axis=1)
    for i in range(DEPTH_2):
        kind, j = i % N_MIXERS, i // N_MIXERS
        y = rmsnorm(h, norm_mix[i])
        if kind == 0:
            mix = fox_mixer(y, fox_w_in[j], fox_b_f[j], fox_q_gain[j], fox_k_gain[j], fox_w_out[j])
        elif kind == 1:
            mix = gla_mixer(y, gla_w_in[j], gla_w_alpha2[j], gla_b_alpha[j], gla_o_gain[j], gla_w_out[j])
        else:
            mix = gdn_mixer(y, gdn_w_in[j], gdn_conv_w[j], gdn_a_log[j], gdn_dt_bias[j], gdn_o_gain[j], gdn_w_out[j])
        h = h + mix
        h = h + swiglu(rmsnorm(h, norm_ffn[i]), w_gate_up[i], w_down[i])
    return h[:, N_META:]


def setup_inputs(seed=0):
    out = dict(first_inputs(seed))
    for name, value in second_inputs(seed + 1).items():
        if name != "x":
            out[name + "_2"] = value
    return out


def reference(
    x, c, ctx, c_ctx, w_mod, b_mod, ln_g, ln_b, w_in_even, w_out_even, sink_logits, lam_q1,
    lam_k1, lam_q2, lam_k2, subln_g, w_in_odd, w_out_odd, q_norm_g, k_norm_g, w_router,
    b_router, w_gate, w_up, w_down, meta_tokens_2, norm_mix_2, norm_ffn_2, w_gate_up_2,
    w_down_2, fox_w_in_2, fox_b_f_2, fox_q_gain_2, fox_k_gain_2, fox_w_out_2, gla_w_in_2,
    gla_w_alpha2_2, gla_b_alpha_2, gla_o_gain_2, gla_w_out_2, gdn_w_in_2, gdn_conv_w_2,
    gdn_a_log_2, gdn_dt_bias_2, gdn_o_gain_2, gdn_w_out_2,
):
    x = first_block(
        x, c, ctx, c_ctx, w_mod, b_mod, ln_g, ln_b, w_in_even, w_out_even, sink_logits, lam_q1,
        lam_k1, lam_q2, lam_k2, subln_g, w_in_odd, w_out_odd, q_norm_g, k_norm_g, w_router,
        b_router, w_gate, w_up, w_down,
    )
    return second_block(
        x, meta_tokens_2, norm_mix_2, norm_ffn_2, w_gate_up_2, w_down_2, fox_w_in_2, fox_b_f_2,
        fox_q_gain_2, fox_k_gain_2, fox_w_out_2, gla_w_in_2, gla_w_alpha2_2, gla_b_alpha_2,
        gla_o_gain_2, gla_w_out_2, gdn_w_in_2, gdn_conv_w_2, gdn_a_log_2, gdn_dt_bias_2,
        gdn_o_gain_2, gdn_w_out_2,
    )


_drawn_inputs = setup_inputs


def setup_inputs(seed=0):
    import zlib

    import numpy as np

    out = dict(_drawn_inputs(seed))
    spreads = {}
    factors = {'sink_logits': 8.0,
     'lam_k1': 8.0,
     'lam_q2': 5.041,
     'lam_k2': 6.836,
     'subln_g': 5.642,
     'q_norm_g': 8.0,
     'k_norm_g': 8.0,
     'fox_q_gain_2': 8.0,
     'fox_k_gain_2': 8.0,
     'gla_o_gain_2': 4.885,
     'gdn_o_gain_2': 7.314}
    for name, (base, spread) in spreads.items():
        noise = np.random.default_rng([zlib.crc32(name.encode()), seed]).standard_normal(out[name].shape)
        drawn = base * np.exp(spread * noise) if base else spread * noise
        out[name] = jnp.asarray(drawn.astype(out[name].dtype))
    for name, factor in factors.items():
        out[name] = (out[name] * factor).astype(out[name].dtype)
    return out
```

```python
from contextlib import ExitStack

import numpy as np
import concourse.bass as bass
from concourse import mybir

F32 = mybir.dt.float32
F32R = mybir.dt.float32r
U32 = mybir.dt.uint32
ACT = mybir.ActivationFunctionType
ALU = mybir.AluOpType
AX_X = mybir.AxisListType.X

P = 128
D = 1024
KC = D // P
SEQ = 256
CTX = 256
T1 = CTX + SEQ
GRID_W = 64
ROPE_THETA = 10000.0
WINDOW = 128
ALPHA = (2 * 2) ** 0.25
LN_EPS, QK_EPS, SUBLN_EPS, NORM_EPS = 1e-5, 1e-6, 1e-5, 1e-6
LAM_INIT = 0.8 - 0.6
EXPERTS, GROUPS, D_EXPERT = 16, 4, 512
META = 16
T2 = META + SEQ
D_FF = 2816
BIG = 1e30

TILES1 = [(0, 128), (128, 128), (256, 128), (384, 128)]
TILES2 = [(0, META), (META, 128), (META + 128, 128)]

SLOTS = 6
ROOM = 22200
SPLIT_SLOTS = 2
SLOT = 2048
WIDE = 256
LEVELS = 7

SMALL_COLS = [
    ("cond", KC * 2), ("b_mod", 96), ("ln_g", 32), ("ln_b", 32), ("norm_mix", 32), ("norm_ffn", 32),
    ("meta", KC * META), ("w_router", KC * EXPERTS), ("b_router", EXPERTS), ("sink", 8), ("lam", 256),
    ("subln_g", 1), ("qn_g", 1), ("kn_g", 1), ("fox_wf", 2 * KC * 16), ("fox_bf", 32), ("fox_qg", 2), ("fox_kg", 2),
    ("gla_wa", KC * 16), ("gla_w2", 512), ("gla_ba", 4), ("gla_og", 2),
    ("gdn_wab", KC * 16), ("gdn_conv", 96), ("gdn_alog", 8), ("gdn_dt", 8), ("gdn_og", 1),
    ("ident", 128), ("ones", 128), ("ones64", 128), ("rot64", 128), ("rot128", 128), ("upto", 128),
    ("cos64", 256), ("sin64", 256), ("cos128", 256), ("sin128", 256), ("window", 256), ("causal", 128),
    ("levels", LEVELS * 128), ("group_rank", 4), ("expert_rank", 16),
]
SMALL_AT = {}
_at = 0
for _name, _cols in SMALL_COLS:
    SMALL_AT[_name] = (_at, _cols)
    _at += _cols
SMALL = _at


def rope_tables(hd):
    n = np.arange(SEQ)
    quarter = hd // 4
    inv = (np.float32(ROPE_THETA) ** (-np.arange(quarter, dtype=np.float32) / np.float32(quarter))).astype(np.float32)
    ang = {0: (n // GRID_W).astype(np.float32)[None, :] * inv[:, None],
           1: (n % GRID_W).astype(np.float32)[None, :] * inv[:, None]}
    cos = np.zeros((P, SEQ), np.float32)
    sin = np.zeros((P, SEQ), np.float32)
    rot = np.zeros((P, P), np.float32)
    for f in range(P):
        axis, r = divmod(f % hd, hd // 2)
        half, q = divmod(r, quarter)
        cos[f] = np.cos(ang[axis][q])
        sin[f] = np.sin(ang[axis][q])
        if half == 0:
            rot[f + quarter, f] = -1.0
        else:
            rot[f - quarter, f] = 1.0
    return cos, sin, rot


def shape_constants():
    c = {}
    i = np.arange(P)
    c["ident"] = np.eye(P, dtype=np.float32)
    c["ones"] = np.ones((P, P), np.float32)
    c["ones64"] = (i[:, None] // 64 == i[None, :] // 64).astype(np.float32)
    c["cos64"], c["sin64"], c["rot64"] = rope_tables(64)
    c["cos128"], c["sin128"], c["rot128"] = rope_tables(128)
    c["upto"] = (i[:, None] <= i[None, :]).astype(np.float32)
    c["window"] = np.concatenate([np.where(np.abs(i[:, None] - (i + 128)[None, :]) > WINDOW, -BIG, 0.0),
                                  np.where(np.abs((i + 128)[:, None] - i[None, :]) > WINDOW, -BIG, 0.0)], 1).astype(np.float32)
    c["causal"] = np.where(i[None, :] > i[:, None], -BIG, 0.0).astype(np.float32)
    lv = np.zeros((P, LEVELS, P), np.float32)
    for l in range(LEVELS):
        h = 1 << l
        lv[:, l, :] = ((i[:, None] // (2 * h) == i[None, :] // (2 * h))
                       & (i[:, None] // h % 2 == 0) & (i[None, :] // h % 2 == 1))
    c["levels"] = lv.reshape(P, LEVELS * P)
    c["group_rank"] = np.broadcast_to(np.arange(4, 0, -1, dtype=np.float32), (P, 4))
    c["expert_rank"] = np.broadcast_to(np.arange(16, 0, -1, dtype=np.float32), (P, 16))
    return c


class Count:

    def __init__(self, sem, numbers):
        self.sem, self.numbers, self.n = sem, numbers, 0

    def mark(self, *name):
        self.n += 1
        self.numbers[name] = self.n
        return 1

    def at(self, *name):
        return self.numbers.get(name, 1)


class Core:

    def __init__(self, nc, ctx, dram, values):
        self.nc, self.ctx, self.dram, self.values = nc, ctx, dram, values
        self.ring = self.sbuf("ring", [P, SLOTS, SLOT])
        self.X = self.sbuf("X", [P, KC, T1])
        self.H = self.sbuf("H", [P, KC, T1])
        self.ACC = self.sbuf("ACC", [P, KC, T1])
        self.MOD = self.sbuf("MOD", [P, 96, 2])
        self.small = self.sbuf("small", [P, SMALL])
        self.stat = self.sbuf("stat", [P, 2, 512])
        self.room_size = ROOM
        with ExitStack() as scope:
            self.room = scope.enter_context(nc.sbuf_tensor("room", [P, self.room_size], F32))
        with ExitStack() as scope:
            def split(name, shape):
                return [scope.enter_context(nc.sbuf_tensor(f"{name}_{part}", shape, F32R)) for part in ("hi", "lo")]

            self.HS = split("H_split", [P, KC, T1])
            self.WS = split("W_split", [P, SPLIT_SLOTS, SLOT])
            self.AS = split("A_split", [P, 4, T1])
            self.gate_row = scope.enter_context(nc.sbuf_tensor("gate_row", [P, 2, T1], F32))
        self.ps = ctx.enter_context(nc.psum_tensor("ps", [P, 8, 512], F32))
        self.ring_full = [self.sem(f"ring_full{j}") for j in range(SLOTS)]
        self.mm_done = self.sem("mm_done")
        self.small_in = self.sem("small_in")
        self.x_in = self.sem("x_in")
        self.stored = self.sem("stored")
        self.stage_done = self.sem("stage_done")
        self.silu_done = self.sem("silu_done")
        self.mod_moved = self.sem("mod_moved")
        self.mul_done = self.sem("mul_done")
        self.hi_done = self.sem("hi_done")
        self.lo_done = self.sem("lo_done")
        self.gates_stored = self.sem("gates_stored")
        self.gate_in = [self.sem(f"gate_in{j}") for j in range(2)]
        self.gated_done = self.sem("gated_done")
        self.add_done = self.sem("add_done")
        self.counts = {}
        self.position = 0
        self.finished = 0
        self.release = []
        self.silus = self.gates = self.muls = self.adds = self.splits = self.gate_loads = 0
        self.uid = 0
        self.ext = self.room[:, self.room_size - 6 * 1024:].rearrange("p (a h t) -> p a h t", a=6, h=8)

    def sbuf(self, name, shape):
        return self.ctx.enter_context(self.nc.sbuf_tensor(name, shape, F32))

    def count(self, name):
        if name not in self.counts:
            self.counts[name] = Count(self.sem(name), self.values.setdefault(name, {}))
        return self.counts[name]

    def sem(self, name):
        return self.ctx.enter_context(self.nc.semaphore(name))

    def s(self, name, rows=P):
        at, n = SMALL_AT[name]
        return self.small[0:rows, at:at + n]

    def carve(self, sizes, reserve=0):
        at, out = 0, {}
        for name, dims in sizes.items():
            n = int(np.prod(dims))
            v = self.room[:, at:at + n]
            if len(dims) == 2:
                v = v.rearrange("p (a b) -> p a b", a=dims[0])
            elif len(dims) == 3:
                v = v.rearrange("p (a b c) -> p a b c", a=dims[0], b=dims[1])
            out[name] = v
            at += n
        assert at <= self.room_size - reserve, at
        return out

    def mod(self, layer, part, k, stream):
        c = layer * 48 + part * 8 + k
        return self.MOD[:, c, stream:stream + 1]

    def plan(self, results_per_slot):
        g0 = self.position
        for n in results_per_slot:
            self.finished += n
            self.release.append((self.mm_done, self.finished))
        self.position += len(results_per_slot)
        return g0

    def load(self, sp, g, src):
        if g >= SLOTS:
            sem, count = self.release[g - SLOTS]
            sp.wait_ge(sem, count)
        sp.dma_start(self.slot(g, src), src).then_inc(self.ring_full[g % SLOTS], 16)

    def slot(self, g, like=None):
        v = self.ring[:, g % SLOTS, :]
        if like is not None and len(like.shape) == 3:
            v = v.rearrange("p (k m) -> p k m", k=like.shape[1])
        return v

    def wide(self, g):
        return self.ring[:, g % SLOTS, :].rearrange("p (k m) -> p k m", k=KC)

    def arrived(self, pe, g, i=None):
        v = 16 * (g // SLOTS + 1)
        pe.wait_ge(self.ring_full[g % SLOTS], v if i is None else v + 16 * i)


def columns(w, c0):
    return w[:, c0:c0 + WIDE].rearrange("(k p) m -> p k m", p=P)


class StageCount:

    def __init__(self, count, stage):
        self.count, self.stage = count, stage

    def mark(self, *name):
        return self.count.mark(self.stage, *name)

    def at(self, *name):
        return self.count.at(self.stage, *name)


class Stage:

    def __init__(self, core):
        self.c = core
        core.uid += 1
        kind = type(self).__name__
        self.pe, self.act, self.dve = (StageCount(core.count(f"{kind}_{e}"), core.uid) for e in ("tensor", "scalar", "vector"))
        self.tensor_done, self.scalar_done, self.vector_done = (x.count.sem for x in (self.pe, self.act, self.dve))

    def sync(self, sp):
        pass

    def tensor(self, pe):
        pass

    def scalar(self, act):
        pass

    def vector(self, dve):
        pass


class Modulation(Stage):

    PER_LAYER = 6 * D // WIDE

    def __init__(self, core, rows):
        super().__init__(core)
        self.rows = rows
        self.g0 = core.plan([1] * (2 * self.PER_LAYER))

    def sync(self, sp):
        c = self.c
        sp.dma_start(c.small[:], c.dram["small"]).then_inc(c.small_in, 16)
        for g in range(SLOTS):
            c.load(sp, g, columns(c.dram["w_mod"][0], g * WIDE))
        sp.dma_start(c.X[:], c.dram["xT"]).then_inc(c.x_in, 16)
        rounds = self.PER_LAYER // SLOTS
        for layer in range(2):
            with sp.Fori(1 if layer == 0 else 0, rounds) as i:
                for j in range(SLOTS):
                    src = c.dram["w_mod"][layer][:, bass.ds(i * (SLOTS * WIDE) + j * WIDE, WIDE)]
                    sp.wait_ge(c.mm_done, i * SLOTS + (layer * rounds - 1) * SLOTS + j + 1)
                    sp.dma_start(c.wide(j), src.rearrange("(k p) m -> p k m", p=P)).then_inc(c.ring_full[j], 16)

    def scalar(self, act):
        c = self.c
        act.wait_ge(c.small_in, 16)
        act.activation(c.s("cond"), c.s("cond"), ACT.Silu).then_inc(self.scalar_done, self.act.mark("cond"))
        with act.Fori(0, 2 * self.PER_LAYER // SLOTS) as i:
            for j in range(SLOTS):
                act.wait_ge(c.mm_done, i * SLOTS + j + 1)
                act.activation(self.rows[0:2, bass.ds(i * (SLOTS * WIDE) + j * WIDE, WIDE)],
                               c.ps[0:2, j, 0:WIDE], ACT.Copy).then_inc(c.mod_moved, 1)
        act.wait_ge(self.vector_done, self.dve.at("mod"))
        act.wait_ge(c.x_in, 16)
        for k in range(KC):
            for st, t0 in ((0, 0), (1, CTX)):
                act.activation(c.H[:, k, t0:t0 + 256], c.X[:, k, t0:t0 + 256], ACT.Identity,
                               bias=c.mod(0, 0, k, st), scale=c.mod(0, 1, k, st))

    def tensor(self, pe):
        c = self.c
        pe.wait_ge(self.scalar_done, self.act.at("cond"))
        cond = c.s("cond").rearrange("p (k s) -> p k s", k=KC)

        def slot(j, i, reused):
            c.arrived(pe, j, i)
            if reused:
                pe.wait_ge(c.mod_moved, (j + 1 - SLOTS) + (SLOTS if i is None else i * SLOTS))
            for k in range(KC):
                mm = pe.matmul(c.ps[0:2, j, 0:WIDE], cond[:, k, :], c.wide(j)[:, k, :], start=(k == 0), stop=(k == KC - 1))
            mm.then_inc(c.mm_done, 1)

        for j in range(SLOTS):
            slot(j, None, False)
        with pe.Fori(1, 2 * self.PER_LAYER // SLOTS) as i:
            for j in range(SLOTS):
                slot(j, i, True)
        pe.wait_ge(c.mod_moved, 2 * self.PER_LAYER)
        for n in range(96):
            tr = pe.transpose(c.ps[:, 6, 2 * n:2 * n + 2], self.rows[0:2, n * P:(n + 1) * P], c.s("ident")[0:2, 0:2])
        tr.then_inc(self.tensor_done, self.pe.mark("turned"))

    def vector(self, dve):
        c = self.c
        dve.wait_ge(c.small_in, 16)
        dve.wait_ge(self.tensor_done, self.pe.at("turned"))
        ps = c.ps[:, 6, 0:192].rearrange("p (c s) -> p c s", s=2)
        for st in range(2):
            dve.tensor_tensor(c.MOD[:, :, st], ps[:, :, st], c.s("b_mod"), ALU.add)\
               .then_inc(self.vector_done, self.dve.mark("bias", st))
        dve.wait_ge(self.vector_done, self.dve.at("bias", 1))
        parts = c.MOD[:].rearrange("p (l t k) s -> p l t (k s)", l=2, t=6)
        dve.tensor_scalar(parts[:, :, 1, :], parts[:, :, 1, :], 1.0, None, ALU.add)
        dve.tensor_scalar(parts[:, :, 4, :], parts[:, :, 4, :], 1.0, None, ALU.add)\
           .then_inc(self.vector_done, self.dve.mark("mod"))


class Project(Stage):

    BANKS = 4

    def __init__(self, core, src, sources, items):
        super().__init__(core)
        self.src, self.sources, self.items = src, sources, items
        self.f0 = core.finished
        self.g0 = core.plan([sum(1 for it in items if it[0] == s) for s in range(len(sources))])

    def sync(self, sp):
        for s, src in enumerate(self.sources):
            self.c.load(sp, self.g0 + s, src)

    def out(self, i):
        _, kind, lo, n, t0, tn, _ = self.items[i]
        rows, cols = (n, tn) if kind == "feature" else (tn, n)
        return self.c.ps[0:rows, i % self.BANKS, 0:cols]

    def tensor(self, pe):
        c = self.c
        last = -1
        for i, (s, kind, lo, n, t0, tn, _) in enumerate(self.items):
            if s != last:
                c.arrived(pe, self.g0 + s)
                last = s
            if i >= self.BANKS:
                pe.wait_ge(self.scalar_done, self.act.at("moved", i - self.BANKS))
            w = c.wide(self.g0 + s)
            for k in range(KC):
                wk, xk = w[:, k, lo:lo + n], self.src[:, k, t0:t0 + tn]
                a, b = (wk, xk) if kind == "feature" else (xk, wk)
                mm = pe.matmul(self.out(i), a, b, start=(k == 0), stop=(k == KC - 1))
            mm.then_inc(c.mm_done, 1)

    def scalar(self, act):
        for i, it in enumerate(self.items):
            act.wait_ge(self.c.mm_done, self.f0 + i + 1)
            it[6](act, self.out(i)).then_inc(self.scalar_done, self.act.mark("moved", i))


def move_to(dst, scale=1.0):
    return lambda act, ps: act.activation(dst, ps, ACT.Copy, scale=scale)


def feature_items(dst, slots, t0, tn, scale=1.0, first=0):
    out = []
    for n, s in enumerate(slots):
        for m in range(2):
            out.append((s, "feature", m * P, P, t0, tn, move_to(dst[:, first + 2 * n + m, t0:t0 + tn], scale)))
    return out


def token_items(dst, slots, tiles, lo=0, n=WIDE, at=0):
    out = []
    for j, s in enumerate(slots):
        for t, (t0, tn) in enumerate(tiles):
            out.append((s, "token", lo, n, t0, tn, move_to(dst[0:tn, t, at + j * WIDE:at + j * WIDE + n])))
    return out


class Rope(Stage):

    def __init__(self, core, chunks, hd, tmp, copies=()):
        super().__init__(core)
        self.chunks, self.hd, self.tmp, self.copies = chunks, hd, tmp, copies

    def tensor(self, pe):
        c = self.c
        for i, x in enumerate(self.chunks):
            if i >= 4:
                pe.wait_ge(self.vector_done, self.dve.at("sin", i - 4))
            pe.matmul(c.ps[:, i % 4, 0:SEQ], c.s(f"rot{self.hd}"), x, start=True, stop=True).then_inc(self.tensor_done, self.pe.mark(i))

    def vector(self, dve):
        c = self.c
        for i, x in enumerate(self.chunks):
            dve.wait_ge(self.tensor_done, self.pe.at(i))
            t = self.tmp[:, i % 2, 0:SEQ]
            if i >= 2:
                dve.wait_ge(self.vector_done, self.dve.at("sum", i - 2))
            dve.tensor_tensor(t, c.ps[:, i % 4, 0:SEQ], c.s(f"sin{self.hd}"), ALU.mult).then_inc(self.vector_done, self.dve.mark("sin", i))
            dve.tensor_tensor(x, x, c.s(f"cos{self.hd}"), ALU.mult).then_inc(self.vector_done, self.dve.mark("cos", i))
            dve.wait_ge(self.vector_done, self.dve.at("cos", i))
            dve.tensor_tensor(x, x, t, ALU.add).then_inc(self.vector_done, self.dve.mark("sum", i))
        dve.wait_ge(self.vector_done, self.dve.at("sum", len(self.chunks) - 1))
        for dst, src in self.copies:
            dve.tensor_copy(dst, src)


class HeadNorm(Stage):

    def __init__(self, core, items, eps, sq, rs, after=1.0):
        super().__init__(core)
        self.after = after
        self.items, self.eps, self.sq, self.rs = items, eps, sq, rs
        self.width = max(len(it[0]) for it in items)

    def scalar(self, act):
        c = self.c
        N = len(self.items)
        for i in range(N + 1):
            if i < N:
                chunks, tn = self.items[i][0], self.items[i][1]
                for j, x in enumerate(chunks):
                    if i >= 2 and j == 0:
                        act.wait_ge(self.tensor_done, self.pe.at(i - 2))
                    act.activation(self.sq[:, (i % 2) * self.width + j, 0:tn], x, ACT.Square).then_inc(self.scalar_done, self.act.mark("sq", i, j))
            if i >= 1:
                tn = self.items[i - 1][1]
                act.wait_ge(self.vector_done, self.dve.at("var", i - 1))
                rs = self.rs[:, (i - 1) % 2, 0:tn]
                act.activation(rs, rs, ACT.Sqrt).then_inc(self.scalar_done, self.act.mark("sd", i - 1))

    def tensor(self, pe):
        c = self.c
        for i, (chunks, tn, ones, *_) in enumerate(self.items):
            if i >= 4:
                pe.wait_ge(self.vector_done, self.dve.at("var", i - 4))
            for j in range(len(chunks)):
                pe.wait_ge(self.scalar_done, self.act.at("sq", i, j))
                mm = pe.matmul(c.ps[:, i % 4, 0:tn], ones, self.sq[:, (i % 2) * self.width + j, 0:tn],
                               start=(j == 0), stop=(j == len(chunks) - 1))
            mm.then_inc(self.tensor_done, self.pe.mark(i))

    def vector(self, dve):
        c = self.c
        N = len(self.items)
        for i in range(N + 1):
            if i < N:
                tn, n = self.items[i][1], self.items[i][3]
                dve.wait_ge(self.tensor_done, self.pe.at(i))
                if i >= 2:
                    dve.wait_ge(self.vector_done, self.dve.at("out", i - 2))
                rs = self.rs[:, i % 2, 0:tn]
                dve.tensor_scalar(rs, c.ps[:, i % 4, 0:tn], 1.0 / n, self.eps, ALU.mult, ALU.add).then_inc(self.vector_done, self.dve.mark("var", i))
            if i >= 1:
                chunks, tn, _, _, gains, factor = self.items[i - 1]
                rs = self.rs[:, (i - 1) % 2, 0:tn]
                dve.wait_ge(self.scalar_done, self.act.at("sd", i - 1))
                dve.reciprocal(rs, rs).then_inc(self.vector_done, self.dve.mark("rs", i - 1))
                dve.wait_ge(self.vector_done, self.dve.at("rs", i - 1))
                if self.after != 1.0:
                    dve.tensor_scalar(rs, rs, self.after, None, ALU.mult).then_inc(self.vector_done, self.dve.mark("rsf", i - 1))
                    dve.wait_ge(self.vector_done, self.dve.at("rsf", i - 1))
                for j, x in enumerate(chunks):
                    g = gains[j] if gains else factor
                    ins = dve.scalar_tensor_tensor(x, x, g, rs, ALU.mult, ALU.mult)
                ins.then_inc(self.vector_done, self.dve.mark("out", i - 1))


class Attention(Stage):

    def __init__(self, core, items, p, s, pT, cols):
        super().__init__(core)
        self.items, self.p, self.sb, self.pT, self.cols = items, p, s, pT, cols

    def bank(self, i, m):
        return (i % 2) * 2 + m

    def blocks(self, it):
        return [(lo, n) for lo, n, _ in it["values"]]

    def tensor(self, pe):
        c, N = self.c, len(self.items)
        ident = c.s("ident")
        for step in range(N + 2):
            if step < N:
                i, it = step, self.items[step]
                if i >= 2:
                    for m in range(len(self.items[i - 2]["maps"])):
                        pe.wait_ge(self.scalar_done, self.act.at("exp", i - 2, m))
                for m, products in enumerate(it["maps"]):
                    for n, (a, b) in enumerate(products):
                        mm = pe.matmul(c.ps[0:it["rows"], self.bank(i, m), 0:it["keys"]], a, b,
                                       start=(n == 0), stop=(n == len(products) - 1))
                    mm.then_inc(self.tensor_done, self.pe.mark("scores", i, m))
            if 1 <= step <= N:
                i, it = step - 1, self.items[step - 1]
                pe.wait_ge(self.vector_done, self.dve.at("weights", i))
                if i >= 2:
                    pe.wait_ge(self.scalar_done, self.act.at("turned", i - 2))
                for b, (lo, n) in enumerate(self.blocks(it)):
                    tr = pe.transpose(c.ps[0:n, 4 + i % 2, b * P:b * P + it["rows"]],
                                      self.p[0:it["rows"], 2 * (i % 2), lo:lo + n], ident[0:it["rows"], 0:it["rows"]])
                tr.then_inc(self.tensor_done, self.pe.mark("turned", i))
            if step >= 2:
                i, it = step - 2, self.items[step - 2]
                pe.wait_ge(self.scalar_done, self.act.at("turned", i))
                if i >= 2:
                    pe.wait_ge(self.scalar_done, self.act.at("out", i - 2))
                o = self.out_ps(i)
                for b, (lo, n, v) in enumerate(it["values"]):
                    mm = pe.matmul(o, v, self.pT[0:n, i % 2, b * P:b * P + it["rows"]],
                                   start=(b == 0), stop=(b == len(it["values"]) - 1))
                mm.then_inc(self.tensor_done, self.pe.mark("out", i))

    def out_ps(self, i):
        it = self.items[i]
        lo, n = it["out_rows"]
        return self.c.ps[lo:lo + n, 6 + i % 2, 0:it["rows"]]

    def vector(self, dve):
        c, N = self.c, len(self.items)
        for step in range(N + 1):
            if step < N:
                i, it = step, self.items[step]
                R, K = it["rows"], it["keys"]
                for m in range(len(it["maps"])):
                    col = self.cols[0:R, self.bank(i, m), :]
                    dve.wait_ge(self.tensor_done, self.pe.at("scores", i, m))
                    if i >= 2:
                        dve.wait_ge(self.scalar_done, self.act.at("exp", i - 2, m if m < len(self.items[i - 2]["maps"]) else 0))
                        dve.wait_ge(self.vector_done, self.dve.at("weights", i - 2))
                    src = c.ps[0:R, self.bank(i, m), 0:K]
                    if it.get("masks"):
                        dst = self.sb[0:R, self.bank(i, m), 0:K]
                        qbias = it.get("qbias")
                        covered = 0
                        for mask, lo, hi in it["masks"] + [(None, K, K)]:
                            if lo > covered:
                                ins = dve.tensor_scalar(dst[:, covered:lo], src[:, covered:lo], it["scale"],
                                                        0.0 if qbias is None else qbias, ALU.mult, ALU.add)
                            if mask is not None:
                                ins = dve.scalar_tensor_tensor(dst[:, lo:hi], src[:, lo:hi],
                                                               it["scale"] if qbias is None else qbias, mask,
                                                               ALU.mult if qbias is None else ALU.add, ALU.add)
                            covered = hi
                        ins.then_inc(self.vector_done, self.dve.mark("masked", i, m))
                        dve.wait_ge(self.vector_done, self.dve.at("masked", i, m))
                        src, scale = dst, 1.0
                    else:
                        scale = it["scale"]
                    dve.reduce_max(col[:, 0:1], src, AX_X).then_inc(self.vector_done, self.dve.mark("max", i, m))
                    dve.wait_ge(self.vector_done, self.dve.at("max", i, m))
                    if it.get("sink") is not None:
                        dve.tensor_scalar(col[:, 1:2], col[:, 0:1], scale, it["sink"], ALU.mult, ALU.max).then_inc(self.vector_done, self.dve.mark("smax", i, m))
                        dve.wait_ge(self.vector_done, self.dve.at("smax", i, m))
                        dve.tensor_scalar(col[:, 2:3], col[:, 1:2], -1.0, None, ALU.mult).then_inc(self.vector_done, self.dve.mark("neg", i, m))
                    else:
                        dve.tensor_scalar(col[:, 2:3], col[:, 0:1], -scale, None, ALU.mult).then_inc(self.vector_done, self.dve.mark("neg", i, m))
            if step >= 1:
                i, it = step - 1, self.items[step - 1]
                R, K, M = it["rows"], it["keys"], len(it["maps"])
                for m in range(M):
                    col = self.cols[0:R, self.bank(i, m), :]
                    dve.wait_ge(self.scalar_done, self.act.at("exp", i, m))
                    total = col[:, 3:4]
                    if it.get("sink") is not None:
                        dve.wait_ge(self.scalar_done, self.act.at("esink", i, m))
                        dve.tensor_tensor(col[:, 5:6], col[:, 3:4], col[:, 4:5], ALU.add).then_inc(self.vector_done, self.dve.mark("total", i, m))
                        dve.wait_ge(self.vector_done, self.dve.at("total", i, m))
                        total = col[:, 5:6]
                    dve.reciprocal(col[:, 6:7], total).then_inc(self.vector_done, self.dve.mark("rec", i, m))
                    dve.wait_ge(self.vector_done, self.dve.at("rec", i, m))
                p0 = self.p[0:R, 2 * (i % 2), 0:K]
                col = self.cols[0:R, self.bank(i, 0), :]
                ins = dve.tensor_scalar(p0, p0, col[:, 6:7], None, ALU.mult)
                if M == 2:
                    ins.then_inc(self.vector_done, self.dve.mark("p0", i))
                    p1 = self.p[0:R, 2 * (i % 2) + 1, 0:K]
                    col1 = self.cols[0:R, self.bank(i, 1), :]
                    dve.tensor_tensor(col1[:, 7:8], col1[:, 6:7], it["lam"], ALU.mult).then_inc(self.vector_done, self.dve.mark("lr", i))
                    dve.wait_ge(self.vector_done, self.dve.at("lr", i))
                    ins = dve.scalar_tensor_tensor(p0, p1, col1[:, 7:8], p0, ALU.mult, ALU.add)
                ins.then_inc(self.vector_done, self.dve.mark("weights", i))

    def scalar(self, act):
        c, N = self.c, len(self.items)
        for step in range(N + 2):
            if step < N:
                i, it = step, self.items[step]
                R, K = it["rows"], it["keys"]
                for m in range(len(it["maps"])):
                    col = self.cols[0:R, self.bank(i, m), :]
                    act.wait_ge(self.vector_done, self.dve.at("neg", i, m))
                    if i >= 2:
                        act.wait_ge(self.tensor_done, self.pe.at("turned", i - 2))
                    masked = bool(it.get("masks"))
                    src = self.sb[0:R, self.bank(i, m), 0:K] if masked else c.ps[0:R, self.bank(i, m), 0:K]
                    if it.get("sink") is not None:
                        act.activation(col[:, 4:5], it["sink"], ACT.Exp, bias=col[:, 2:3]).then_inc(self.scalar_done, self.act.mark("esink", i, m))
                    act.activation(self.p[0:R, 2 * (i % 2) + m, 0:K], src, ACT.Exp, bias=col[:, 2:3],
                                              scale=1.0 if masked else it["scale"], accum_out=col[:, 3:4]).then_inc(self.scalar_done, self.act.mark("exp", i, m))
            if 1 <= step <= N:
                i, it = step - 1, self.items[step - 1]
                act.wait_ge(self.tensor_done, self.pe.at("turned", i))
                if i >= 2:
                    act.wait_ge(self.tensor_done, self.pe.at("out", i - 2))
                R = it["rows"]
                full = all(n == P for _, n in self.blocks(it)) and R == P
                if full:
                    w = len(self.blocks(it)) * P
                    ins = act.activation(self.pT[:, i % 2, 0:w], c.ps[:, 4 + i % 2, 0:w], ACT.Copy)
                else:
                    for b, (lo, n) in enumerate(self.blocks(it)):
                        ins = act.activation(self.pT[0:n, i % 2, b * P:b * P + R], c.ps[0:n, 4 + i % 2, b * P:b * P + R],
                                             ACT.Copy)
                ins.then_inc(self.scalar_done, self.act.mark("turned", i))
            if step >= 2:
                i, it = step - 2, self.items[step - 2]
                act.wait_ge(self.tensor_done, self.pe.at("out", i))
                act.activation(it["out"], self.out_ps(i), ACT.Copy).then_inc(self.scalar_done, self.act.mark("out", i))


class LayerNorm(Stage):

    def __init__(self, core, layer, which, streams, nxt, shift_to=None):
        super().__init__(core)
        self.layer, self.which, self.streams, self.nxt, self.shift_to = layer, which, streams, nxt, shift_to
        self.t0 = streams[0][1]
        self.tn = 256 * len(streams)

    def scalar(self, act):
        c, t = self.c, slice(self.t0, self.t0 + self.tn)
        for k in range(KC):
            act.activation(c.H[:, k, t], c.X[:, k, t], ACT.Copy, scale=ALPHA).then_inc(self.scalar_done, self.act.mark("ax", k))
        for k in range(KC):
            act.wait_ge(self.vector_done, self.dve.at("centred", k))
            act.activation(c.H[:, k, t], c.ACC[:, k, t], ACT.Square).then_inc(self.scalar_done, self.act.mark("sq", k))
        act.wait_ge(self.vector_done, self.dve.at("var"))
        act.activation(c.stat[:, 0, 0:self.tn], c.stat[:, 0, 0:self.tn], ACT.Sqrt).then_inc(self.scalar_done, self.act.mark("sd"))
        col = self.layer * 16 + self.which * 8
        for k in range(KC):
            act.wait_ge(self.vector_done, self.dve.at("normed", k))
            dst = c.X[:, k, t] if self.shift_to is None else c.X[:, k, self.shift_to:self.shift_to + self.tn]
            act.activation(dst, c.ACC[:, k, t], ACT.Identity, bias=c.s("ln_b")[:, col + k:col + k + 1],
                                      scale=c.s("ln_g")[:, col + k:col + k + 1]).then_inc(self.scalar_done, self.act.mark("x", k))
        if self.shift_to is not None:
            act.activation(c.X[:, :, 0:META], c.s("meta").rearrange("p (k t) -> p k t", k=KC), ACT.Copy)

    def tensor(self, pe):
        c, t = self.c, slice(self.t0, self.t0 + self.tn)
        for k in range(KC):
            pe.wait_ge(self.vector_done, self.dve.at("z", k))
            mm = pe.matmul(c.ps[:, 0, 0:self.tn], c.s("ones"), c.ACC[:, k, t], start=(k == 0), stop=(k == KC - 1))
        mm.then_inc(self.tensor_done, self.pe.mark("sum"))
        for k in range(KC):
            pe.wait_ge(self.scalar_done, self.act.at("sq", k))
            mm = pe.matmul(c.ps[:, 1, 0:self.tn], c.s("ones"), c.H[:, k, t], start=(k == 0), stop=(k == KC - 1))
        mm.then_inc(self.tensor_done, self.pe.mark("sumsq"))

    def vector(self, dve):
        c, t = self.c, slice(self.t0, self.t0 + self.tn)
        gate = 2 if self.which == 0 else 5
        for k in range(KC):
            dve.wait_ge(self.scalar_done, self.act.at("ax", k))
            for st, s0 in self.streams:
                u = slice(s0, s0 + 256)
                ins = dve.scalar_tensor_tensor(c.ACC[:, k, u], c.ACC[:, k, u], c.mod(self.layer, gate, k, st),
                                               c.H[:, k, u], ALU.mult, ALU.add)
            ins.then_inc(self.vector_done, self.dve.mark("z", k))
        dve.wait_ge(self.tensor_done, self.pe.at("sum"))
        for k in range(KC):
            dve.scalar_tensor_tensor(c.ACC[:, k, t], c.ps[:, 0, 0:self.tn], -1.0 / D, c.ACC[:, k, t],
                                                ALU.mult, ALU.add).then_inc(self.vector_done, self.dve.mark("centred", k))
        dve.wait_ge(self.tensor_done, self.pe.at("sumsq"))
        rs = c.stat[:, 0, 0:self.tn]
        dve.tensor_scalar(rs, c.ps[:, 1, 0:self.tn], 1.0 / D, LN_EPS, ALU.mult, ALU.add).then_inc(self.vector_done, self.dve.mark("var"))
        dve.wait_ge(self.scalar_done, self.act.at("sd"))
        dve.reciprocal(rs, rs).then_inc(self.vector_done, self.dve.mark("rs"))
        dve.wait_ge(self.vector_done, self.dve.at("rs"))
        for k in range(KC):
            dve.tensor_tensor(c.ACC[:, k, t], c.ACC[:, k, t], rs, ALU.mult).then_inc(self.vector_done, self.dve.mark("normed", k))
        if self.nxt:
            layer, part = self.nxt
            for k in range(KC):
                dve.wait_ge(self.scalar_done, self.act.at("x", k))
                for st, s0 in (self.streams if self.which == 0 else ((0, 0), (1, CTX))):
                    u = slice(s0, s0 + 256)
                    dve.tensor_scalar(c.H[:, k, u], c.X[:, k, u], c.mod(layer, part + 1, k, st),
                                      c.mod(layer, part, k, st), ALU.mult, ALU.add)


class RmsNorm(Stage):

    def __init__(self, core, gain, add):
        super().__init__(core)
        self.gain, self.add = gain, add

    def scalar(self, act):
        c = self.c
        for k in range(KC):
            if self.add:
                act.wait_ge(self.vector_done, self.dve.at("x", k))
            act.activation(c.H[:, k, 0:T2], c.X[:, k, 0:T2], ACT.Square).then_inc(self.scalar_done, self.act.mark("sq", k))
        act.wait_ge(self.vector_done, self.dve.at("var"))
        act.activation(c.stat[:, 0, 0:T2], c.stat[:, 0, 0:T2], ACT.Sqrt).then_inc(self.scalar_done, self.act.mark("sd"))

    def tensor(self, pe):
        c = self.c
        for k in range(KC):
            pe.wait_ge(self.scalar_done, self.act.at("sq", k))
            mm = pe.matmul(c.ps[:, 0, 0:T2], c.s("ones"), c.H[:, k, 0:T2], start=(k == 0), stop=(k == KC - 1))
        mm.then_inc(self.tensor_done, self.pe.mark("sumsq"))

    def vector(self, dve):
        c = self.c
        if self.add:
            for k in range(KC):
                dve.tensor_tensor(c.X[:, k, 0:T2], c.X[:, k, 0:T2], c.ACC[:, k, 0:T2], ALU.add).then_inc(self.vector_done, self.dve.mark("x", k))
        dve.wait_ge(self.tensor_done, self.pe.at("sumsq"))
        rs = c.stat[:, 0, 0:T2]
        dve.tensor_scalar(rs, c.ps[:, 0, 0:T2], 1.0 / D, NORM_EPS, ALU.mult, ALU.add).then_inc(self.vector_done, self.dve.mark("var"))
        dve.wait_ge(self.scalar_done, self.act.at("sd"))
        dve.reciprocal(rs, rs).then_inc(self.vector_done, self.dve.mark("rs"))
        dve.wait_ge(self.vector_done, self.dve.at("rs"))
        for k in range(KC):
            dve.scalar_tensor_tensor(c.H[:, k, 0:T2], c.X[:, k, 0:T2], self.gain[:, k:k + 1], rs, ALU.mult, ALU.mult)


class Router(Stage):

    def __init__(self, core, t0, tn, m):
        super().__init__(core)
        self.t0, self.tn, self.nt, self.m = t0, tn, tn // P, m

    def tensor(self, pe):
        c, nt = self.c, self.nt
        w = c.s("w_router").rearrange("p (k e) -> p k e", k=KC)
        for t in range(nt):
            for k in range(KC):
                mm = pe.matmul(c.ps[:, 0, t * 16:(t + 1) * 16], c.H[:, k, self.t0 + t * P:self.t0 + (t + 1) * P],
                               w[:, k, :], start=(k == 0), stop=(k == KC - 1))
        mm.then_inc(self.tensor_done, self.pe.mark("logits"))
        pe.wait_ge(self.vector_done, self.dve.at("gates"))
        for t in range(nt):
            tr = pe.transpose(c.ps[0:16, 1, t * P:(t + 1) * P], self.m["g"][:, t, :], c.s("ident"))
        tr.then_inc(self.tensor_done, self.pe.mark("gT"))


    def scalar(self, act):
        c = self.c
        act.wait_ge(self.tensor_done, self.pe.at("logits"))
        sc = self.m["sc"].rearrange("p t e -> p (t e)")[:, 0:self.nt * 16]
        act.activation(sc, c.ps[:, 0, 0:self.nt * 16], ACT.Sigmoid).then_inc(self.scalar_done, self.act.mark("scores"))
        act.wait_ge(self.tensor_done, self.pe.at("gT"))
        act.activation(self.m["gT"][0:16, 0:self.tn], c.ps[0:16, 1, 0:self.tn], ACT.Copy).then_inc(self.scalar_done, self.act.mark("gT"))
        act.wait_ge(self.scalar_done, self.act.at("gT"))
        act.dma_start(c.dram["gates"][:, 0:self.tn], self.m["gT"][0:16, 0:self.tn]).then_inc(c.gates_stored, 16)

    def vector(self, dve):
        c, nt, m = self.c, self.nt, self.m
        n = [0]

        def step(ins):
            ins.then_inc(self.vector_done, self.dve.mark("pick", n[0]))
            dve.wait_ge(self.vector_done, self.dve.at("pick", n[0]))
            n[0] += 1

        sc, sel, a, b = (m[x][:, 0:nt, :] for x in ("sc", "sel", "ta", "tb"))
        dve.wait_ge(self.scalar_done, self.act.at("scores"))
        bias = c.s("b_router").unsqueeze(1).to_broadcast([P, nt, 16])
        step(dve.tensor_tensor(sel, sc, bias, ALU.add))
        v = sel.rearrange("p t (g e) -> p (t g) e", e=4)
        hi, lo = m["hi"][:, 0:nt * 4, :], m["lo"][:, 0:nt * 4, :]
        dve.tensor_tensor(hi, v[:, :, 0:2], v[:, :, 2:4], ALU.max)
        step(dve.tensor_tensor(lo, v[:, :, 0:2], v[:, :, 2:4], ALU.min))
        gs, g2, g3 = (m["gs"][:, j, 0:nt * 4] for j in range(3))
        dve.tensor_tensor(gs, hi[:, :, 0], hi[:, :, 1], ALU.max)
        dve.tensor_tensor(g2, hi[:, :, 0], hi[:, :, 1], ALU.min)
        step(dve.tensor_tensor(g3, lo[:, :, 0], lo[:, :, 1], ALU.max))
        step(dve.tensor_tensor(g2, g2, g3, ALU.max))
        step(dve.tensor_tensor(gs, gs, g2, ALU.add))
        gv, g2v = (x.rearrange("p (t g) -> p t g", g=4) for x in (gs, g2))
        mx = m["mx"][:, 0:nt]
        mxb4 = mx.unsqueeze(2).to_broadcast([P, nt, 4])
        mxb16 = mx.unsqueeze(2).to_broadcast([P, nt, 16])
        step(dve.reduce_max(mx, gv, AX_X))
        step(dve.tensor_tensor(g2v, gv, mxb4, ALU.is_ge))
        step(dve.tensor_tensor(g2v, g2v, c.s("group_rank").unsqueeze(1).to_broadcast([P, nt, 4]), ALU.mult))
        step(dve.reduce_max(mx, g2v, AX_X))
        step(dve.tensor_tensor(g2v, g2v, mxb4, ALU.is_ge))
        member = g2.unsqueeze(2).to_broadcast([P, nt * 4, 4])
        step(dve.tensor_tensor(v, v, member, ALU.mult))
        step(dve.tensor_scalar(g3, g2, -1.0, BIG, ALU.add, ALU.mult))
        step(dve.tensor_tensor(v, v, g3.unsqueeze(2).to_broadcast([P, nt * 4, 4]), ALU.add))
        rank = c.s("expert_rank").unsqueeze(1).to_broadcast([P, nt, 16])
        picked = m["g"][:, 0:nt, :]
        for n_pick in range(2):
            step(dve.reduce_max(mx, sel, AX_X))
            step(dve.tensor_tensor(a, sel, mxb16, ALU.is_ge))
            step(dve.tensor_tensor(a, a, rank, ALU.mult))
            step(dve.reduce_max(mx, a, AX_X))
            step(dve.tensor_tensor(a, a, mxb16, ALU.is_ge))
            if n_pick == 0:
                step(dve.scalar_tensor_tensor(sel, a, -2.0 * BIG, sel, ALU.mult, ALU.add))
                step(dve.tensor_copy(b, a))
            else:
                step(dve.tensor_tensor(a, a, b, ALU.add))
        step(dve.tensor_tensor(a, a, sc, ALU.mult))
        step(dve.reduce_sum(mx, a, AX_X))
        step(dve.reciprocal(mx, mx))
        dve.tensor_tensor(picked, a, mxb16, ALU.mult).then_inc(self.vector_done, self.dve.mark("gates"))


class FeedForward(Stage):

    def __init__(self, core, t0, tn, groups, gate, up, down, gates=0):
        super().__init__(core)
        self.t0, self.tn, self.N = t0, tn, groups
        self.src = {"G": gate, "U": up, "D": down}
        self.gates = gates
        self.R = (groups - 2) // 2
        self.M0 = core.finished
        self.g0 = core.plan([2, 2] + [2, 2, 8] * (groups - 1) + [8])
        self.L0 = core.splits
        core.splits += 2 * 3 * groups
        core.release[self.g0:] = [(core.lo_done, self.L0 + 2 * (p + 1)) for p in range(3 * groups)]
        self.s0, self.a0, self.q0 = core.silus, core.gates, core.muls
        core.silus += 2 * groups
        core.gates += 2 * groups
        self.ops = 3 if gates else 2
        core.muls += 2 * self.ops * groups
        self.d0 = core.adds + KC
        core.adds += KC + KC * groups
        self.r0 = core.gate_loads
        if gates:
            core.gate_loads += groups // 2

    def pos(self, kind, n):
        if kind == "D":
            return 4 + 3 * n if n < self.N - 1 else 2 + 3 * n
        return (kind == "U") + (0 if n == 0 else 2 + 3 * (n - 1))

    def result(self, kind, n):
        if kind == "D":
            return self.M0 + 4 + 12 * n + (4 if n < self.N - 1 else 0)
        return self.M0 + (2 if kind == "U" else 0) + (0 if n == 0 else 4 + 12 * (n - 1))

    def through(self, p):
        if p < 2:
            return self.M0 + 2 * (p + 1)
        step, j = divmod(p - 2, 3)
        return self.M0 + 4 + 12 * step + (2, 4, 12)[j]

    @staticmethod
    def at(v, i, per_round):
        return v if i is None else v + i * per_round

    def load(self, sp, kind, n, i=None):
        c, g = self.c, self.g0 + self.pos(kind, n)
        offset = (lambda size: (n // 2) * size) if i is None else (lambda size: i * size + (n // 2) * size)
        if i is None:
            sem, count = c.release[g - SLOTS]
            sp.wait_ge(sem, count)
        else:
            sp.wait_ge(c.lo_done, i * 12 + (self.L0 + 2 * (g - self.g0 + 1) - 12))
        src = self.src[kind](offset, n % 2)
        dst = c.ring[:, g % SLOTS, :].rearrange("p (k m) -> p k m", k=src.shape[1])
        sp.dma_start(dst, src).then_inc(c.ring_full[g % SLOTS], 16)

    def sync(self, sp):
        self.load(sp, "G", 0)
        self.load(sp, "U", 0)

        def step(n, i=None):
            self.load(sp, "G", n + 1, i)
            self.load(sp, "U", n + 1, i)
            self.load(sp, "D", n, i)

        step(0)
        step(1)
        with sp.Fori(1, self.R) as i:
            step(0, i)
            step(1, i)
        for n in range(2 * self.R, self.N - 1):
            step(n)
        self.load(sp, "D", self.N - 1)

    def tensor(self, pe):
        c, tn = self.c, self.tn
        Hh, Hl = c.HS
        Wh, Wl = c.WS
        Ah, Al = c.AS
        X = slice(0, tn)

        def split_slot(kind, n, i, k):
            p = self.pos(kind, n)
            pe.wait_ge(c.lo_done, self.at(self.L0 + 2 * (p + 1), i, 12))
            return [w[:, p % SPLIT_SLOTS, :].rearrange("p (k m) -> p k m", k=k) for w in (Wh, Wl)]

        def wide(kind, n, i=None):
            wh, wl = split_slot(kind, n, i, KC)
            for u in range(2):
                if n > 0:
                    if kind == "G":
                        pe.wait_ge(c.silu_done, self.at(self.s0 + 2 * (n - 1) + u + 1, i, 4))
                    else:
                        pe.wait_ge(c.mul_done, self.at(self.q0 + 2 * self.ops * (n - 1) + u + 1, i, 4 * self.ops))
                out = c.ps[:, u + (2 if kind == "U" else 0), 0:tn]
                M = slice(u * P, (u + 1) * P)
                for k in range(KC):
                    if n == 0 and kind == "G" and u == 0:
                        pe.wait_ge(self.vector_done, self.dve.at("H", k))
                    pe.matmul(out, wh[:, k, M], Hh[:, k, X], start=(k == 0), stop=False)
                    pe.matmul(out, wh[:, k, M], Hl[:, k, X], start=False, stop=False)
                    mm = pe.matmul(out, wl[:, k, M], Hh[:, k, X], start=False, stop=(k == KC - 1))
                mm.then_inc(c.mm_done, 1)

        def down(n, i=None):
            wh, wl = split_slot("D", n, i, 2)
            pe.wait_ge(c.gated_done, self.at(self.a0 + 2 * n + 2, i, 4))
            for j in range(KC):
                pe.wait_ge(c.add_done, self.at(self.d0 + 8 * n + j - 3, i, 16))
                out = c.ps[:, 4 + j % 4, 0:tn]
                M = slice(j * P, (j + 1) * P)
                for k in range(2):
                    ah, al = (a[:, 2 * (n % 2) + k, X] for a in (Ah, Al))
                    pe.matmul(out, wh[:, k, M], ah, start=(k == 0), stop=False)
                    pe.matmul(out, wh[:, k, M], al, start=False, stop=False)
                    mm = pe.matmul(out, wl[:, k, M], ah, start=False, stop=(k == 1))
                mm.then_inc(c.mm_done, 1)

        def step(n, i=None):
            wide("G", n + 1, i)
            wide("U", n + 1, i)
            down(n, i)

        wide("G", 0)
        wide("U", 0)
        with pe.Fori(0, self.R) as i:
            step(0, i)
            step(1, i)
        for n in range(2 * self.R, self.N - 1):
            step(n)
        down(self.N - 1)

    def scalar(self, act):
        c, tn = self.c, self.tn

        def upper(kind, n, i=None):
            p = self.pos(kind, n)
            g = self.g0 + p
            c.arrived(act, g, i)
            if p >= SPLIT_SLOTS:
                act.wait_ge(c.mm_done, self.at(self.through(p - SPLIT_SLOTS), i, 24))
            for half in range(2):
                C = slice(half * SLOT // 2, (half + 1) * SLOT // 2)
                act.activation(c.WS[0][:, p % SPLIT_SLOTS, C], c.ring[:, g % SLOTS, C], ACT.Copy).then_inc(c.hi_done, 1)

        def silu(n, i=None):
            for u in range(2):
                if n > 0:
                    act.wait_ge(c.gated_done, self.at(self.a0 + 2 * (n - 1) + u + 1, i, 4))
                act.wait_ge(c.mm_done, self.at(self.result("G", n) + u + 1, i, 24))
                act.activation(c.stat[:, u, 0:tn], c.ps[:, u, 0:tn], ACT.Silu).then_inc(c.silu_done, 1)

        def gate_row(n, i=None):
            if not self.gates:
                return
            if n >= 2:
                act.wait_ge(c.gated_done, self.at(self.a0 + 2 * (n - 2) + 2, i, 4))
            e = n // 2 if i is None else i + n // 2
            row = c.dram["gates"][bass.ds(e, 1), 0:tn].to_broadcast([P, tn])
            act.dma_start(c.gate_row[:, n % 2, 0:tn], row).then_inc(c.gate_in[n % 2], 16)

        if self.gates:
            act.wait_ge(c.gates_stored, 16 * self.gates)
        for k in range(KC):
            act.activation(c.HS[0][:, k, 0:tn], c.H[:, k, self.t0:self.t0 + tn], ACT.Copy)\
               .then_inc(self.scalar_done, self.act.mark("H", k))
        gate_row(0)
        gate_row(1)
        upper("G", 0)
        upper("U", 0)
        silu(0)
        upper("G", 1)

        def step(n, i=None):
            upper("U", n + 1, i)
            silu(n + 1, i)
            upper("D", n, i)
            if i is not None or n + 2 < self.N:
                upper("G", n + 2, i)
                gate_row(n + 2, i)

        with act.Fori(0, self.R) as i:
            step(0, i)
            step(1, i)
        for n in range(2 * self.R, self.N - 1):
            step(n)
        upper("D", self.N - 1)

    def vector(self, dve):
        c, tn = self.c, self.tn
        Ah, Al = c.AS

        def lower(kind, n, i=None, halves=(0, 1)):
            p = self.pos(kind, n)
            for half in halves:
                C = slice(half * SLOT // 2, (half + 1) * SLOT // 2)
                hi, lo = (w[:, p % SPLIT_SLOTS, C] for w in c.WS)
                dve.wait_ge(c.hi_done, self.at(self.L0 + 2 * p + half + 1, i, 12))
                dve.tensor_tensor(lo, c.ring[:, (self.g0 + p) % SLOTS, C], hi.bitcast(F32), ALU.subtract)\
                   .then_inc(c.lo_done, 1)

        def gated(n, i=None):
            q = self.q0 + 2 * self.ops * n

            def product(op, u):
                return self.at(q + 2 * op + u + 1, i, 4 * self.ops)

            for u in range(2):
                dve.wait_ge(c.mm_done, self.at(self.result("U", n) + u + 1, i, 24))
                dve.wait_ge(c.silu_done, self.at(self.s0 + 2 * n + u + 1, i, 4))
                dve.tensor_tensor(c.stat[:, u, 0:tn], c.stat[:, u, 0:tn], c.ps[:, 2 + u, 0:tn], ALU.mult)\
                   .then_inc(c.mul_done, 1)
            if self.gates:
                dve.wait_ge(c.gate_in[n % 2], self.at(16 * (self.r0 + n // 2 + 1), i, 16))
                for u in range(2):
                    dve.wait_ge(c.mul_done, product(0, u))
                    dve.tensor_tensor(c.stat[:, u, 0:tn], c.stat[:, u, 0:tn], c.gate_row[:, n % 2, 0:tn], ALU.mult)\
                       .then_inc(c.mul_done, 1)
            for u in range(2):
                dve.wait_ge(c.mul_done, product(self.ops - 2, u))
                dve.tensor_copy(Ah[:, 2 * (n % 2) + u, 0:tn], c.stat[:, u, 0:tn]).then_inc(c.mul_done, 1)
            for u in range(2):
                dve.wait_ge(c.mul_done, product(self.ops - 1, u))
                hi = Ah[:, 2 * (n % 2) + u, 0:tn].bitcast(F32)
                dve.tensor_tensor(Al[:, 2 * (n % 2) + u, 0:tn], c.stat[:, u, 0:tn], hi, ALU.subtract)\
                   .then_inc(c.gated_done, 1)

        def add(n, js, i=None):
            for j in js:
                dve.wait_ge(c.mm_done, self.at(self.result("D", n) + j + 1, i, 24))
                dve.wait_ge(c.add_done, self.at(self.d0 + 8 * (n - 1) + j + 1, i, 16))
                acc = c.ACC[:, j, self.t0:self.t0 + tn]
                dve.tensor_tensor(acc, acc, c.ps[:, 4 + j % 4, 0:tn], ALU.add).then_inc(c.add_done, 1)

        for k in range(KC):
            dve.wait_ge(self.scalar_done, self.act.at("H", k))
            dve.tensor_tensor(c.HS[1][:, k, 0:tn], c.H[:, k, self.t0:self.t0 + tn], c.HS[0][:, k, 0:tn].bitcast(F32),
                              ALU.subtract).then_inc(self.vector_done, self.dve.mark("H", k))
        lower("G", 0)
        lower("U", 0)
        for j in range(KC):
            dve.memset(c.ACC[:, j, self.t0:self.t0 + tn], 0.0).then_inc(c.add_done, 1)
        lower("G", 1)

        def step(n, i=None):
            lower("U", n + 1, i)
            gated(n, i)
            lower("D", n, i)
            ahead = i is not None or n + 2 < self.N
            add(n, (0, 1), i)
            if ahead:
                lower("G", n + 2, i, halves=(0,))
            add(n, (2, 3), i)
            if ahead:
                lower("G", n + 2, i, halves=(1,))
            add(n, (4, 5, 6, 7), i)

        with dve.Fori(0, self.R) as i:
            step(0, i)
            step(1, i)
        for n in range(2 * self.R, self.N - 1):
            step(n)
        gated(self.N - 1)
        lower("D", self.N - 1)
        add(self.N - 1, range(KC))


class Lambda(Stage):

    def __init__(self, core, out):
        super().__init__(core)
        self.out = out

    def vector(self, dve):
        c = self.c
        v = c.s("lam").rearrange("p (j d) -> p j d", j=4)
        for j in range(2):
            dve.tensor_tensor(c.stat[:, j, 0:64], v[:, 2 * j, :], v[:, 2 * j + 1, :], ALU.mult).then_inc(self.vector_done, self.dve.mark("prod", j))
            dve.wait_ge(self.vector_done, self.dve.at("prod", j))
            dve.reduce_sum(self.out[:, j:j + 1], c.stat[:, j, 0:64], AX_X).then_inc(self.vector_done, self.dve.mark("sum", j))
        dve.wait_ge(self.scalar_done, self.act.at("exp"))
        dve.tensor_tensor(self.out[:, 2:3], self.out[:, 1:2], self.out[:, 0:1], ALU.subtract).then_inc(self.vector_done, self.dve.mark("d"))
        dve.wait_ge(self.vector_done, self.dve.at("d"))
        dve.tensor_scalar(self.out[:, 3:4], self.out[:, 2:3], -LAM_INIT, None, ALU.add)

    def scalar(self, act):
        c = self.c
        act.wait_ge(self.vector_done, self.dve.at("sum", 1))
        act.activation(self.out[:, 0:2], self.out[:, 0:2], ACT.Exp).then_inc(self.scalar_done, self.act.mark("exp"))


class LogForget(Stage):

    def __init__(self, core, wf, bf, m):
        super().__init__(core)
        self.wf, self.bf, self.m = wf, bf, m

    def tensor(self, pe):
        c, m = self.c, self.m
        for t, (t0, tn) in enumerate(TILES2):
            for k in range(KC):
                mm = pe.matmul(c.ps[0:tn, 0, t * 16:(t + 1) * 16], c.H[:, k, t0:t0 + tn], self.wf[:, k, :],
                               start=(k == 0), stop=(k == KC - 1))
            mm.then_inc(self.tensor_done, self.pe.mark("f", t))
        pe.wait_ge(self.vector_done, self.dve.at("lf", 2))
        for q, (q0, qn) in enumerate(TILES2):
            for s in range(q + 1):
                sn = TILES2[s][1]
                upto = c.s("upto" if s == q else "ones")[0:sn, 0:qn]
                pe.matmul(c.ps[0:qn, 1, q * 16:(q + 1) * 16], upto, m["lf"][0:sn, s, :], start=(s == 0), stop=(s == q))
            for s in range(q + 1):
                sn = TILES2[s][1]
                upto = c.s("upto" if s == q else "ones")[0:sn, 0:qn]
                mm = pe.matmul(c.ps[0:16, 2, q0:q0 + qn], m["lf"][0:sn, s, :], upto, start=(s == 0), stop=(s == q))
            mm.then_inc(self.tensor_done, self.pe.mark("c", q))

    def vector(self, dve):
        c, m = self.c, self.m
        for t, (t0, tn) in enumerate(TILES2):
            z, w = m["z"][0:tn, t, :], m["w"][0:tn, t, :]
            dve.wait_ge(self.tensor_done, self.pe.at("f", 2))
            dve.tensor_tensor(z, c.ps[0:tn, 0, t * 16:(t + 1) * 16], self.bf[0:tn], ALU.add).then_inc(self.vector_done, self.dve.mark("z", t))
            dve.wait_ge(self.vector_done, self.dve.at("z", t))
            dve.scalar_tensor_tensor(w, z, -1.0, z, ALU.mult, ALU.max).then_inc(self.vector_done, self.dve.mark("abs", t))
            dve.wait_ge(self.scalar_done, self.act.at("ln", t))
            dve.scalar_tensor_tensor(m["lf"][0:tn, t, :], z, 0.0, w, ALU.min, ALU.subtract).then_inc(self.vector_done, self.dve.mark("lf", t))

    def scalar(self, act):
        c, m = self.c, self.m
        for t, (t0, tn) in enumerate(TILES2):
            w = m["w"][0:tn, t, :]
            act.wait_ge(self.vector_done, self.dve.at("abs", t))
            act.activation(w, w, ACT.Exp, scale=-1.0).then_inc(self.scalar_done, self.act.mark("e", t))
            act.wait_ge(self.scalar_done, self.act.at("e", t))
            act.activation(w, w, ACT.Ln, bias=1.0).then_inc(self.scalar_done, self.act.mark("ln", t))
        act.wait_ge(self.tensor_done, self.pe.at("c", 2))
        for q, (q0, qn) in enumerate(TILES2):
            act.activation(m["C"][0:qn, q, :], c.ps[0:qn, 1, q * 16:(q + 1) * 16], ACT.Copy)
            act.activation(m["CT"][0:16, q0:q0 + qn], c.ps[0:16, 2, q0:q0 + qn], ACT.Copy, scale=-1.0)


class Multiply(Stage):

    def __init__(self, core, out, factor):
        super().__init__(core)
        self.out, self.factor = out, factor

    def vector(self, dve):
        for k in range(KC):
            dve.tensor_tensor(self.out[:, k, 0:T2], self.out[:, k, 0:T2], self.factor[:, k, 0:T2], ALU.mult)


class Store(Stage):

    def vector(self, dve):
        c = self.c
        for k in range(KC):
            dve.tensor_tensor(c.X[:, k, 0:T2], c.X[:, k, 0:T2], c.ACC[:, k, 0:T2], ALU.add).then_inc(self.vector_done, self.dve.mark("x", k))

    def sync(self, sp):
        c = self.c
        for k in range(KC):
            sp.wait_ge(self.vector_done, self.dve.at("x", k))
            sp.dma_start(c.dram["outT"][k * P:(k + 1) * P, :], c.X[:, k, META:T2]).then_inc(c.stored, 16)
        sp.wait_ge(c.stored, 16 * KC)


class GlaGates(Stage):

    def __init__(self, core, m):
        super().__init__(core)
        self.m = m

    def tensor(self, pe):
        c, m = self.c, self.m
        wa = c.s("gla_wa").rearrange("p (k e) -> p k e", k=KC)
        for k in range(KC):
            mm = pe.matmul(c.ps[0:16, 0, 0:T2], wa[:, k, :], c.H[:, k, 0:T2], start=(k == 0), stop=(k == KC - 1))
        mm.then_inc(self.tensor_done, self.pe.mark("lr"))
        pe.wait_ge(self.scalar_done, self.act.at("lr"))
        for h in range(4):
            mm = pe.matmul(c.ps[:, 1 + h, 0:T2], c.s("gla_w2", 16)[:, h * P:(h + 1) * P], m["lr"][0:16, :],
                           start=True, stop=True)
            mm.then_inc(self.tensor_done, self.pe.mark("z", h))

    def scalar(self, act):
        c, m = self.c, self.m
        act.wait_ge(self.tensor_done, self.pe.at("lr"))
        act.activation(m["lr"][0:16, :], c.ps[0:16, 0, 0:T2], ACT.Copy).then_inc(self.scalar_done, self.act.mark("lr"))
        for h in range(4):
            act.wait_ge(self.tensor_done, self.pe.at("z", h))
            act.activation(m["b"][:, h, :], c.ps[:, 1 + h, 0:T2], ACT.Identity,
                                      bias=c.s("gla_ba")[:, h:h + 1]).then_inc(self.scalar_done, self.act.mark("z", h))
        act.wait_ge(self.vector_done, self.dve.at("abs"))
        act.activation(m["e"], m["e"], ACT.Exp, scale=-1.0).then_inc(self.scalar_done, self.act.mark("e"))
        act.wait_ge(self.scalar_done, self.act.at("e"))
        act.activation(m["e"], m["e"], ACT.Ln, bias=1.0).then_inc(self.scalar_done, self.act.mark("ln"))

    def vector(self, dve):
        c, m = self.c, self.m
        dve.wait_ge(self.scalar_done, self.act.at("z", 3))
        dve.scalar_tensor_tensor(m["e"], m["b"], -1.0, m["b"], ALU.mult, ALU.max).then_inc(self.vector_done, self.dve.mark("abs"))
        dve.memset(m["one"], 1.0).then_inc(self.vector_done, self.dve.mark("one"))
        dve.wait_ge(self.scalar_done, self.act.at("ln"))
        dve.scalar_tensor_tensor(m["g"], m["b"], 0.0, m["e"], ALU.min, ALU.subtract).then_inc(self.vector_done, self.dve.mark("g"))
        dve.wait_ge(self.vector_done, self.dve.at("g"))
        for h in range(4):
            for t0, tn in TILES2:
                dve.tensor_tensor_scan(m["b"][:, h, t0:t0 + tn], m["one"][:, 0:tn], m["g"][:, h, t0:t0 + tn],
                                       0.0, ALU.mult, ALU.add)


class GlaScores(Stage):

    def __init__(self, core, m):
        super().__init__(core)
        self.m = m

    def view(self, x, l):
        if l <= 3:
            return x.rearrange("p h t -> p (h t)").rearrange("p (n w) -> p n w", w=2 << l)
        return x[:, :, META:].rearrange("p h (n w) -> p h n w", w=2 << l)

    def units(self, l):
        for h in range(4):
            for t, (t0, tn) in enumerate(TILES2):
                if tn > (1 << max(l, 0)):
                    yield h, t, t0, tn

    def out(self, l, h, t, tn):
        if t == 0:
            return self.c.ps[0:tn, 6 + l % 2, h * META:h * META + tn]
        return self.c.ps[0:tn, 3 * (l % 2) + t - 1, h * P:h * P + tn]

    def tensor(self, pe):
        c, m = self.c, self.m
        for l in range(-1, LEVELS):
            if l >= 0:
                pe.wait_ge(self.vector_done, self.dve.at("scaled", l))
            if l >= 1:
                pe.wait_ge(self.vector_done, self.dve.at("kept", l - 2))
            q, k = (m["Q"], m["K"]) if l < 0 else (m["q"][l % 2], m["k"][l % 2])
            for h, t, t0, tn in self.units(l):
                mm = pe.matmul(self.out(l, h, t, tn), k[:, h, t0:t0 + tn], q[:, h, t0:t0 + tn], start=True, stop=True)
            mm.then_inc(self.tensor_done, self.pe.mark("pairs", l))

    def scalar(self, act):
        c, m = self.c, self.m
        for l in range(LEVELS):
            d = self.view(m["e"], l)
            act.wait_ge(self.vector_done, self.dve.at("diff", l))
            act.activation(m["e"], m["e"], ACT.Exp, scale=-1.0 / 16.0).then_inc(self.scalar_done, self.act.mark("decay", l))

    def vector(self, dve):
        c, m = self.c, self.m
        dve.memset(m["A"], 0.0)
        dve.memset(m["e"], 0.0).then_inc(self.vector_done, self.dve.mark("zero"))

        def keep(l):
            dve.wait_ge(self.tensor_done, self.pe.at("pairs", l))
            mask = c.s("ident") if l < 0 else c.s("levels").rearrange("p (l t) -> p l t", l=LEVELS)[:, l, :]
            mask = mask.bitcast(U32)
            for t in (1, 2):
                ins = dve.copy_predicated(m["A"][:, t - 1, :, :], mask.unsqueeze(1).to_broadcast([P, 4, P]),
                                          c.ps[:, 3 * (l % 2) + t - 1, :].rearrange("p (h t) -> p h t", h=4))
            if l <= 3:
                ins = dve.copy_predicated(m["A0"][0:META, :, :],
                                          mask[0:META, 0:META].unsqueeze(1).to_broadcast([META, 4, META]),
                                          c.ps[0:META, 6 + l % 2, 0:64].rearrange("p (h t) -> p h t", h=4))
            ins.then_inc(self.vector_done, self.dve.mark("kept", l))

        dve.memset(m["A0"], 0.0).then_inc(self.vector_done, self.dve.mark("zero0"))
        dve.wait_ge(self.vector_done, self.dve.at("zero0"))
        for l in range(LEVELS):
            half = 1 << l
            b, e = self.view(m["b"], l), self.view(m["e"], l)
            if l >= 1:
                dve.wait_ge(self.vector_done, self.dve.at("scaled", l - 1))
            if l <= 3:
                n = b.shape[1]
                ins = dve.tensor_tensor(e, b, b[:, :, half - 1:half].to_broadcast([P, n, 2 * half]), ALU.subtract)
            else:
                n = b.shape[2]
                for h in range(4):
                    ins = dve.tensor_tensor(e[:, h], b[:, h],
                                            b[:, h, :, half - 1:half].to_broadcast([P, n, 2 * half]), ALU.subtract)
            ins.then_inc(self.vector_done, self.dve.mark("raw", l))
            dve.wait_ge(self.vector_done, self.dve.at("raw", l))
            dve.scalar_tensor_tensor(m["e"], m["e"], -1.0, m["e"], ALU.mult, ALU.max).then_inc(self.vector_done, self.dve.mark("diff", l))
            keep(l - 1)
            dve.wait_ge(self.scalar_done, self.act.at("decay", l))
            dve.tensor_tensor(m["q"][l % 2], m["Q"], m["e"], ALU.mult)
            dve.tensor_tensor(m["k"][l % 2], m["K"], m["e"], ALU.mult).then_inc(self.vector_done, self.dve.mark("scaled", l))
            dve.wait_ge(self.vector_done, self.dve.at("kept", l - 1))
        keep(LEVELS - 1)


class GlaOutput(Stage):

    def __init__(self, core, m):
        super().__init__(core)
        self.m = m

    def vector(self, dve):
        c, m = self.c, self.m
        for t, (t0, tn) in enumerate(TILES2):
            b = m["b"][:, :, t0:t0 + tn]
            dve.tensor_tensor(m["e"][:, :, t0:t0 + tn], b[:, :, tn - 1:tn].to_broadcast([P, 4, tn]), b, ALU.subtract)
        dve.tensor_copy(m["last"], m["b"][:, :, T2 - 1]).then_inc(self.vector_done, self.dve.mark("rest"))
        for h in range(4):
            dve.wait_ge(self.scalar_done, self.act.at("inter", h))
            dve.tensor_tensor(m["q"][0][:, h, :], m["Q"][:, h, :], m["q"][1][:, h, :], ALU.mult)
            dve.tensor_tensor(m["k"][0][:, h, :], m["K"][:, h, :], m["e"][:, h, :], ALU.mult).then_inc(self.vector_done, self.dve.mark("scaled", h))
        for t in range(2):
            for h in range(4):
                dve.wait_ge(self.tensor_done, self.pe.at("kv", t, h))
                S = m["S"][:, h, :]
                if t == 0:
                    ins = dve.tensor_copy(S, c.ps[:, 4 + h % 2, 0:256])
                else:
                    dve.wait_ge(self.scalar_done, self.act.at("eb"))
                    dve.wait_ge(self.tensor_done, self.pe.at("o", t, 2 * h + 1))
                    ins = dve.scalar_tensor_tensor(S, S, m["ebl"][:, h:h + 1], c.ps[:, 4 + h % 2, 0:256],
                                                   ALU.mult, ALU.add)
                ins.then_inc(self.vector_done, self.dve.mark("state", t, h))

    def scalar(self, act):
        c, m = self.c, self.m
        act.activation(m["ebl"], m["b"][:, :, META + P - 1], ACT.Exp, scale=1.0 / 16.0).then_inc(self.scalar_done, self.act.mark("eb"))
        act.wait_ge(self.vector_done, self.dve.at("rest"))
        for h in range(4):
            act.activation(m["q"][1][:, h, :], m["b"][:, h, :], ACT.Exp, scale=1.0 / 16.0)
            act.activation(m["e"][:, h, :], m["e"][:, h, :], ACT.Exp, scale=1.0 / 16.0).then_inc(self.scalar_done, self.act.mark("inter", h))
        for t, (t0, tn) in enumerate(TILES2):
            if t < 2:
                for h in range(4):
                    act.wait_ge(self.tensor_done, self.pe.at("turned", t, h))
                    act.activation(m["kT"][0:tn, h, :], c.ps[0:tn, 2 + h % 2, 0:P], ACT.Copy).then_inc(self.scalar_done, self.act.mark("turned", t, h))
            for u in range(8):
                act.wait_ge(self.tensor_done, self.pe.at("o", t, u))
                act.activation(m["OT"][:, u, t0:t0 + tn], c.ps[:, u % 2, 0:tn], ACT.Copy).then_inc(self.scalar_done, self.act.mark("o", t, u))

    def tensor(self, pe):
        c, m = self.c, self.m
        for t, (t0, tn) in enumerate(TILES2):
            if t < 2:
                for h in range(4):
                    if t == 0:
                        pe.wait_ge(self.vector_done, self.dve.at("scaled", h))
                    if 4 * t + h >= 2:
                        pt, ph = divmod(4 * t + h - 2, 4)
                        pe.wait_ge(self.scalar_done, self.act.at("turned", pt, ph))
                    tr = pe.transpose(c.ps[0:tn, 2 + h % 2, 0:P], m["k"][0][:, h, t0:t0 + tn], c.s("ident"))
                    tr.then_inc(self.tensor_done, self.pe.mark("turned", t, h))
            for u in range(8):
                h, half = divmod(u, 2)
                if 8 * t + u >= 2:
                    pt, pu = divmod(8 * t + u - 2, 8)
                    pe.wait_ge(self.scalar_done, self.act.at("o", pt, pu))
                A = m["A0"][0:tn, h, :] if t == 0 else m["A"][0:tn, t - 1, h, :]
                cols = slice(h * 256 + half * P, h * 256 + half * P + P)
                if t > 0:
                    pe.wait_ge(self.vector_done, self.dve.at("state", t - 1, h))
                mm = pe.matmul(c.ps[:, u % 2, 0:tn], m["V"][0:tn, t, cols], A, start=True, stop=(t == 0))
                if t > 0:
                    mm = pe.matmul(c.ps[:, u % 2, 0:tn], m["S"][:, h, half * P:(half + 1) * P],
                                   m["q"][0][:, h, t0:t0 + tn], start=False, stop=True)
                mm.then_inc(self.tensor_done, self.pe.mark("o", t, u))
            if t < 2:
                for h in range(4):
                    if 4 * t + h >= 2:
                        pt, ph = divmod(4 * t + h - 2, 4)
                        pe.wait_ge(self.vector_done, self.dve.at("state", pt, ph))
                    pe.wait_ge(self.scalar_done, self.act.at("turned", t, h))
                    mm = pe.matmul(c.ps[:, 4 + h % 2, 0:256], m["kT"][0:tn, h, :], m["V"][0:tn, t, h * 256:(h + 1) * 256],
                                   start=True, stop=True)
                    mm.then_inc(self.tensor_done, self.pe.mark("kv", t, h))


class Convolve(Stage):

    def __init__(self, core, pre, tmp):
        super().__init__(core)
        self.pre, self.tmp = pre, tmp

    def vector(self, dve):
        c = self.c
        w = c.s("gdn_conv").rearrange("p (j k) -> p j k", j=4)
        N = 24
        for i in range(0, N, 2):
            if i >= 4:
                dve.wait_ge(self.scalar_done, self.act.at(i - 3))
            for j in range(4):
                for u in (i, i + 1):
                    x, t = self.pre[:, u, j:j + T2], self.tmp[:, u % 4, :]
                    if j > 0:
                        dve.wait_ge(self.vector_done, self.dve.at("tap", u, j - 1))
                        ins = dve.scalar_tensor_tensor(t, x, w[:, j, u:u + 1], t, ALU.mult, ALU.add)
                    else:
                        ins = dve.tensor_scalar(t, x, w[:, j, u:u + 1], None, ALU.mult)
                    ins.then_inc(self.vector_done, self.dve.mark("tap", u, j))

    def scalar(self, act):
        c = self.c
        for i in range(24):
            act.wait_ge(self.vector_done, self.dve.at("tap", i, 3))
            act.activation(self.pre[:, i, 3:3 + T2], self.tmp[:, i % 4, :], ACT.Silu).then_inc(self.scalar_done, self.act.mark(i))


class GdnGates(Stage):

    def __init__(self, core, m):
        super().__init__(core)
        self.m = m

    def tensor(self, pe):
        c, m = self.c, self.m
        w = c.s("gdn_wab").rearrange("p (k e) -> p k e", k=KC)
        for t, (t0, tn) in enumerate(TILES2):
            for k in range(KC):
                mm = pe.matmul(c.ps[0:tn, 0, t * 16:(t + 1) * 16], c.H[:, k, t0:t0 + tn], w[:, k, :],
                               start=(k == 0), stop=(k == KC - 1))
            mm.then_inc(self.tensor_done, self.pe.mark("ab", t))
        pe.wait_ge(self.vector_done, self.dve.at("g", 2))
        for t, (t0, tn) in enumerate(TILES2):
            pe.matmul(c.ps[0:tn, 1, t * 8:(t + 1) * 8], c.s("upto")[0:tn, 0:tn], m["g"][0:tn, t, :],
                      start=True, stop=True)
            pe.matmul(c.ps[0:8, 2, t0:t0 + tn], m["g"][0:tn, t, :], c.s("upto")[0:tn, 0:tn], start=True, stop=True)
            mm = pe.matmul(c.ps[0:8, 3, t0:t0 + tn], m["beta"][0:tn, t, :], c.s("ident")[0:tn, 0:tn],
                           start=True, stop=True)
        mm.then_inc(self.tensor_done, self.pe.mark("b"))
        pe.wait_ge(self.scalar_done, self.act.at("rows"))
        for h in range(8):
            if h >= 2:
                pe.wait_ge(self.scalar_done, self.act.at("eb", h - 2))
                pe.wait_ge(self.vector_done, self.dve.at("kb", h - 2))
            row = c.s("ident", 8)[:, h:h + 1].to_broadcast([8, P])
            pe.matmul(c.ps[:, 4 + h % 2, 0:T2], row, m["bT"][0:8, :], start=True, stop=True)
            pe.matmul(c.ps[:, 6 + h % 2, 0:T2], row, m["betaT"][0:8, :], start=True, stop=True).then_inc(self.tensor_done, self.pe.mark("bc", h))

    def vector(self, dve):
        c, m = self.c, self.m
        dve.wait_ge(self.scalar_done, self.act.at("alog"))
        for t, (t0, tn) in enumerate(TILES2):
            a, w = m["a"][0:tn, t, :], m["w"][0:tn, t, :]
            dve.wait_ge(self.tensor_done, self.pe.at("ab", 2))
            dve.tensor_tensor(a, c.ps[0:tn, 0, t * 16:t * 16 + 8], c.s("gdn_dt", tn), ALU.add).then_inc(self.vector_done, self.dve.mark("a", t))
            dve.wait_ge(self.vector_done, self.dve.at("a", t))
            dve.scalar_tensor_tensor(w, a, -1.0, a, ALU.mult, ALU.max).then_inc(self.vector_done, self.dve.mark("abs", t))
            dve.wait_ge(self.scalar_done, self.act.at("ln", t))
            dve.scalar_tensor_tensor(a, a, 0.0, w, ALU.max, ALU.add).then_inc(self.vector_done, self.dve.mark("sp", t))
            dve.wait_ge(self.vector_done, self.dve.at("sp", t))
            dve.scalar_tensor_tensor(m["g"][0:tn, t, :], a, -1.0, m["alog"][0:tn, :], ALU.mult, ALU.mult).then_inc(self.vector_done, self.dve.mark("g", t))
        for h in range(8):
            dve.wait_ge(self.tensor_done, self.pe.at("bc", h))
            dve.wait_ge(self.scalar_done, self.act.at("eb", h))
            dve.tensor_tensor(m["KB"][:, h, :], m["K"][:, h, 3:3 + T2], c.ps[:, 6 + h % 2, 0:T2], ALU.mult).then_inc(self.vector_done, self.dve.mark("kb", h))
            dve.tensor_tensor(m["QE"][:, h, :], m["Q"][:, h, 3:3 + T2], m["EB"][:, h, :], ALU.mult)
            dve.wait_ge(self.vector_done, self.dve.at("kb", h))
            dve.tensor_tensor(m["KBE"][:, h, :], m["KB"][:, h, :], m["EB"][:, h, :], ALU.mult)

    def scalar(self, act):
        c, m = self.c, self.m
        for t, (t0, tn) in enumerate(TILES2):
            act.wait_ge(self.tensor_done, self.pe.at("ab", 2))
            ins = act.activation(m["beta"][0:tn, t, :], c.ps[0:tn, 0, t * 16 + 8:t * 16 + 16], ACT.Sigmoid)
        act.activation(m["alog"], c.s("gdn_alog"), ACT.Exp).then_inc(self.scalar_done, self.act.mark("alog"))
        for t, (t0, tn) in enumerate(TILES2):
            w = m["w"][0:tn, t, :]
            act.wait_ge(self.vector_done, self.dve.at("abs", t))
            act.activation(w, w, ACT.Exp, scale=-1.0).then_inc(self.scalar_done, self.act.mark("e", t))
            act.wait_ge(self.scalar_done, self.act.at("e", t))
            act.activation(w, w, ACT.Ln, bias=1.0).then_inc(self.scalar_done, self.act.mark("ln", t))
        act.wait_ge(self.tensor_done, self.pe.at("b"))
        for t, (t0, tn) in enumerate(TILES2):
            act.activation(m["b"][0:tn, t, :], c.ps[0:tn, 1, t * 8:(t + 1) * 8], ACT.Copy)
        act.activation(m["bT"][0:8, :], c.ps[0:8, 2, 0:T2], ACT.Copy)
        act.activation(m["betaT"][0:8, :], c.ps[0:8, 3, 0:T2], ACT.Copy).then_inc(self.scalar_done, self.act.mark("rows"))
        for h in range(8):
            act.wait_ge(self.tensor_done, self.pe.at("bc", h))
            act.activation(m["BB"][:, h, :], c.ps[:, 4 + h % 2, 0:T2], ACT.Copy)
            act.activation(m["EB"][:, h, :], c.ps[:, 4 + h % 2, 0:T2], ACT.Exp).then_inc(self.scalar_done, self.act.mark("eb", h))


class GdnChunk(Stage):

    def __init__(self, core, m, t):
        super().__init__(core)
        self.m, self.t = m, t
        self.t0, self.tn = TILES2[t]
        self.levels = (self.tn - 1).bit_length()

    def psv(self, bank, n=None):
        return self.c.ps[0:self.tn, bank:bank + 2, :].rearrange("p a (h t) -> p (a h) t", h=4)[:, :, 0:n or self.tn]

    def head(self, bank, h, n=None):
        return self.c.ps[0:self.tn, bank + h // 4, (h % 4) * P:(h % 4) * P + (n or self.tn)]

    def tensor(self, pe):
        c, m, t0, n = self.c, self.m, self.t0, self.tn
        T, T3 = slice(t0, t0 + n), slice(3 + t0, 3 + t0 + n)
        for h in range(8):
            pe.matmul(self.head(0, h), m["K"][:, h, T3], m["KB"][:, h, T], start=True, stop=True)
            mm = pe.matmul(self.head(2, h), m["K"][:, h, T3], m["Q"][:, h, T3], start=True, stop=True)
        mm.then_inc(self.tensor_done, self.pe.mark("kk"))
        for h in range(8):
            pe.transpose(self.head(4, h, P), m["K"][:, h, T3], c.s("ident"))
            mm = pe.transpose(self.head(6, h, P), m["V"][:, h, T3], c.s("ident"))
        mm.then_inc(self.tensor_done, self.pe.mark("turned"))
        for l in range(self.levels):
            pe.wait_ge(self.vector_done, self.dve.at("part", l))
            if l == 0:
                pe.wait_ge(self.scalar_done, self.act.at("vb"))
            else:
                pe.wait_ge(self.vector_done, self.dve.at("X", l - 1))
            for h in range(8):
                mm = pe.matmul(self.head(0, h), m["BT"][0:n, l % 2, h, 0:n], m["Xm"][0:n, h, 0:n], start=True, stop=True)
            mm.then_inc(self.tensor_done, self.pe.mark("BX", l))
            pe.wait_ge(self.scalar_done, self.act.at("BX", l))
            for h in range(8):
                pe.matmul(self.head(2, h), m["XT"][0:n, h, 0:n], m["U"][0:n, h, 0:n], start=True, stop=True)
                mm = pe.matmul(self.head(4, h), m["U"][0:n, h, 0:n], m["XT"][0:n, h, 0:n], start=True, stop=True)
            mm.then_inc(self.tensor_done, self.pe.mark("XBX", l))
        pe.wait_ge(self.vector_done, self.dve.at("X", self.levels - 1))
        for h in range(8):
            mm = pe.matmul(self.head(0, h, P), m["KBE"][:, h, T], m["S"][:, h, :], start=True, stop=True)
        mm.then_inc(self.tensor_done, self.pe.mark("kS"))
        pe.wait_ge(self.vector_done, self.dve.at("r"))
        for h in range(8):
            mm = pe.matmul(self.head(2, h, P), m["XT"][0:n, h, 0:n], m["U"][0:n, h, :], start=True, stop=True)
        mm.then_inc(self.tensor_done, self.pe.mark("vnew"))
        pe.wait_ge(self.scalar_done, self.act.at("vnew"))
        for h in range(8):
            o = c.ps[:, 4 + h // 4, (h % 4) * P:(h % 4) * P + n]
            pe.matmul(o, m["VN"][0:n, h, :], m["AT"][0:n, h, 0:n], start=True, stop=False)
            mm = pe.matmul(o, m["S"][:, h, :], m["QE"][:, h, T], start=False, stop=True)
        mm.then_inc(self.tensor_done, self.pe.mark("o"))
        for h in range(8):
            mm = pe.matmul(c.ps[:, 6 + h // 4, (h % 4) * P:(h % 4 + 1) * P], m["KD"][0:n, h, :], m["VN"][0:n, h, :],
                           start=True, stop=True)
        mm.then_inc(self.tensor_done, self.pe.mark("kv"))

    def vector(self, dve):
        c, m, t0, n = self.c, self.m, self.t0, self.tn
        T = slice(t0, t0 + n)
        if self.t == 0:
            dve.memset(m["S"], 0.0)
        dve.tensor_tensor(m["bl"][0:n, :], m["BB"][0:n, :, t0 + n - 1], m["b"][0:n, self.t, :], ALU.subtract).then_inc(self.vector_done, self.dve.mark("bl"))
        for h in range(8):
            dve.tensor_scalar(m["U"][0:n, h, 0:n], m["BB"][0:n, h, T], m["b"][0:n, self.t, h:h + 1], 0.0,
                                         ALU.subtract, ALU.min).then_inc(self.vector_done, self.dve.mark("diff", h))
        ident = c.s("ident")[0:n, 0:n].unsqueeze(1).to_broadcast([n, 8, n])
        dve.tensor_copy(m["Xm"][0:n, :, 0:n], ident)
        dve.tensor_copy(m["XT"][0:n, :, 0:n], ident)
        dve.wait_ge(self.scalar_done, self.act.at("decay"))
        dve.wait_ge(self.tensor_done, self.pe.at("kk"))
        LT, AT, U = m["LT"][0:n, :, 0:n], m["AT"][0:n, :, 0:n], m["U"][0:n, :, 0:n]
        dve.tensor_tensor(LT, self.psv(0), U, ALU.mult).then_inc(self.vector_done, self.dve.mark("LT"))
        dve.tensor_tensor(AT, self.psv(2), U, ALU.mult).then_inc(self.vector_done, self.dve.mark("AT0"))
        dve.wait_ge(self.vector_done, self.dve.at("AT0"))
        dve.tensor_tensor(AT, AT, c.s("upto")[0:n, 0:n].unsqueeze(1).to_broadcast([n, 8, n]), ALU.mult).then_inc(self.vector_done, self.dve.mark("AT"))
        levels = c.s("levels").rearrange("p (l t) -> p l t", l=LEVELS)

        def part(l):
            mask = levels[0:n, l, 0:n].unsqueeze(1).to_broadcast([n, 8, n])
            dve.tensor_tensor(m["BT"][0:n, l % 2, :, 0:n], LT, mask, ALU.mult).then_inc(self.vector_done, self.dve.mark("part", l))

        part(0)
        for l in range(self.levels):
            if l + 1 < self.levels:
                part(l + 1)
            dve.wait_ge(self.tensor_done, self.pe.at("XBX", l))
            X, XT = m["Xm"][0:n, :, 0:n], m["XT"][0:n, :, 0:n]
            if l > 0:
                dve.wait_ge(self.vector_done, self.dve.at("X", l - 1))
            dve.tensor_tensor(X, X, self.psv(2), ALU.subtract)
            dve.tensor_tensor(XT, XT, self.psv(4), ALU.subtract).then_inc(self.vector_done, self.dve.mark("X", l))
        dve.wait_ge(self.tensor_done, self.pe.at("kS"))
        dve.wait_ge(self.scalar_done, self.act.at("vb"))
        dve.tensor_tensor(m["U"][0:n, :, :], m["VB"][0:n, :, :], self.psv(0, P), ALU.subtract).then_inc(self.vector_done, self.dve.mark("r"))
        if self.t < 2:
            dve.wait_ge(self.tensor_done, self.pe.at("kv"))
            kv = c.ps[:, 6:8, :].rearrange("p a (h t) -> p (a h) t", h=4)
            for h in range(8):
                dve.scalar_tensor_tensor(m["S"][:, h, :], m["S"][:, h, :], m["EB"][:, h, t0 + n - 1:t0 + n],
                                         kv[:, h, :], ALU.mult, ALU.add)

    def scalar(self, act):
        c, m, t0, n = self.c, self.m, self.t0, self.tn
        U = m["U"][0:n, :, 0:n]
        act.wait_ge(self.vector_done, self.dve.at("bl"))
        act.activation(m["bl"][0:n, :], m["bl"][0:n, :], ACT.Exp).then_inc(self.scalar_done, self.act.mark("bl"))
        act.wait_ge(self.vector_done, self.dve.at("diff", 7))
        act.activation(U, U, ACT.Exp).then_inc(self.scalar_done, self.act.mark("decay"))
        act.wait_ge(self.tensor_done, self.pe.at("turned"))
        act.wait_ge(self.scalar_done, self.act.at("bl"))
        for h in range(8):
            act.activation(m["KD"][0:n, h, :], self.head(4, h, P), ACT.Copy, scale=m["bl"][0:n, h:h + 1])
            ins = act.activation(m["VB"][0:n, h, :], self.head(6, h, P), ACT.Copy, scale=m["beta"][0:n, self.t, h:h + 1])
        ins.then_inc(self.scalar_done, self.act.mark("vb"))
        for l in range(self.levels):
            act.wait_ge(self.tensor_done, self.pe.at("BX", l))
            if l == 0:
                act.wait_ge(self.vector_done, self.dve.at("AT0"))
            else:
                act.wait_ge(self.tensor_done, self.pe.at("XBX", l - 1))
            act.activation(U, self.psv(0), ACT.Copy).then_inc(self.scalar_done, self.act.mark("BX", l))
        act.wait_ge(self.tensor_done, self.pe.at("vnew"))
        act.activation(m["VN"][0:n, :, :], self.psv(2, P), ACT.Copy).then_inc(self.scalar_done, self.act.mark("vnew"))
        act.wait_ge(self.tensor_done, self.pe.at("o"))
        o = c.ps[:, 4:6, :].rearrange("p a (h t) -> p (a h) t", h=4)[:, :, 0:n]
        act.activation(m["OT"][:, :, t0:t0 + n], o, ACT.Copy)


class Zero(Stage):

    def __init__(self, core, dst):
        super().__init__(core)
        self.dst = dst

    def vector(self, dve):
        dve.memset(self.dst, 0.0)


def first_stack(c):
    d = c.dram
    yield Modulation(c, c.carve({"rows": (2 * 6 * D,)})["rows"])

    m = c.carve({"QK": (13, 512), "KD": (2, 512), "V": (4, 640), "OT": (8, 512), "p": (4, 512), "s": (4, 512),
                 "pT": (2, 512), "col": (4, 8), "lam": (4,)})
    QK, KD, V, OT = m["QK"], m["KD"], m["V"], m["OT"]
    w = d["w_in_even"]
    items = feature_items(QK, [0, 1], 0, T1)
    items.append((2, "feature", 0, P, 0, T1, move_to(QK[:, 4, :])))
    items += token_items(V, [2], TILES1, lo=P, n=P, at=0)
    items += feature_items(QK, [3, 4, 5, 6], 0, T1, first=5)
    items += token_items(V, [7, 8], TILES1, at=P)
    yield Project(c, c.H, [columns(w, s * WIDE) for s in range(9)], items)
    yield Lambda(c, m["lam"])
    yield Rope(c, [QK[:, j, CTX:T1] for j in range(13)], 64, m["s"],
               copies=[(KD[o * 64:(o + 1) * 64, g, :], QK[g * 64:(g + 1) * 64, 4, :]) for g in range(2) for o in range(2)])
    window = c.s("window").rearrange("p (q k) -> p q k", q=2)
    items = []
    for h in range(8):
        r, g = 64 * (h % 2), h // 4
        R = slice(r, r + 64)
        for t, (t0, tn) in enumerate(TILES1):
            keys = CTX if t < 2 else T1
            items.append(dict(
                rows=tn, keys=keys, maps=[[(QK[R, h // 2, t0:t0 + tn], KD[R, g, 0:keys])]], scale=64 ** -0.5,
                masks=[[], [], [(window[:, 0, :], 384, 512)], [(window[:, 1, :], 256, 384)]][t], sink=c.s("sink")[:, h:h + 1],
                values=[(b * P, P, V[:, b, g * 64:(g + 1) * 64]) for b in range(keys // P)],
                out_rows=(r, 64), out=OT[R, h // 2, t0:t0 + tn]))
    for h in range(4):
        for t, (t0, tn) in enumerate(TILES1):
            keys = CTX if t < 2 else T1
            items.append(dict(
                rows=tn, keys=keys, scale=64 ** -0.5, lam=m["lam"][:, 3:4],
                maps=[[(QK[64 * j:64 * j + 64, 5 + h, t0:t0 + tn], QK[64 * j:64 * j + 64, 9 + h, 0:keys])] for j in range(2)],
                values=[(b * P, P, V[:, b, P + h * P:P + (h + 1) * P]) for b in range(keys // P)],
                out_rows=(0, P), out=OT[:, 4 + h, t0:t0 + tn]))
    yield Attention(c, items, m["p"], m["s"], m["pT"], m["col"])
    yield HeadNorm(c, [([OT[:, 4 + h, :]], T1, c.s("ones"), P, [c.s("subln_g")], None) for h in range(4)],
                   SUBLN_EPS, m["s"], m["p"], after=1.0 - LAM_INIT)
    yield Project(c, OT, [columns(d["w_out_even"], s * WIDE) for s in range(4)], feature_items(c.ACC, range(4), 0, T1))
    yield LayerNorm(c, 0, 0, [(0, 0), (1, CTX)], (0, 3))
    yield from experts(c, 0, 0, T1)
    yield LayerNorm(c, 0, 1, [(0, 0), (1, CTX)], (1, 0))

    m = c.carve({"Q": (8, 512), "K": (2, 512), "V": (4, 256), "OT": (8, 512), "p": (4, 512), "s": (4, 512),
                 "pT": (2, 512), "col": (4, 8)})
    Q, K, V, OT = m["Q"], m["K"], m["V"], m["OT"]
    w = d["w_in_odd"]
    yield Project(c, c.H, [columns(w, s * WIDE) for s in range(6)],
                  feature_items(Q, range(4), CTX, SEQ) + feature_items(K, [4], 0, T1) + token_items(V, [5], TILES1))
    yield HeadNorm(c, [([Q[:, h, CTX:T1]], SEQ, c.s("ones"), P, [c.s("qn_g")], None) for h in range(8)]
                   + [([K[:, h, :]], T1, c.s("ones"), P, [c.s("kn_g")], None) for h in range(2)],
                   QK_EPS, m["s"], m["p"])
    yield Rope(c, [Q[:, h, CTX:T1] for h in range(8)] + [K[:, h, CTX:T1] for h in range(2)], 128, m["s"])
    items = [dict(rows=P, keys=T1, scale=P ** -0.5, maps=[[(Q[:, h, t0:t0 + P], K[:, h // 4, :])]],
                  values=[(b * P, P, V[:, b, (h // 4) * P:(h // 4 + 1) * P]) for b in range(4)],
                  out_rows=(0, P), out=OT[:, h, t0:t0 + P])
             for h in range(8) for t0 in (256, 384)]
    yield Attention(c, items, m["p"], m["s"], m["pT"], m["col"])
    yield Project(c, OT, [columns(d["w_out_odd"], s * WIDE) for s in range(4)], feature_items(c.ACC, range(4), CTX, SEQ))
    yield LayerNorm(c, 1, 0, [(1, CTX)], (1, 3))
    yield from experts(c, 1, CTX, SEQ)
    yield LayerNorm(c, 1, 1, [(1, CTX)], None, shift_to=META)


def experts(c, layer, t0, tn):
    d = c.dram
    m = c.carve({"sc": (4, 16), "sel": (4, 16), "ta": (4, 16),
                 "tb": (4, 16), "g": (4, 16), "hi": (16, 2), "lo": (16, 2), "gs": (3, 16), "mx": (4,), "gT": (512,)})
    yield Router(c, t0, tn, m)

    def rows(name):
        w = d[name][layer].rearrange("e k m -> (e k) m")

        def src(offset, half):
            return w[bass.ds(offset(D), D), half * WIDE:(half + 1) * WIDE].rearrange("(k p) m -> p k m", p=P)
        return src

    def down(offset, half):
        w = d["w_down"][layer].rearrange("e k m -> (e k) m")
        return w[bass.ds(offset(D_EXPERT) + half * WIDE, WIDE), :].rearrange("(k p) m -> p k m", p=P)

    yield FeedForward(c, t0, tn, 2 * EXPERTS, rows("w_gate"), rows("w_up"), down, gates=layer + 1)


def swiglu(c, layer):
    d = c.dram
    w, wd = d["w_gate_up_2"][layer], d["w_down_2"][layer]

    def cols(base):
        def src(offset, half):
            return w[:, bass.ds(offset(2 * WIDE) + (base + half * WIDE), WIDE)].rearrange("(k p) m -> p k m", p=P)
        return src

    def down(offset, half):
        return wd[bass.ds(offset(2 * WIDE) + half * WIDE, WIDE), :].rearrange("(k p) m -> p k m", p=P)

    yield FeedForward(c, 0, T2, D_FF // WIDE, cols(0), cols(D_FF), down)


def fox(c, j):
    d = c.dram
    m = c.carve({"Q": (8, T2), "K": (8, T2), "V": (3, 1024), "G": (8, T2), "OT": (8, T2), "z": (3, 16), "w": (3, 16),
                 "lf": (3, 16), "C": (3, 16), "CT": (T2,), "p": (4, 512), "s": (4, 512), "pT": (2, 512), "col": (4, 8)})
    Q, K, V, OT = m["Q"], m["K"], m["V"], m["OT"]
    w = d["fox_w_in"][j]
    gate = [(12 + n // 2, "feature", (n % 2) * P, P, 0, T2,
             (lambda dst: lambda act, ps: act.activation(dst, ps, ACT.Sigmoid))(m["G"][:, n, :])) for n in range(8)]
    yield Project(c, c.H, [columns(w, s * WIDE) for s in range(16)],
                  feature_items(Q, range(4), 0, T2) + feature_items(K, range(4, 8), 0, T2)
                  + token_items(V, range(8, 12), TILES2) + gate)
    yield LogForget(c, c.s("fox_wf").rearrange("p (j k e) -> p j k e", j=2, k=KC)[:, j], c.s("fox_bf")[:, j * 16:(j + 1) * 16], m)
    yield HeadNorm(c, [([Q[:, n, :]], T2, c.s("ones64"), 64, [c.s("fox_qg")[:, j:j + 1]], None) for n in range(8)],
                   NORM_EPS, m["s"], m["p"], after=64 ** -0.5)
    yield HeadNorm(c, [([K[:, n, :]], T2, c.s("ones64"), 64, [c.s("fox_kg")[:, j:j + 1]], None) for n in range(8)],
                   NORM_EPS, m["s"], m["p"])
    items = []
    for h in range(16):
        r = 64 * (h % 2)
        R = slice(r, r + 64)
        for t, (t0, tn) in enumerate(TILES2):
            keys = t0 + tn
            minus_c = (c.s("ident", 16)[:, h:h + 1].to_broadcast([16, tn]), m["CT"][0:16, 0:keys])
            items.append(dict(
                rows=tn, keys=keys, scale=1.0, maps=[[(Q[R, h // 2, t0:t0 + tn], K[R, h // 2, 0:keys]), minus_c]],
                qbias=m["C"][0:tn, t, h:h + 1], masks=[(c.s("causal")[0:tn, 0:tn], t0, keys)],
                values=[(TILES2[b][0], TILES2[b][1], V[0:TILES2[b][1], b, h * 64:(h + 1) * 64]) for b in range(t + 1)],
                out_rows=(r, 64), out=OT[R, h // 2, t0:t0 + tn]))
    yield Attention(c, items, m["p"], m["s"], m["pT"], m["col"])
    yield Multiply(c, OT, m["G"])
    yield Project(c, OT, [columns(d["fox_w_out"][j], s * WIDE) for s in range(4)], feature_items(c.ACC, range(4), 0, T2))


def silu_items(dst, slots):
    return [(s, "feature", m * P, P, 0, T2, (lambda x: lambda act, ps: act.activation(x, ps, ACT.Silu))(dst[:, 2 * n + m, :]))
            for n, s in enumerate(slots) for m in range(2)]


def gla(c):
    d = c.dram
    m = c.carve({"Q": (4, T2), "K": (4, T2), "V": (3, 1024), "R": (8, T2), "OT": (8, T2), "b": (4, T2), "e": (4, T2),
                 "g": (4, T2), "q0": (4, T2), "k0": (4, T2), "q1": (4, T2), "k1": (4, T2), "one": (P,), "lr": (T2,),
                 "A0": (4, META), "S": (4, 256), "kT": (4, P), "ebl": (4,), "last": (4,), "A": (8, P),
                 })
    m["q"], m["k"] = [m["q0"], m["q1"]], [m["k0"], m["k1"]]
    m["A"] = m["A"].rearrange("p (a h) t -> p a h t", a=2)
    w = d["gla_w_in"]
    yield Project(c, c.H, [columns(w, s * WIDE) for s in range(12)],
                  feature_items(m["Q"], [0, 1], 0, T2, scale=P ** -0.5) + feature_items(m["K"], [2, 3], 0, T2)
                  + token_items(m["V"], range(4, 8), TILES2) + silu_items(m["R"], range(8, 12)))
    yield GlaGates(c, m)
    yield GlaScores(c, m)
    yield GlaOutput(c, m)
    OT = m["OT"]
    og = c.s("gla_og")
    sq = m["V"].rearrange("p t n -> p (t n)")
    yield HeadNorm(c, [([OT[:, 2 * h, :], OT[:, 2 * h + 1, :]], T2, c.s("ones"), 256, [og[:, 0:1], og[:, 1:2]], None)
                       for h in range(4)], NORM_EPS, m["e"], m["g"])
    yield Multiply(c, OT, m["R"])
    yield Project(c, OT, [columns(d["gla_w_out"], s * WIDE) for s in range(4)], feature_items(c.ACC, range(4), 0, T2))


def gdn(c):
    d = c.dram
    m = c.carve({"pre": (24, 3 + T2), "G": (8, T2), "OT": (8, T2), "BB": (8, T2), "KB": (8, T2),
                 "a": (3, 8), "w": (3, 8), "g": (3, 8), "b": (3, 8), "beta": (3, 8), "bT": (T2,), "betaT": (T2,),
                 "alog": (8,), "bl": (8,)}, reserve=6 * 1024)
    m["Q"], m["K"], m["V"] = (m["pre"][:, 8 * j:8 * j + 8, :] for j in range(3))
    m["QE"], m["EB"], m["KBE"] = m["OT"], c.ACC[:, :, 0:T2], c.H[:, :, 0:T2]
    m["Xm"], m["LT"], m["XT"] = (x[:, :, T2:T2 + P] for x in (c.X, c.H, c.ACC))
    m["VB"], m["KD"], m["U"], m["AT"] = (c.ext[:, j] for j in range(4))
    m["VN"], m["BT"] = m["VB"], c.ext[:, 4:6]
    m["S"] = c.stat[:].rearrange("p a (h t) -> p (a h) t", h=4)
    w = d["gdn_w_in"]
    items = [(n // 2, "feature", (n % 2) * P, P, 0, T2, move_to(m["pre"][:, n, 3:3 + T2])) for n in range(24)]
    yield Zero(c, m["pre"][:, :, 0:3])
    yield Project(c, c.H, [columns(w, s * WIDE) for s in range(16)], items + silu_items(m["G"], range(12, 16)))
    tmp = c.ext[:, 0:2].rearrange("p a h t -> p (a h t)")[:, 0:4 * T2].rearrange("p (i t) -> p i t", i=4)
    yield Convolve(c, m["pre"], tmp)
    tmp2 = c.ext[:, 2:4].rearrange("p a h t -> p (a h t)")[:, 0:4 * T2].rearrange("p (i t) -> p i t", i=4)
    for j, after in ((0, P ** -0.5), (1, 1.0)):
        yield HeadNorm(c, [([m["pre"][:, 8 * j + h, 3:3 + T2]], T2, c.s("ones"), 1.0, None, after) for h in range(8)],
                       NORM_EPS, tmp, tmp2)
    yield GdnGates(c, m)
    for t in range(3):
        yield GdnChunk(c, m, t)
    OT = m["OT"]
    yield HeadNorm(c, [([OT[:, h, :]], T2, c.s("ones"), P, [c.s("gdn_og")], None) for h in range(8)],
                   NORM_EPS, tmp, tmp2)
    yield Multiply(c, OT, m["G"])
    yield Project(c, OT, [columns(d["gdn_w_out"], s * WIDE) for s in range(4)], feature_items(c.ACC, range(4), 0, T2))


def second_stack(c):
    for i, mixer in enumerate((lambda: fox(c, 0), lambda: gla(c), lambda: gdn(c), lambda: fox(c, 1))):
        yield RmsNorm(c, c.s("norm_mix")[:, i * 8:(i + 1) * 8], add=(i > 0))
        yield from mixer()
        yield RmsNorm(c, c.s("norm_ffn")[:, i * 8:(i + 1) * 8], add=True)
        yield from swiglu(c, i)
    yield Store(c)


def build(nc, dram, values, limit=None):
    with ExitStack() as ctx:
        core = Core(nc, ctx, dram, values)
        stages = list(first_stack(core)) + list(second_stack(core))
        if limit:
            stages = stages[:limit]
        block = ctx.enter_context(nc.Block())

        def run(eng, part):
            for n, stage in enumerate(stages):
                if n:
                    eng.wait_ge(core.stage_done, 3 * n)
                part(stage, eng)
                eng.drain().then_inc(core.stage_done, 1)

        @block.sync
        def _(sp):
            for stage in stages:
                stage.sync(sp)

        @block.tensor
        def _(pe):
            run(pe, lambda stage, eng: stage.tensor(eng))

        @block.scalar
        def _(act):
            run(act, lambda stage, eng: stage.scalar(eng))

        @block.vector
        def _(dve):
            run(dve, lambda stage, eng: stage.vector(eng))
        return stages


WEIGHTS = {"w_mod": "w_mod", "w_in_even": "w_in_even", "w_out_even": "w_out_even", "w_in_odd": "w_in_odd",
           "w_out_odd": "w_out_odd", "w_gate": "w_gate", "w_up": "w_up", "w_down": "w_down",
           "w_gate_up_2": "w_gate_up_2", "w_down_2": "w_down_2", "fox_w_in": "fox_w_in_2", "fox_w_out": "fox_w_out_2",
           "gla_w_in": "gla_w_in_2", "gla_w_out": "gla_w_out_2", "gdn_w_in": "gdn_w_in_2", "gdn_w_out": "gdn_w_out_2"}
ONE_LAYER = ("w_in_even", "w_out_even", "w_in_odd", "w_out_odd", "gla_w_in", "gla_w_out", "gdn_w_in", "gdn_w_out")


def lay_out(inputs):
    x = {k: np.asarray(v) for k, v in inputs.items()}
    arrays = {}
    for name, key in WEIGHTS.items():
        a = x[key]
        arrays[name] = np.ascontiguousarray(a[0] if name in ONE_LAYER else a)

    def chunked(a):
        a = a.reshape(a.shape[:-1] + (-1, P))
        return np.moveaxis(a, -1, 0).reshape(P, -1)

    def features(a):
        return a.reshape(-1, P, a.shape[-1]).transpose(1, 0, 2).reshape(P, -1)

    def rows(a):
        return np.broadcast_to(a.reshape(1, -1), (P, a.size))

    tokens = np.concatenate([x["ctx"][0], x["x"][0]], 0)
    arrays["xT"] = np.ascontiguousarray(tokens.T.reshape(KC, P, T1).transpose(1, 0, 2))
    w2 = np.zeros((P, 512), np.float32)
    w2[:16] = x["gla_w_alpha2_2"][0]
    small = {
        "cond": features(np.stack([x["c_ctx"], x["c"][0]], 1)), "b_mod": chunked(x["b_mod"]),
        "ln_g": chunked(x["ln_g"]), "ln_b": chunked(x["ln_b"]), "norm_mix": chunked(x["norm_mix_2"]),
        "norm_ffn": chunked(x["norm_ffn_2"]), "meta": features(x["meta_tokens_2"].T),
        "w_router": features(x["w_router"]), "b_router": rows(x["b_router"]), "sink": rows(x["sink_logits"]),
        "lam": rows(np.concatenate([x["lam_q1"], x["lam_k1"], x["lam_q2"], x["lam_k2"]])),
        "subln_g": x["subln_g"].T, "qn_g": x["q_norm_g"].T, "kn_g": x["k_norm_g"].T,
        "fox_wf": np.concatenate([features(x["fox_w_in_2"][j][:, 4 * D:]) for j in range(2)], 1),
        "fox_bf": rows(x["fox_b_f_2"]), "fox_qg": np.tile(x["fox_q_gain_2"].T, (2, 1)),
        "fox_kg": np.tile(x["fox_k_gain_2"].T, (2, 1)),
        "gla_wa": features(x["gla_w_in_2"][0][:, 3072:]), "gla_w2": w2, "gla_ba": chunked(x["gla_b_alpha_2"]),
        "gla_og": chunked(x["gla_o_gain_2"]),
        "gdn_wab": features(x["gdn_w_in_2"][0][:, 4096:]), "gdn_conv": chunked(x["gdn_conv_w_2"]),
        "gdn_alog": rows(x["gdn_a_log_2"]), "gdn_dt": rows(x["gdn_dt_bias_2"]), "gdn_og": x["gdn_o_gain_2"].T,
    }
    small.update(shape_constants())
    parts = []
    for name, cols in SMALL_COLS:
        assert small[name].shape == (P, cols), (name, small[name].shape)
        parts.append(small[name])
    arrays["small"] = np.concatenate(parts, 1)
    return arrays


def program(nc, arrays, numbers, limit=None):
    dram = {name: nc.dram_tensor(f"in_{name}", a.shape, F32, kind="ExternalInput").ap() for name, a in arrays.items()}
    dram["gates"] = nc.dram_tensor("gates", (EXPERTS, T1), F32, kind="Internal").ap()
    dram["outT"] = nc.dram_tensor("out_xT", (D, SEQ), F32, kind="ExternalOutput").ap()
    build(nc, dram, numbers, limit)


def kernel(**inputs):
    import concourse.bacc as bacc
    from concourse.bass_utils import run_bass_kernel_spmd as run

    arrays = lay_out(inputs)
    numbers = {}
    for _ in range(2):
        nc = bacc.Bacc("TRN2", target_bir_lowering=False, num_devices=1)
        program(nc, arrays, numbers)
    r = run(nc, [{f"in_{name}": a for name, a in arrays.items()}], core_ids=[0])
    return np.ascontiguousarray(r.results[0]["out_xT"].T)[None]
```

```python
from contextlib import ExitStack

import numpy as np
import concourse.bass as bass
from concourse import mybir

F32 = mybir.dt.float32
F32R = mybir.dt.float32r
U32 = mybir.dt.uint32
ACT = mybir.ActivationFunctionType
ALU = mybir.AluOpType
AX_X = mybir.AxisListType.X

P = 128
D = 1024
KC = D // P
SEQ = 256
CTX = 256
T1 = CTX + SEQ
GRID_W = 64
ROPE_THETA = 10000.0
WINDOW = 128
ALPHA = (2 * 2) ** 0.25
LN_EPS, QK_EPS, SUBLN_EPS, NORM_EPS = 1e-5, 1e-6, 1e-5, 1e-6
LAM_INIT = 0.8 - 0.6
EXPERTS, GROUPS, D_EXPERT = 16, 4, 512
CAPACITY = 128
META = 16
T2 = META + SEQ
D_FF = 2816
BIG = 1e30

TILES1 = [(0, 128), (128, 128), (256, 128), (384, 128)]
TILES2 = [(0, META), (META, 128), (META + 128, 128)]

SLOTS = 6
ROOM = 22144
SPLIT_SLOTS = 3
SLOT = 2048
WIDE = 256
LEVELS = 7

SMALL_COLS = [
    ("cond", KC * 2), ("b_mod", 96), ("ln_g", 32), ("ln_b", 32), ("norm_mix", 32), ("norm_ffn", 32),
    ("meta", KC * META), ("w_router", KC * EXPERTS), ("b_router", EXPERTS), ("sink", 8), ("lam", 256),
    ("subln_g", 1), ("qn_g", 1), ("kn_g", 1), ("fox_wf", 2 * KC * 16), ("fox_bf", 32), ("fox_qg", 2), ("fox_kg", 2),
    ("gla_wa", KC * 16), ("gla_w2", 512), ("gla_ba", 4), ("gla_og", 2),
    ("gdn_wab", KC * 16), ("gdn_conv", 96), ("gdn_alog", 8), ("gdn_dt", 8), ("gdn_og", 1),
    ("ident", 128), ("ones", 128), ("ones64", 128), ("rot64", 128), ("rot128", 128), ("upto", 128),
    ("cos64", 256), ("sin64", 256), ("cos128", 256), ("sin128", 256), ("window", 256), ("causal", 128),
    ("levels", LEVELS * 128), ("group_rank", 4), ("expert_rank", 16), ("slots", 128), ("slot", 1), ("eps", 5),
]
SMALL_AT = {}
_at = 0
for _name, _cols in SMALL_COLS:
    SMALL_AT[_name] = (_at, _cols)
    _at += _cols
SMALL = _at


def rope_tables(hd):
    n = np.arange(SEQ)
    quarter = hd // 4
    inv = (np.float32(ROPE_THETA) ** (-np.arange(quarter, dtype=np.float32) / np.float32(quarter))).astype(np.float32)
    ang = {0: (n // GRID_W).astype(np.float32)[None, :] * inv[:, None],
           1: (n % GRID_W).astype(np.float32)[None, :] * inv[:, None]}
    cos = np.zeros((P, SEQ), np.float32)
    sin = np.zeros((P, SEQ), np.float32)
    rot = np.zeros((P, P), np.float32)
    for f in range(P):
        axis, r = divmod(f % hd, hd // 2)
        half, q = divmod(r, quarter)
        cos[f] = np.cos(ang[axis][q])
        sin[f] = np.sin(ang[axis][q])
        if half == 0:
            rot[f + quarter, f] = -1.0
        else:
            rot[f - quarter, f] = 1.0
    return cos, sin, rot


EPS = [LN_EPS, QK_EPS, SUBLN_EPS / (1.0 - LAM_INIT) ** 2, NORM_EPS, NORM_EPS * 64]


def shape_constants():
    c = {}
    i = np.arange(P)
    c["ident"] = np.eye(P, dtype=np.float32)
    c["ones"] = np.ones((P, P), np.float32)
    c["ones64"] = (i[:, None] // 64 == i[None, :] // 64).astype(np.float32)
    c["cos64"], c["sin64"], c["rot64"] = rope_tables(64)
    c["cos128"], c["sin128"], c["rot128"] = rope_tables(128)
    c["upto"] = (i[:, None] <= i[None, :]).astype(np.float32)
    c["window"] = np.concatenate([np.where(np.abs(i[:, None] - (i + 128)[None, :]) > WINDOW, -BIG, 0.0),
                                  np.where(np.abs((i + 128)[:, None] - i[None, :]) > WINDOW, -BIG, 0.0)], 1).astype(np.float32)
    c["causal"] = np.where(i[None, :] > i[:, None], -BIG, 0.0).astype(np.float32)
    lv = np.zeros((P, LEVELS, P), np.float32)
    for l in range(LEVELS):
        h = 1 << l
        lv[:, l, :] = ((i[:, None] // (2 * h) == i[None, :] // (2 * h))
                       & (i[:, None] // h % 2 == 0) & (i[None, :] // h % 2 == 1))
    c["levels"] = lv.reshape(P, LEVELS * P)
    c["group_rank"] = np.broadcast_to(np.arange(4, 0, -1, dtype=np.float32), (P, 4))
    c["eps"] = np.broadcast_to(np.array(EPS, np.float32), (P, len(EPS)))
    c["slots"] = np.broadcast_to(i.astype(np.float32), (P, P))
    c["slot"] = i.astype(np.float32)[:, None]
    c["expert_rank"] = np.broadcast_to(np.arange(16, 0, -1, dtype=np.float32), (P, 16))
    return c


class Count:

    def __init__(self, sem, numbers):
        self.sem, self.numbers, self.n = sem, numbers, 0

    def mark(self, *name):
        self.n += 1
        self.numbers[name] = self.n
        return 1

    def at(self, *name):
        return self.numbers.get(name, 1)


class Core:

    def __init__(self, nc, ctx, dram, values):
        self.nc, self.ctx, self.dram, self.values = nc, ctx, dram, values
        with ExitStack() as scope:
            self.ring = scope.enter_context(nc.sbuf_tensor("ring", [P, SLOTS, SLOT], F32))
        self.WL = ctx.enter_context(nc.sbuf_tensor("W_lo", [P, SLOTS, SLOT], F32R))
        self.X = self.sbuf("X", [P, KC, T1])
        with ExitStack() as scope:
            self.H = scope.enter_context(nc.sbuf_tensor("H", [P, KC, T1], F32))
        self.H_part = ctx.enter_context(nc.sbuf_tensor("H_part", [P, KC, T1], F32R))
        with ExitStack() as scope:
            self.ACC = scope.enter_context(nc.sbuf_tensor("ACC", [P, KC, T1], F32))
        self.ACC_part = ctx.enter_context(nc.sbuf_tensor("ACC_part", [P, KC, T1], F32R))
        self.MOD = self.sbuf("MOD", [P, 96, 2])
        self.small = self.sbuf("small", [P, SMALL])
        with ExitStack() as scope:
            self.stat = scope.enter_context(nc.sbuf_tensor("stat", [P, 2, 512], F32))
        self.stat_part = ctx.enter_context(nc.sbuf_tensor("stat_part", [P, 2, 512], F32R))
        self.flag = ctx.enter_context(nc.sbuf_tensor("flag", [P, 1], mybir.dt.int32))
        self.place = self.sbuf("place", [P, 4, EXPERTS])
        self.slot_gate = self.sbuf("slot_gate", [P, 1])
        self.room_size = ROOM
        with ExitStack() as scope:
            self.room = scope.enter_context(nc.sbuf_tensor("room", [P, self.room_size], F32))
        with ExitStack() as scope:
            self.room_part = scope.enter_context(nc.sbuf_tensor("room_part", [P, self.room_size], F32R))
        with ExitStack() as scope:
            scope.enter_context(nc.sbuf_tensor("before_W_hi", [P, self.room_size - SPLIT_SLOTS * SLOT], F32))
            self.WH = scope.enter_context(nc.sbuf_tensor("W_hi", [P, SPLIT_SLOTS, SLOT], F32R))
        self.gate_row = self.H[:, 0:2, :]
        self.route_row = self.H[:, 0:2, :]
        with ExitStack() as scope:
            def split(name, shape):
                return [scope.enter_context(nc.sbuf_tensor(f"{name}_{part}", shape, F32R)) for part in ("hi", "lo")]

            self.HS = split("H_split", [P, KC, T1])
            self.AS = split("A_split", [P, 4, T1])
            self.SEL = scope.enter_context(nc.sbuf_tensor("select", [P, 12, P], F32R))
        acc = self.ACC_part[:].rearrange("p k t -> p (k t)")
        spare = [acc[:, j * T2:(j + 1) * T2] for j in range(2 * KC - 1)]
        self.H_parts = [spare[0:KC], spare[KC:] + [self.stat_part[:, 0, 0:T2]]]
        self.ps = ctx.enter_context(nc.psum_tensor("ps", [P, 8, 512], F32))
        self.ring_full = [self.sem(f"ring_full{j}") for j in range(SLOTS)]
        self.mm_done = self.sem("mm_done")
        self.small_in = self.sem("small_in")
        self.x_in = self.sem("x_in")
        self.stored = self.sem("stored")
        self.stage_done = self.sem("stage_done")
        self.silu_done = self.sem("silu_done")
        self.mod_moved = self.sem("mod_moved")
        self.mul_done = self.sem("mul_done")
        self.hi_done = self.sem("hi_done")
        self.lo_done = self.sem("lo_done")
        self.routes_stored = self.sem("routes_stored")
        self.gate_in = [self.sem(f"gate_in{j}") for j in range(2)]
        self.gated_done = self.sem("gated_done")
        self.add_done = self.sem("add_done")
        self.counts = {}
        self.position = 0
        self.finished = 0
        self.release = []
        self.silus = self.gates = self.muls = self.adds = self.splits = self.gate_loads = 0
        self.uid = 0
        self.ext = self.room[:, self.room_size - 6 * 1024:].rearrange("p (a h t) -> p a h t", a=6, h=8)

    def sbuf(self, name, shape):
        return self.ctx.enter_context(self.nc.sbuf_tensor(name, shape, F32))

    def count(self, name):
        if name not in self.counts:
            self.counts[name] = Count(self.sem(name), self.values.setdefault(name, {}))
        return self.counts[name]

    def sem(self, name):
        return self.ctx.enter_context(self.nc.semaphore(name))

    def s(self, name, rows=P):
        at, n = SMALL_AT[name]
        return self.small[0:rows, at:at + n]

    def carve(self, sizes, reserve=0):
        at, out = 0, {}
        for name, dims in sizes.items():
            n = int(np.prod(dims))
            views = []
            for room in (self.room, self.room_part):
                v = room[:, at:at + n]
                if len(dims) == 2:
                    v = v.rearrange("p (a b) -> p a b", a=dims[0])
                elif len(dims) == 3:
                    v = v.rearrange("p (a b c) -> p a b c", a=dims[0], b=dims[1])
                views.append(v)
            out[name] = views[0]
            if name == "OT":
                out["OT_parts"] = [chunks_of(self.H_part), chunks_of(views[1])]
            at += n
        assert at <= self.room_size - reserve, at
        return out

    def mod(self, layer, part, k, stream):
        c = layer * 48 + part * 8 + k
        return self.MOD[:, c, stream:stream + 1]

    def plan(self, results_per_slot):
        g0 = self.position
        for n in results_per_slot:
            self.finished += n
            self.release.append((self.mm_done, self.finished))
        self.position += len(results_per_slot)
        return g0

    def load(self, sp, g, src):
        if g >= SLOTS:
            sem, count = self.release[g - SLOTS]
            sp.wait_ge(sem, count)
        sp.dma_start(self.slot(g, src), src).then_inc(self.ring_full[g % SLOTS], 16)

    def slot(self, g, like=None):
        v = self.ring[:, g % SLOTS, :]
        if like is not None and len(like.shape) == 3:
            v = v.rearrange("p (k m) -> p k m", k=like.shape[1])
        return v

    def wide(self, g):
        return self.ring[:, g % SLOTS, :].rearrange("p (k m) -> p k m", k=KC)

    def arrived(self, pe, g, i=None):
        v = 16 * (g // SLOTS + 1)
        pe.wait_ge(self.ring_full[g % SLOTS], v if i is None else v + 16 * i)


def columns(w, c0):
    return w[:, c0:c0 + WIDE].rearrange("(k p) m -> p k m", p=P)


class StageCount:

    def __init__(self, count, stage):
        self.count, self.stage = count, stage

    def mark(self, *name):
        return self.count.mark(self.stage, *name)

    def at(self, *name):
        return self.count.at(self.stage, *name)


class Stage:

    def __init__(self, core):
        self.c = core
        core.uid += 1
        kind = type(self).__name__
        self.pe, self.act, self.dve = (StageCount(core.count(f"{kind}_{e}"), core.uid) for e in ("tensor", "scalar", "vector"))
        self.tensor_done, self.scalar_done, self.vector_done = (x.count.sem for x in (self.pe, self.act, self.dve))

    def sync(self, sp):
        pass

    def tensor(self, pe):
        pass

    def scalar(self, act):
        pass

    def vector(self, dve):
        pass


class Modulation(Stage):

    PER_LAYER = 6 * D // WIDE

    def __init__(self, core, rows):
        super().__init__(core)
        self.rows = rows
        self.g0 = core.plan([1] * (2 * self.PER_LAYER))

    def sync(self, sp):
        c = self.c
        sp.dma_start(c.small[:], c.dram["small"]).then_inc(c.small_in, 16)
        for g in range(SLOTS):
            c.load(sp, g, columns(c.dram["w_mod"][0], g * WIDE))
        sp.dma_start(c.X[:], c.dram["xT"]).then_inc(c.x_in, 16)
        rounds = self.PER_LAYER // SLOTS
        for layer in range(2):
            with sp.Fori(1 if layer == 0 else 0, rounds) as i:
                for j in range(SLOTS):
                    src = c.dram["w_mod"][layer][:, bass.ds(i * (SLOTS * WIDE) + j * WIDE, WIDE)]
                    sp.wait_ge(c.mm_done, i * SLOTS + (layer * rounds - 1) * SLOTS + j + 1)
                    sp.dma_start(c.wide(j), src.rearrange("(k p) m -> p k m", p=P)).then_inc(c.ring_full[j], 16)

    def scalar(self, act):
        c = self.c
        act.wait_ge(c.small_in, 16)
        act.activation(c.s("cond"), c.s("cond"), ACT.Silu).then_inc(self.scalar_done, self.act.mark("cond"))
        with act.Fori(0, 2 * self.PER_LAYER // SLOTS) as i:
            for j in range(SLOTS):
                act.wait_ge(c.mm_done, i * SLOTS + j + 1)
                act.activation(self.rows[0:2, bass.ds(i * (SLOTS * WIDE) + j * WIDE, WIDE)],
                               c.ps[0:2, j, 0:WIDE], ACT.Copy).then_inc(c.mod_moved, 1)
        act.wait_ge(self.vector_done, self.dve.at("mod"))
        act.wait_ge(c.x_in, 16)
        for k in range(KC):
            for st, t0 in ((0, 0), (1, CTX)):
                act.activation(c.H[:, k, t0:t0 + 256], c.X[:, k, t0:t0 + 256], ACT.Identity,
                               bias=c.mod(0, 0, k, st), scale=c.mod(0, 1, k, st))

    def tensor(self, pe):
        c = self.c
        pe.wait_ge(self.scalar_done, self.act.at("cond"))
        cond = c.s("cond").rearrange("p (k s) -> p k s", k=KC)

        def slot(j, i, reused):
            c.arrived(pe, j, i)
            if reused:
                pe.wait_ge(c.mod_moved, (j + 1 - SLOTS) + (SLOTS if i is None else i * SLOTS))
            for k in range(KC):
                mm = pe.matmul(c.ps[0:2, j, 0:WIDE], cond[:, k, :], c.wide(j)[:, k, :], start=(k == 0), stop=(k == KC - 1))
            mm.then_inc(c.mm_done, 1)

        for j in range(SLOTS):
            slot(j, None, False)
        with pe.Fori(1, 2 * self.PER_LAYER // SLOTS) as i:
            for j in range(SLOTS):
                slot(j, i, True)
        pe.wait_ge(c.mod_moved, 2 * self.PER_LAYER)
        for n in range(96):
            tr = pe.transpose(c.ps[:, 6, 2 * n:2 * n + 2], self.rows[0:2, n * P:(n + 1) * P], c.s("ident")[0:2, 0:2])
        tr.then_inc(self.tensor_done, self.pe.mark("turned"))

    def vector(self, dve):
        c = self.c
        dve.wait_ge(c.small_in, 16)
        dve.wait_ge(self.tensor_done, self.pe.at("turned"))
        ps = c.ps[:, 6, 0:192].rearrange("p (c s) -> p c s", s=2)
        for st in range(2):
            dve.tensor_tensor(c.MOD[:, :, st], ps[:, :, st], c.s("b_mod"), ALU.add)\
               .then_inc(self.vector_done, self.dve.mark("bias", st))
        dve.wait_ge(self.vector_done, self.dve.at("bias", 1))
        parts = c.MOD[:].rearrange("p (l t k) s -> p l t (k s)", l=2, t=6)
        dve.tensor_scalar(parts[:, :, 1, :], parts[:, :, 1, :], 1.0, None, ALU.add)
        dve.tensor_scalar(parts[:, :, 4, :], parts[:, :, 4, :], 1.0, None, ALU.add)\
           .then_inc(self.vector_done, self.dve.mark("mod"))


class Project(Stage):

    BANKS = 4

    def __init__(self, core, src, sources, items, parts):
        super().__init__(core)
        self.src, self.sources, self.items = src, sources, items
        self.parts = parts
        self.t0 = min(it[4] for it in items)
        self.t1 = max(it[4] + it[5] for it in items)
        self.L0 = core.splits
        core.splits += 2 * len(sources)
        self.f0 = core.finished
        self.g0 = core.plan([sum(1 for it in items if it[0] == s) for s in range(len(sources))])

    def sync(self, sp):
        for s, src in enumerate(self.sources):
            self.c.load(sp, self.g0 + s, src)

    def out(self, i):
        _, kind, lo, n, t0, tn, _ = self.items[i]
        rows, cols = (n, tn) if kind == "feature" else (tn, n)
        return self.c.ps[0:rows, i % self.BANKS, 0:cols]

    def slot_parts(self, s):
        return self.c.WH[:, s % SPLIT_SLOTS, :], self.c.WL[:, (self.g0 + s) % SLOTS, :]

    def tensor(self, pe):
        c = self.c
        last = -1
        for i, (s, kind, lo, n, t0, tn, _) in enumerate(self.items):
            if s != last:
                pe.wait_ge(c.lo_done, self.L0 + 2 * (s + 1))
                last = s
            if i >= self.BANKS:
                pe.wait_ge(self.scalar_done, self.act.at("moved", i - self.BANKS))
            w = [p.rearrange("p (k m) -> p k m", k=KC)[:, :, lo:lo + n] for p in self.slot_parts(s)]
            for k in range(KC):
                if i == 0:
                    pe.wait_ge(self.vector_done, self.dve.at("src", k))
                for n_part, (u, v) in enumerate(((0, 0), (0, 1), (1, 0))):
                    wk, xk = w[u][:, k, :], self.parts[v][k][:, t0:t0 + tn]
                    a, b = (wk, xk) if kind == "feature" else (xk, wk)
                    mm = pe.matmul(self.out(i), a, b, start=(k == 0 and n_part == 0), stop=(k == KC - 1 and n_part == 2))
            mm.then_inc(c.mm_done, 1)

    def scalar(self, act):
        c, T = self.c, slice(self.t0, self.t1)

        def upper(s):
            c.arrived(act, self.g0 + s)
            for half in range(2):
                W = slice(half * SLOT // 2, (half + 1) * SLOT // 2)
                act.activation(self.slot_parts(s)[0][:, W], c.ring[:, (self.g0 + s) % SLOTS, W], ACT.Copy)\
                   .then_inc(c.hi_done, 1)

        upper(0)
        for k in range(KC):
            act.activation(self.parts[0][k][:, T], self.src[:, k, T], ACT.Copy)\
               .then_inc(self.scalar_done, self.act.mark("src", k))
        for s in range(1, SPLIT_SLOTS):
            upper(s)
        for i, it in enumerate(self.items):
            act.wait_ge(c.mm_done, self.f0 + i + 1)
            it[6](act, self.out(i)).then_inc(self.scalar_done, self.act.mark("moved", i))
            s = it[0]
            if s + SPLIT_SLOTS < len(self.sources) and self.items[i + 1][0] != s:
                upper(s + SPLIT_SLOTS)

    def vector(self, dve):
        c, T = self.c, slice(self.t0, self.t1)

        def lower(s):
            hi, lo = self.slot_parts(s)
            for half in range(2):
                W = slice(half * SLOT // 2, (half + 1) * SLOT // 2)
                dve.wait_ge(c.hi_done, self.L0 + 2 * s + half + 1)
                dve.tensor_tensor(lo[:, W], c.ring[:, (self.g0 + s) % SLOTS, W], hi[:, W].bitcast(F32), ALU.subtract)\
                   .then_inc(c.lo_done, 1)

        lower(0)
        for k in range(KC):
            dve.wait_ge(self.scalar_done, self.act.at("src", k))
            hi, lo = (p[k][:, T] for p in self.parts)
            dve.tensor_tensor(lo, self.src[:, k, T], hi.bitcast(F32), ALU.subtract)\
               .then_inc(self.vector_done, self.dve.mark("src", k))
        for s in range(1, len(self.sources)):
            lower(s)


def chunks_of(tensor):
    return [tensor[:, k, :] for k in range(KC)]


def move_to(dst, scale=1.0):
    return lambda act, ps: act.activation(dst, ps, ACT.Copy, scale=scale)


def feature_items(dst, slots, t0, tn, scale=1.0, first=0):
    out = []
    for n, s in enumerate(slots):
        for m in range(2):
            out.append((s, "feature", m * P, P, t0, tn, move_to(dst[:, first + 2 * n + m, t0:t0 + tn], scale)))
    return out


def token_items(dst, slots, tiles, lo=0, n=WIDE, at=0):
    out = []
    for j, s in enumerate(slots):
        for t, (t0, tn) in enumerate(tiles):
            out.append((s, "token", lo, n, t0, tn, move_to(dst[0:tn, t, at + j * WIDE:at + j * WIDE + n])))
    return out


class Rope(Stage):

    def __init__(self, core, chunks, hd, tmp, copies=()):
        super().__init__(core)
        self.chunks, self.hd, self.tmp, self.copies = chunks, hd, tmp, copies

    def tensor(self, pe):
        c = self.c
        for i, x in enumerate(self.chunks):
            if i >= 4:
                pe.wait_ge(self.vector_done, self.dve.at("sin", i - 4))
            pe.matmul(c.ps[:, i % 4, 0:SEQ], c.s(f"rot{self.hd}"), x, start=True, stop=True).then_inc(self.tensor_done, self.pe.mark(i))

    def vector(self, dve):
        c = self.c
        for i, x in enumerate(self.chunks):
            dve.wait_ge(self.tensor_done, self.pe.at(i))
            t = self.tmp[:, i % 2, 0:SEQ]
            if i >= 2:
                dve.wait_ge(self.vector_done, self.dve.at("sum", i - 2))
            dve.tensor_tensor(t, c.ps[:, i % 4, 0:SEQ], c.s(f"sin{self.hd}"), ALU.mult).then_inc(self.vector_done, self.dve.mark("sin", i))
            dve.tensor_tensor(x, x, c.s(f"cos{self.hd}"), ALU.mult).then_inc(self.vector_done, self.dve.mark("cos", i))
            dve.wait_ge(self.vector_done, self.dve.at("cos", i))
            dve.tensor_tensor(x, x, t, ALU.add).then_inc(self.vector_done, self.dve.mark("sum", i))
        dve.wait_ge(self.vector_done, self.dve.at("sum", len(self.chunks) - 1))
        for dst, src in self.copies:
            dve.tensor_copy(dst, src)


class HeadNorm(Stage):

    def __init__(self, core, items, eps, sq, rs, after=1.0):
        super().__init__(core)
        self.after = after
        self.items, self.sq, self.rs = items, sq, rs
        at = min(range(len(EPS)), key=lambda j: abs(EPS[j] * after * after / eps - 1.0))
        self.eps = core.s("eps")[:, at:at + 1]
        self.width = max(len(it[0]) for it in items)

    def scalar(self, act):
        c = self.c
        N = len(self.items)
        for i in range(N + 1):
            if i < N:
                chunks, tn = self.items[i][0], self.items[i][1]
                for j, x in enumerate(chunks):
                    if i >= 2 and j == 0:
                        act.wait_ge(self.tensor_done, self.pe.at(i - 2))
                    act.activation(self.sq[:, (i % 2) * self.width + j, 0:tn], x, ACT.Square).then_inc(self.scalar_done, self.act.mark("sq", i, j))
            if i >= 1:
                tn, n = self.items[i - 1][1], self.items[i - 1][3]
                act.wait_ge(self.tensor_done, self.pe.at(i - 1))
                if i >= 3:
                    act.wait_ge(self.vector_done, self.dve.at("out", i - 3))
                act.activation(self.rs[:, (i - 1) % 2, 0:tn], c.ps[:, (i - 1) % 4, 0:tn], ACT.Sqrt, bias=self.eps,
                               scale=1.0 / (n * self.after ** 2)).then_inc(self.scalar_done, self.act.mark("sd", i - 1))

    def tensor(self, pe):
        c = self.c
        for i, (chunks, tn, ones, *_) in enumerate(self.items):
            if i >= 4:
                pe.wait_ge(self.scalar_done, self.act.at("sd", i - 4))
            for j in range(len(chunks)):
                pe.wait_ge(self.scalar_done, self.act.at("sq", i, j))
                mm = pe.matmul(c.ps[:, i % 4, 0:tn], ones, self.sq[:, (i % 2) * self.width + j, 0:tn],
                               start=(j == 0), stop=(j == len(chunks) - 1))
            mm.then_inc(self.tensor_done, self.pe.mark(i))

    def vector(self, dve):
        for i, (chunks, tn, _, _, gains, factor) in enumerate(self.items):
            rs = self.rs[:, i % 2, 0:tn]
            dve.wait_ge(self.scalar_done, self.act.at("sd", i))
            dve.reciprocal(rs, rs).then_inc(self.vector_done, self.dve.mark("rs", i))
            dve.wait_ge(self.vector_done, self.dve.at("rs", i))
            for j, x in enumerate(chunks):
                g = gains[j] if gains else factor
                ins = dve.scalar_tensor_tensor(x, x, g, rs, ALU.mult, ALU.mult)
            ins.then_inc(self.vector_done, self.dve.mark("out", i))


class Attention(Stage):

    def __init__(self, core, items, p, s, pT, cols):
        super().__init__(core)
        self.items, self.p, self.sb, self.pT, self.cols = items, p, s, pT, cols

    def bank(self, i, m):
        return (i % 2) * 2 + m

    def blocks(self, it):
        return [(lo, n) for lo, n, _ in it["values"]]

    def tensor(self, pe):
        c, N = self.c, len(self.items)
        ident = c.s("ident")
        for step in range(N + 3):
            if step < N:
                i, it = step, self.items[step]
                if i >= 2:
                    for m in range(len(self.items[i - 2]["maps"])):
                        pe.wait_ge(self.scalar_done, self.act.at("exp", i - 2, m))
                for m, products in enumerate(it["maps"]):
                    for n, (a, b) in enumerate(products):
                        mm = pe.matmul(c.ps[0:it["rows"], self.bank(i, m), 0:it["keys"]], a, b,
                                       start=(n == 0), stop=(n == len(products) - 1))
                    mm.then_inc(self.tensor_done, self.pe.mark("scores", i, m))
            if 2 <= step < N + 2:
                i, it = step - 2, self.items[step - 2]
                pe.wait_ge(self.vector_done, self.dve.at("weights", i))
                if i >= 2:
                    pe.wait_ge(self.scalar_done, self.act.at("turned", i - 2))
                for b, (lo, n) in enumerate(self.blocks(it)):
                    tr = pe.transpose(c.ps[0:n, 4 + i % 2, b * P:b * P + it["rows"]],
                                      self.p[0:it["rows"], 2 * (i % 2), lo:lo + n], ident[0:it["rows"], 0:it["rows"]])
                tr.then_inc(self.tensor_done, self.pe.mark("turned", i))
            if step >= 3:
                i, it = step - 3, self.items[step - 3]
                pe.wait_ge(self.scalar_done, self.act.at("turned", i))
                if i >= 2:
                    pe.wait_ge(self.scalar_done, self.act.at("out", i - 2))
                o = self.out_ps(i)
                for b, (lo, n, v) in enumerate(it["values"]):
                    mm = pe.matmul(o, v, self.pT[0:n, i % 2, b * P:b * P + it["rows"]],
                                   start=(b == 0), stop=(b == len(it["values"]) - 1))
                mm.then_inc(self.tensor_done, self.pe.mark("out", i))

    def out_ps(self, i):
        it = self.items[i]
        lo, n = it["out_rows"]
        return self.c.ps[lo:lo + n, 6 + i % 2, 0:it["rows"]]

    def vector(self, dve):
        c, N = self.c, len(self.items)
        for step in range(N + 1):
            if step < N:
                i, it = step, self.items[step]
                R, K = it["rows"], it["keys"]
                for m in range(len(it["maps"])):
                    col = self.cols[0:R, self.bank(i, m), :]
                    dve.wait_ge(self.tensor_done, self.pe.at("scores", i, m))
                    if i >= 2:
                        dve.wait_ge(self.scalar_done, self.act.at("exp", i - 2, m if m < len(self.items[i - 2]["maps"]) else 0))
                        dve.wait_ge(self.vector_done, self.dve.at("weights", i - 2))
                    src = c.ps[0:R, self.bank(i, m), 0:K]
                    if it.get("masks"):
                        dst = self.sb[0:R, self.bank(i, m), 0:K]
                        qbias = it.get("qbias")
                        covered = 0
                        for mask, lo, hi in it["masks"] + [(None, K, K)]:
                            if lo > covered:
                                ins = dve.tensor_scalar(dst[:, covered:lo], src[:, covered:lo], it["scale"],
                                                        0.0 if qbias is None else qbias, ALU.mult, ALU.add)
                            if mask is not None:
                                ins = dve.scalar_tensor_tensor(dst[:, lo:hi], src[:, lo:hi],
                                                               it["scale"] if qbias is None else qbias, mask,
                                                               ALU.mult if qbias is None else ALU.add, ALU.add)
                            covered = hi
                        ins.then_inc(self.vector_done, self.dve.mark("masked", i, m))
                        dve.wait_ge(self.vector_done, self.dve.at("masked", i, m))
                        src, scale = dst, 1.0
                    else:
                        scale = it["scale"]
                    dve.reduce_max(col[:, 0:1], src, AX_X).then_inc(self.vector_done, self.dve.mark("max", i, m))
                    dve.wait_ge(self.vector_done, self.dve.at("max", i, m))
                    if it.get("sink") is not None:
                        dve.tensor_scalar(col[:, 1:2], col[:, 0:1], scale, it["sink"], ALU.mult, ALU.max).then_inc(self.vector_done, self.dve.mark("smax", i, m))
                        dve.wait_ge(self.vector_done, self.dve.at("smax", i, m))
                        dve.tensor_scalar(col[:, 2:3], col[:, 1:2], -1.0, None, ALU.mult).then_inc(self.vector_done, self.dve.mark("neg", i, m))
                    else:
                        dve.tensor_scalar(col[:, 2:3], col[:, 0:1], -scale, None, ALU.mult).then_inc(self.vector_done, self.dve.mark("neg", i, m))
            if step >= 1:
                i, it = step - 1, self.items[step - 1]
                R, K, M = it["rows"], it["keys"], len(it["maps"])
                for m in range(M):
                    col = self.cols[0:R, self.bank(i, m), :]
                    dve.wait_ge(self.scalar_done, self.act.at("exp", i, m))
                    total = col[:, 3:4]
                    if it.get("sink") is not None:
                        dve.wait_ge(self.scalar_done, self.act.at("esink", i, m))
                        dve.tensor_tensor(col[:, 5:6], col[:, 3:4], col[:, 4:5], ALU.add).then_inc(self.vector_done, self.dve.mark("total", i, m))
                        dve.wait_ge(self.vector_done, self.dve.at("total", i, m))
                        total = col[:, 5:6]
                    dve.reciprocal(col[:, 6:7], total).then_inc(self.vector_done, self.dve.mark("rec", i, m))
                    dve.wait_ge(self.vector_done, self.dve.at("rec", i, m))
                p0 = self.p[0:R, 2 * (i % 2), 0:K]
                col = self.cols[0:R, self.bank(i, 0), :]
                ins = dve.tensor_scalar(p0, p0, col[:, 6:7], None, ALU.mult)
                if M == 2:
                    ins.then_inc(self.vector_done, self.dve.mark("p0", i))
                    p1 = self.p[0:R, 2 * (i % 2) + 1, 0:K]
                    col1 = self.cols[0:R, self.bank(i, 1), :]
                    dve.tensor_tensor(col1[:, 7:8], col1[:, 6:7], it["lam"], ALU.mult).then_inc(self.vector_done, self.dve.mark("lr", i))
                    dve.wait_ge(self.vector_done, self.dve.at("lr", i))
                    ins = dve.scalar_tensor_tensor(p0, p1, col1[:, 7:8], p0, ALU.mult, ALU.add)
                ins.then_inc(self.vector_done, self.dve.mark("weights", i))

    def scalar(self, act):
        c, N = self.c, len(self.items)
        for step in range(N + 3):
            if step < N:
                i, it = step, self.items[step]
                R, K = it["rows"], it["keys"]
                for m in range(len(it["maps"])):
                    col = self.cols[0:R, self.bank(i, m), :]
                    act.wait_ge(self.vector_done, self.dve.at("neg", i, m))
                    if i >= 2:
                        act.wait_ge(self.tensor_done, self.pe.at("turned", i - 2))
                    masked = bool(it.get("masks"))
                    src = self.sb[0:R, self.bank(i, m), 0:K] if masked else c.ps[0:R, self.bank(i, m), 0:K]
                    if it.get("sink") is not None:
                        act.activation(col[:, 4:5], it["sink"], ACT.Exp, bias=col[:, 2:3]).then_inc(self.scalar_done, self.act.mark("esink", i, m))
                    act.activation(self.p[0:R, 2 * (i % 2) + m, 0:K], src, ACT.Exp, bias=col[:, 2:3],
                                              scale=1.0 if masked else it["scale"], accum_out=col[:, 3:4]).then_inc(self.scalar_done, self.act.mark("exp", i, m))
            if 2 <= step < N + 2:
                i, it = step - 2, self.items[step - 2]
                act.wait_ge(self.tensor_done, self.pe.at("turned", i))
                if i >= 2:
                    act.wait_ge(self.tensor_done, self.pe.at("out", i - 2))
                R = it["rows"]
                full = all(n == P for _, n in self.blocks(it)) and R == P
                if full:
                    w = len(self.blocks(it)) * P
                    ins = act.activation(self.pT[:, i % 2, 0:w], c.ps[:, 4 + i % 2, 0:w], ACT.Copy)
                else:
                    for b, (lo, n) in enumerate(self.blocks(it)):
                        ins = act.activation(self.pT[0:n, i % 2, b * P:b * P + R], c.ps[0:n, 4 + i % 2, b * P:b * P + R],
                                             ACT.Copy)
                ins.then_inc(self.scalar_done, self.act.mark("turned", i))
            if step >= 3:
                i, it = step - 3, self.items[step - 3]
                act.wait_ge(self.tensor_done, self.pe.at("out", i))
                act.activation(it["out"], self.out_ps(i), ACT.Copy).then_inc(self.scalar_done, self.act.mark("out", i))


class LayerNorm(Stage):

    def __init__(self, core, layer, which, streams, nxt, shift_to=None):
        super().__init__(core)
        self.layer, self.which, self.streams, self.nxt, self.shift_to = layer, which, streams, nxt, shift_to
        self.t0 = streams[0][1]
        self.tn = 256 * len(streams)

    def scalar(self, act):
        c, t = self.c, slice(self.t0, self.t0 + self.tn)
        for k in range(KC):
            act.activation(c.H[:, k, t], c.X[:, k, t], ACT.Copy, scale=ALPHA).then_inc(self.scalar_done, self.act.mark("ax", k))
        for k in range(KC):
            act.wait_ge(self.vector_done, self.dve.at("centred", k))
            act.activation(c.H[:, k, t], c.ACC[:, k, t], ACT.Square).then_inc(self.scalar_done, self.act.mark("sq", k))
        act.wait_ge(self.vector_done, self.dve.at("var"))
        act.activation(c.stat[:, 0, 0:self.tn], c.stat[:, 0, 0:self.tn], ACT.Sqrt).then_inc(self.scalar_done, self.act.mark("sd"))
        col = self.layer * 16 + self.which * 8
        for k in range(KC):
            act.wait_ge(self.vector_done, self.dve.at("normed", k))
            dst = c.X[:, k, t] if self.shift_to is None else c.X[:, k, self.shift_to:self.shift_to + self.tn]
            act.activation(dst, c.ACC[:, k, t], ACT.Identity, bias=c.s("ln_b")[:, col + k:col + k + 1],
                                      scale=c.s("ln_g")[:, col + k:col + k + 1]).then_inc(self.scalar_done, self.act.mark("x", k))
        if self.shift_to is not None:
            act.activation(c.X[:, :, 0:META], c.s("meta").rearrange("p (k t) -> p k t", k=KC), ACT.Copy)

    def tensor(self, pe):
        c, t = self.c, slice(self.t0, self.t0 + self.tn)
        for k in range(KC):
            pe.wait_ge(self.vector_done, self.dve.at("z", k))
            mm = pe.matmul(c.ps[:, 0, 0:self.tn], c.s("ones"), c.ACC[:, k, t], start=(k == 0), stop=(k == KC - 1))
        mm.then_inc(self.tensor_done, self.pe.mark("sum"))
        for k in range(KC):
            pe.wait_ge(self.scalar_done, self.act.at("sq", k))
            mm = pe.matmul(c.ps[:, 1, 0:self.tn], c.s("ones"), c.H[:, k, t], start=(k == 0), stop=(k == KC - 1))
        mm.then_inc(self.tensor_done, self.pe.mark("sumsq"))

    def vector(self, dve):
        c, t = self.c, slice(self.t0, self.t0 + self.tn)
        gate = 2 if self.which == 0 else 5
        for k in range(KC):
            dve.wait_ge(self.scalar_done, self.act.at("ax", k))
            for st, s0 in self.streams:
                u = slice(s0, s0 + 256)
                ins = dve.scalar_tensor_tensor(c.ACC[:, k, u], c.ACC[:, k, u], c.mod(self.layer, gate, k, st),
                                               c.H[:, k, u], ALU.mult, ALU.add)
            ins.then_inc(self.vector_done, self.dve.mark("z", k))
        dve.wait_ge(self.tensor_done, self.pe.at("sum"))
        for k in range(KC):
            dve.scalar_tensor_tensor(c.ACC[:, k, t], c.ps[:, 0, 0:self.tn], -1.0 / D, c.ACC[:, k, t],
                                                ALU.mult, ALU.add).then_inc(self.vector_done, self.dve.mark("centred", k))
        dve.wait_ge(self.tensor_done, self.pe.at("sumsq"))
        rs = c.stat[:, 0, 0:self.tn]
        dve.tensor_scalar(rs, c.ps[:, 1, 0:self.tn], 1.0 / D, LN_EPS, ALU.mult, ALU.add).then_inc(self.vector_done, self.dve.mark("var"))
        dve.wait_ge(self.scalar_done, self.act.at("sd"))
        dve.reciprocal(rs, rs).then_inc(self.vector_done, self.dve.mark("rs"))
        dve.wait_ge(self.vector_done, self.dve.at("rs"))
        for k in range(KC):
            dve.tensor_tensor(c.ACC[:, k, t], c.ACC[:, k, t], rs, ALU.mult).then_inc(self.vector_done, self.dve.mark("normed", k))
        if self.nxt:
            layer, part = self.nxt
            for k in range(KC):
                dve.wait_ge(self.scalar_done, self.act.at("x", k))
                for st, s0 in (self.streams if self.which == 0 else ((0, 0), (1, CTX))):
                    u = slice(s0, s0 + 256)
                    dve.tensor_scalar(c.H[:, k, u], c.X[:, k, u], c.mod(layer, part + 1, k, st),
                                      c.mod(layer, part, k, st), ALU.mult, ALU.add)


class RmsNorm(Stage):

    def __init__(self, core, gain, add):
        super().__init__(core)
        self.gain, self.add = gain, add

    def scalar(self, act):
        c = self.c
        for k in range(KC):
            if self.add:
                act.wait_ge(self.vector_done, self.dve.at("x", k))
            act.activation(c.H[:, k, 0:T2], c.X[:, k, 0:T2], ACT.Square).then_inc(self.scalar_done, self.act.mark("sq", k))
        act.wait_ge(self.vector_done, self.dve.at("var"))
        act.activation(c.stat[:, 0, 0:T2], c.stat[:, 0, 0:T2], ACT.Sqrt).then_inc(self.scalar_done, self.act.mark("sd"))

    def tensor(self, pe):
        c = self.c
        for k in range(KC):
            pe.wait_ge(self.scalar_done, self.act.at("sq", k))
            mm = pe.matmul(c.ps[:, 0, 0:T2], c.s("ones"), c.H[:, k, 0:T2], start=(k == 0), stop=(k == KC - 1))
        mm.then_inc(self.tensor_done, self.pe.mark("sumsq"))

    def vector(self, dve):
        c = self.c
        if self.add:
            for k in range(KC):
                dve.tensor_tensor(c.X[:, k, 0:T2], c.X[:, k, 0:T2], c.ACC[:, k, 0:T2], ALU.add).then_inc(self.vector_done, self.dve.mark("x", k))
        dve.wait_ge(self.tensor_done, self.pe.at("sumsq"))
        rs = c.stat[:, 0, 0:T2]
        dve.tensor_scalar(rs, c.ps[:, 0, 0:T2], 1.0 / D, NORM_EPS, ALU.mult, ALU.add).then_inc(self.vector_done, self.dve.mark("var"))
        dve.wait_ge(self.scalar_done, self.act.at("sd"))
        dve.reciprocal(rs, rs).then_inc(self.vector_done, self.dve.mark("rs"))
        dve.wait_ge(self.vector_done, self.dve.at("rs"))
        for k in range(KC):
            dve.scalar_tensor_tensor(c.H[:, k, 0:T2], c.X[:, k, 0:T2], self.gain[:, k:k + 1], rs, ALU.mult, ALU.mult)


class Router(Stage):

    def __init__(self, core, t0, tn, m):
        super().__init__(core)
        self.t0, self.tn, self.nt, self.m = t0, tn, tn // P, m

    def tensor(self, pe):
        c, nt = self.c, self.nt
        w = c.s("w_router").rearrange("p (k e) -> p k e", k=KC)
        for t in range(nt):
            for k in range(KC):
                mm = pe.matmul(c.ps[:, 0, t * 16:(t + 1) * 16], c.H[:, k, self.t0 + t * P:self.t0 + (t + 1) * P],
                               w[:, k, :], start=(k == 0), stop=(k == KC - 1))
        mm.then_inc(self.tensor_done, self.pe.mark("logits"))
        pe.wait_ge(self.vector_done, self.dve.at("member"))
        for q in range(nt):
            for t in range(q + 1):
                pe.matmul(c.ps[:, 3, q * 16:(q + 1) * 16], c.s("upto" if t == q else "ones"), self.m["b"][:, t, :],
                          start=(t == 0), stop=(t == q))
        for t in range(nt):
            mm = pe.matmul(c.ps[:, 4, 0:16], c.s("ones"), self.m["b"][:, t, :], start=(t == 0), stop=(t == nt - 1))
        mm.then_inc(self.tensor_done, self.pe.mark("places"))
        pe.wait_ge(self.vector_done, self.dve.at("gates"))
        for t in range(nt):
            pe.transpose(c.ps[0:16, 1, t * P:(t + 1) * P], self.m["g"][:, t, :], c.s("ident"))
            tr = pe.transpose(c.ps[0:16, 2, t * P:(t + 1) * P], self.m["place"][:, t, :], c.s("ident"))
        tr.then_inc(self.tensor_done, self.pe.mark("turned"))

    def scalar(self, act):
        c = self.c
        act.wait_ge(self.tensor_done, self.pe.at("logits"))
        sc = self.m["sc"].rearrange("p t e -> p (t e)")[:, 0:self.nt * 16]
        act.activation(sc, c.ps[:, 0, 0:self.nt * 16], ACT.Sigmoid).then_inc(self.scalar_done, self.act.mark("scores"))
        act.wait_ge(self.tensor_done, self.pe.at("turned"))
        rows = self.m["rows"][0:16, :, 0:self.tn]
        act.activation(rows, c.ps[0:16, 1:3, 0:self.tn], ACT.Copy).then_inc(self.scalar_done, self.act.mark("rows"))
        act.wait_ge(self.scalar_done, self.act.at("rows"))
        act.dma_start(c.dram["routes"][:, :, 0:self.tn], rows).then_inc(c.routes_stored, 16)

    def vector(self, dve):
        c, nt, m = self.c, self.nt, self.m
        n = [0]

        def step(ins):
            ins.then_inc(self.vector_done, self.dve.mark("pick", n[0]))
            dve.wait_ge(self.vector_done, self.dve.at("pick", n[0]))
            n[0] += 1

        sc, sel, a, b = (m[x][:, 0:nt, :] for x in ("sc", "sel", "ta", "tb"))
        dve.wait_ge(self.scalar_done, self.act.at("scores"))
        bias = c.s("b_router").unsqueeze(1).to_broadcast([P, nt, 16])
        step(dve.tensor_tensor(sel, sc, bias, ALU.add))
        v = sel.rearrange("p t (g e) -> p (t g) e", e=4)
        hi, lo = m["hi"][:, 0:nt * 4, :], m["lo"][:, 0:nt * 4, :]
        dve.tensor_tensor(hi, v[:, :, 0:2], v[:, :, 2:4], ALU.max)
        step(dve.tensor_tensor(lo, v[:, :, 0:2], v[:, :, 2:4], ALU.min))
        gs, g2, g3 = (m["gs"][:, j, 0:nt * 4] for j in range(3))
        dve.tensor_tensor(gs, hi[:, :, 0], hi[:, :, 1], ALU.max)
        dve.tensor_tensor(g2, hi[:, :, 0], hi[:, :, 1], ALU.min)
        step(dve.tensor_tensor(g3, lo[:, :, 0], lo[:, :, 1], ALU.max))
        step(dve.tensor_tensor(g2, g2, g3, ALU.max))
        step(dve.tensor_tensor(gs, gs, g2, ALU.add))
        gv, g2v = (x.rearrange("p (t g) -> p t g", g=4) for x in (gs, g2))
        mx = m["mx"][:, 0:nt]
        mxb4 = mx.unsqueeze(2).to_broadcast([P, nt, 4])
        mxb16 = mx.unsqueeze(2).to_broadcast([P, nt, 16])
        step(dve.reduce_max(mx, gv, AX_X))
        step(dve.tensor_tensor(g2v, gv, mxb4, ALU.is_ge))
        step(dve.tensor_tensor(g2v, g2v, c.s("group_rank").unsqueeze(1).to_broadcast([P, nt, 4]), ALU.mult))
        step(dve.reduce_max(mx, g2v, AX_X))
        step(dve.tensor_tensor(g2v, g2v, mxb4, ALU.is_ge))
        member = g2.unsqueeze(2).to_broadcast([P, nt * 4, 4])
        step(dve.tensor_tensor(v, v, member, ALU.mult))
        step(dve.tensor_scalar(g3, g2, -1.0, BIG, ALU.add, ALU.mult))
        step(dve.tensor_tensor(v, v, g3.unsqueeze(2).to_broadcast([P, nt * 4, 4]), ALU.add))
        rank = c.s("expert_rank").unsqueeze(1).to_broadcast([P, nt, 16])
        picked = m["g"][:, 0:nt, :]
        for n_pick in range(2):
            step(dve.reduce_max(mx, sel, AX_X))
            step(dve.tensor_tensor(a, sel, mxb16, ALU.is_ge))
            step(dve.tensor_tensor(a, a, rank, ALU.mult))
            step(dve.reduce_max(mx, a, AX_X))
            step(dve.tensor_tensor(a, a, mxb16, ALU.is_ge))
            if n_pick == 0:
                step(dve.scalar_tensor_tensor(sel, a, -2.0 * BIG, sel, ALU.mult, ALU.add))
                step(dve.tensor_copy(b, a))
            else:
                step(dve.tensor_tensor(b, a, b, ALU.add))
                dve.tensor_copy(m["b"], b).then_inc(self.vector_done, self.dve.mark("member"))
        step(dve.tensor_tensor(a, b, sc, ALU.mult))
        step(dve.reduce_sum(mx, a, AX_X))
        step(dve.reciprocal(mx, mx))
        step(dve.tensor_tensor(picked, a, mxb16, ALU.mult))
        dve.wait_ge(self.tensor_done, self.pe.at("places"))
        places = c.ps[:, 3, 0:nt * 16].rearrange("p (t e) -> p t e", e=16)
        step(dve.tensor_tensor(sel, places, b, ALU.mult))
        step(dve.reduce_max(mx[:, 0:1], c.ps[:, 4, 0:16], AX_X))
        dve.tensor_scalar(c.flag[:, 0:1], mx[:, 0:1], float(CAPACITY), None, ALU.is_gt)
        dve.tensor_scalar(c.place[:, 0:nt, :], sel, -1.0, None, ALU.add)
        dve.tensor_scalar(m["place"][:, 0:nt, :], sel, -1.0, None, ALU.add)\
           .then_inc(self.vector_done, self.dve.mark("gates"))


class FeedForward(Stage):

    def __init__(self, core, t0, tn, groups, gate, up, down, gates=0):
        super().__init__(core)
        self.t0, self.tn, self.N = t0, tn, groups
        self.src = {"G": gate, "U": up, "D": down}
        self.gates = gates
        self.R = (groups - 2) // 2
        self.M0 = core.finished
        self.g0 = core.plan([2, 2] + [2, 2, 8] * (groups - 1) + [8])
        self.L0 = core.splits
        core.splits += 2 * 3 * groups
        self.s0, self.a0, self.q0 = core.silus, core.gates, core.muls
        core.silus += 2 * groups
        core.gates += 2 * groups
        self.ops = 3 if gates else 2
        core.muls += 2 * self.ops * groups
        self.d0 = core.adds + KC
        core.adds += KC + KC * groups
        self.r0 = core.gate_loads
        if gates:
            core.gate_loads += groups // 2

    def pos(self, kind, n):
        if kind == "D":
            return 4 + 3 * n if n < self.N - 1 else 2 + 3 * n
        return (kind == "U") + (0 if n == 0 else 2 + 3 * (n - 1))

    def result(self, kind, n):
        if kind == "D":
            return self.M0 + 4 + 12 * n + (4 if n < self.N - 1 else 0)
        return self.M0 + (2 if kind == "U" else 0) + (0 if n == 0 else 4 + 12 * (n - 1))

    def through(self, p):
        if p < 2:
            return self.M0 + 2 * (p + 1)
        step, j = divmod(p - 2, 3)
        return self.M0 + 4 + 12 * step + (2, 4, 12)[j]

    def parts(self, p):
        c = self.c
        return c.WH[:, p % SPLIT_SLOTS, :], c.WL[:, (self.g0 + p) % SLOTS, :]

    @staticmethod
    def at(v, i, per_round):
        return v if i is None else v + i * per_round

    def load(self, sp, kind, n, i=None):
        c, g = self.c, self.g0 + self.pos(kind, n)
        offset = (lambda size: (n // 2) * size) if i is None else (lambda size: i * size + (n // 2) * size)
        if i is None:
            sem, count = c.release[g - SLOTS]
            sp.wait_ge(sem, count)
        else:
            sp.wait_ge(c.mm_done, i * 24 + (self.through(g - self.g0) - 24))
        src = self.src[kind](offset, n % 2)
        dst = c.ring[:, g % SLOTS, :].rearrange("p (k m) -> p k m", k=src.shape[1])
        sp.dma_start(dst, src).then_inc(c.ring_full[g % SLOTS], 16)

    def sync(self, sp):
        self.load(sp, "G", 0)
        self.load(sp, "U", 0)

        def step(n, i=None):
            self.load(sp, "G", n + 1, i)
            self.load(sp, "U", n + 1, i)
            self.load(sp, "D", n, i)

        step(0)
        step(1)
        with sp.Fori(1, self.R) as i:
            step(0, i)
            step(1, i)
        for n in range(2 * self.R, self.N - 1):
            step(n)
        self.load(sp, "D", self.N - 1)

    def tensor(self, pe):
        c, tn = self.c, self.tn
        Hh, Hl = c.HS
        Ah, Al = c.AS
        X = slice(0, tn)

        def split_slot(kind, n, i, k):
            p = self.pos(kind, n)
            pe.wait_ge(c.lo_done, self.at(self.L0 + 2 * (p + 1), i, 12))
            return [w.rearrange("p (k m) -> p k m", k=k) for w in self.parts(p)]

        def wide(kind, n, i=None):
            wh, wl = split_slot(kind, n, i, KC)
            for u in range(2):
                if n > 0:
                    if kind == "G":
                        pe.wait_ge(c.silu_done, self.at(self.s0 + 2 * (n - 1) + u + 1, i, 4))
                    else:
                        pe.wait_ge(c.mul_done, self.at(self.q0 + 2 * self.ops * (n - 1) + u + 1, i, 4 * self.ops))
                out = c.ps[:, u + (2 if kind == "U" else 0), 0:tn]
                M = slice(u * P, (u + 1) * P)
                for k in range(KC):
                    if n == 0 and kind == "G" and u == 0:
                        pe.wait_ge(self.vector_done, self.dve.at("H", k))
                    pe.matmul(out, wh[:, k, M], Hh[:, k, X], start=(k == 0), stop=False)
                    pe.matmul(out, wh[:, k, M], Hl[:, k, X], start=False, stop=False)
                    mm = pe.matmul(out, wl[:, k, M], Hh[:, k, X], start=False, stop=(k == KC - 1))
                mm.then_inc(c.mm_done, 1)

        def down(n, i=None):
            wh, wl = split_slot("D", n, i, 2)
            pe.wait_ge(c.gated_done, self.at(self.a0 + 2 * n + 2, i, 4))
            for j in range(KC):
                pe.wait_ge(c.add_done, self.at(self.d0 + 8 * n + j - 3, i, 16))
                out = c.ps[:, 4 + j % 4, 0:tn]
                M = slice(j * P, (j + 1) * P)
                for k in range(2):
                    ah, al = (a[:, 2 * (n % 2) + k, X] for a in (Ah, Al))
                    pe.matmul(out, wh[:, k, M], ah, start=(k == 0), stop=False)
                    pe.matmul(out, wh[:, k, M], al, start=False, stop=False)
                    mm = pe.matmul(out, wl[:, k, M], ah, start=False, stop=(k == 1))
                mm.then_inc(c.mm_done, 1)

        def step(n, i=None):
            wide("G", n + 1, i)
            wide("U", n + 1, i)
            down(n, i)

        wide("G", 0)
        wide("U", 0)
        with pe.Fori(0, self.R) as i:
            step(0, i)
            step(1, i)
        for n in range(2 * self.R, self.N - 1):
            step(n)
        down(self.N - 1)

    def scalar(self, act):
        c, tn = self.c, self.tn

        def upper(kind, n, i=None):
            p = self.pos(kind, n)
            g = self.g0 + p
            c.arrived(act, g, i)
            if p >= SPLIT_SLOTS:
                act.wait_ge(c.mm_done, self.at(self.through(p - SPLIT_SLOTS), i, 24))
            for half in range(2):
                C = slice(half * SLOT // 2, (half + 1) * SLOT // 2)
                act.activation(self.parts(p)[0][:, C], c.ring[:, g % SLOTS, C], ACT.Copy).then_inc(c.hi_done, 1)

        def silu(n, i=None):
            for u in range(2):
                if n > 0:
                    act.wait_ge(c.gated_done, self.at(self.a0 + 2 * (n - 1) + u + 1, i, 4))
                act.wait_ge(c.mm_done, self.at(self.result("G", n) + u + 1, i, 24))
                act.activation(c.stat[:, u, 0:tn], c.ps[:, u, 0:tn], ACT.Silu).then_inc(c.silu_done, 1)

        def gate_row(n, i=None):
            if not self.gates:
                return
            if n >= 2:
                act.wait_ge(c.gated_done, self.at(self.a0 + 2 * (n - 2) + 2, i, 4))
            e = n // 2 if i is None else i + n // 2
            row = c.dram["routes"][bass.ds(e, 1), 0, 0:tn].to_broadcast([P, tn])
            act.dma_start(c.gate_row[:, n % 2, 0:tn], row).then_inc(c.gate_in[n % 2], 16)

        if self.gates:
            act.wait_ge(c.routes_stored, 16 * self.gates)
        for k in range(KC):
            act.activation(c.HS[0][:, k, 0:tn], c.H[:, k, self.t0:self.t0 + tn], ACT.Copy)\
               .then_inc(self.scalar_done, self.act.mark("H", k))
        if self.gates:
            act.wait_ge(self.vector_done, self.dve.at("H", KC - 1))
        gate_row(0)
        gate_row(1)
        upper("G", 0)
        upper("U", 0)
        silu(0)
        upper("G", 1)

        def step(n, i=None):
            upper("U", n + 1, i)
            silu(n + 1, i)
            upper("D", n, i)
            if i is not None or n + 2 < self.N:
                upper("G", n + 2, i)
                gate_row(n + 2, i)

        with act.Fori(0, self.R) as i:
            step(0, i)
            step(1, i)
        for n in range(2 * self.R, self.N - 1):
            step(n)
        upper("D", self.N - 1)

    def vector(self, dve):
        c, tn = self.c, self.tn
        Ah, Al = c.AS

        def lower(kind, n, i=None, halves=(0, 1)):
            p = self.pos(kind, n)
            for half in halves:
                C = slice(half * SLOT // 2, (half + 1) * SLOT // 2)
                hi, lo = (w[:, C] for w in self.parts(p))
                dve.wait_ge(c.hi_done, self.at(self.L0 + 2 * p + half + 1, i, 12))
                dve.tensor_tensor(lo, c.ring[:, (self.g0 + p) % SLOTS, C], hi.bitcast(F32), ALU.subtract)\
                   .then_inc(c.lo_done, 1)

        def gated(n, i=None):
            q = self.q0 + 2 * self.ops * n

            def product(op, u):
                return self.at(q + 2 * op + u + 1, i, 4 * self.ops)

            for u in range(2):
                dve.wait_ge(c.mm_done, self.at(self.result("U", n) + u + 1, i, 24))
                dve.wait_ge(c.silu_done, self.at(self.s0 + 2 * n + u + 1, i, 4))
                dve.tensor_tensor(c.stat[:, u, 0:tn], c.stat[:, u, 0:tn], c.ps[:, 2 + u, 0:tn], ALU.mult)\
                   .then_inc(c.mul_done, 1)
            if self.gates:
                dve.wait_ge(c.gate_in[n % 2], self.at(16 * (self.r0 + n // 2 + 1), i, 16))
                for u in range(2):
                    dve.wait_ge(c.mul_done, product(0, u))
                    dve.tensor_tensor(c.stat[:, u, 0:tn], c.stat[:, u, 0:tn], c.gate_row[:, n % 2, 0:tn], ALU.mult)\
                       .then_inc(c.mul_done, 1)
            for u in range(2):
                dve.wait_ge(c.mul_done, product(self.ops - 2, u))
                dve.tensor_copy(Ah[:, 2 * (n % 2) + u, 0:tn], c.stat[:, u, 0:tn]).then_inc(c.mul_done, 1)
            for u in range(2):
                dve.wait_ge(c.mul_done, product(self.ops - 1, u))
                hi = Ah[:, 2 * (n % 2) + u, 0:tn].bitcast(F32)
                dve.tensor_tensor(Al[:, 2 * (n % 2) + u, 0:tn], c.stat[:, u, 0:tn], hi, ALU.subtract)\
                   .then_inc(c.gated_done, 1)

        def add(n, js, i=None):
            for j in js:
                dve.wait_ge(c.mm_done, self.at(self.result("D", n) + j + 1, i, 24))
                dve.wait_ge(c.add_done, self.at(self.d0 + 8 * (n - 1) + j + 1, i, 16))
                acc = c.ACC[:, j, self.t0:self.t0 + tn]
                dve.tensor_tensor(acc, acc, c.ps[:, 4 + j % 4, 0:tn], ALU.add).then_inc(c.add_done, 1)

        for k in range(KC):
            dve.wait_ge(self.scalar_done, self.act.at("H", k))
            dve.tensor_tensor(c.HS[1][:, k, 0:tn], c.H[:, k, self.t0:self.t0 + tn], c.HS[0][:, k, 0:tn].bitcast(F32),
                              ALU.subtract).then_inc(self.vector_done, self.dve.mark("H", k))
        lower("G", 0)
        lower("U", 0)
        for j in range(KC):
            dve.memset(c.ACC[:, j, self.t0:self.t0 + tn], 0.0).then_inc(c.add_done, 1)
        lower("G", 1)

        def step(n, i=None):
            lower("U", n + 1, i)
            gated(n, i)
            lower("D", n, i)
            ahead = i is not None or n + 2 < self.N
            add(n, (0, 1), i)
            if ahead:
                lower("G", n + 2, i, halves=(0,))
            add(n, (2, 3), i)
            if ahead:
                lower("G", n + 2, i, halves=(1,))
            add(n, (4, 5, 6, 7), i)

        with dve.Fori(0, self.R) as i:
            step(0, i)
            step(1, i)
        for n in range(2 * self.R, self.N - 1):
            step(n)
        gated(self.N - 1)
        lower("D", self.N - 1)
        add(self.N - 1, range(KC))


class Experts(FeedForward):

    def __init__(self, core, t0, tn, groups, gate, up, down, gates):
        super().__init__(core, t0, tn, groups, gate, up, down, gates)
        self.nt = tn // P
        c, L = core, gates
        self.tok_turned = c.sem(f"tok_turned{L}")
        self.tok_hi = c.sem(f"tok_hi{L}")
        self.gates_summed = c.sem(f"gates_summed{L}")
        self.tok_lo = c.sem(f"tok_lo{L}")
        self.sel_done = c.sem(f"sel_done{L}")
        self.selT_done = c.sem(f"selT_done{L}")
        self.gathered = c.sem(f"gathered{L}")
        self.xe_done = c.sem(f"xe_done{L}")
        self.sparse_silu = c.sem(f"sparse_silu{L}")
        self.sparse_prod = c.sem(f"sparse_prod{L}")
        self.prod_turned = c.sem(f"prod_turned{L}")
        self.ahi_done = c.sem(f"ahi_done{L}")
        self.alo_done = c.sem(f"alo_done{L}")
        self.yehi_done = c.sem(f"yehi_done{L}")
        self.yelo_done = c.sem(f"yelo_done{L}")
        self.scattered = c.sem(f"scattered{L}")
        self.sums_done = c.sem(f"sums_done{L}")
        self.Xe = [a[:, 0:2, :].rearrange("p a (b s) -> p (a b) s", s=P) for a in c.AS]
        self.Ye = [a[:, 2:4, :].rearrange("p a t -> p (a t)") for a in c.AS]
        self.Htok = [h[:].rearrange("p (t a) n -> p t (a n)", t=4) for h in c.HS]
        self.sel = c.SEL[:, 0:4, :]
        self.selT = c.SEL[:, 4:8, :].rearrange("p a t -> p (a t)")
        self.aT = [c.SEL[:, 8:10, :], c.SEL[:, 10:12, :]]

    def moved_by_dense(self):
        c, N = self.c, self.N
        return {"pe": [], "act": [(c.silu_done, 2 * N), (self.scalar_done, KC)],
                "dve": [(self.vector_done, KC), (c.mul_done, 2 * self.ops * N), (c.gated_done, 2 * N), (c.add_done, KC + KC * N)]}

    def either(self, eng, name, dense, gathered):
        flag = eng.value_load(self.c.flag[0:1, 0:1], min_val=0, max_val=1)
        with eng.If(flag):
            dense(eng)
            eng.nop()
        with eng.Else():
            gathered(eng)
            eng.drain()
            for sem, count in self.moved_by_dense()[name]:
                eng.sem_inc(sem, count)
            eng.nop()

    def tensor(self, pe):
        self.either(pe, "pe", super().tensor, self.gathered_tensor)

    def scalar(self, act):
        self.either(act, "act", super().scalar, self.gathered_scalar)

    def vector(self, dve):
        self.either(dve, "dve", super().vector, self.gathered_vector)

    def gathered_tensor(self, pe):
        c, tn, nt = self.c, self.tn, self.nt
        at = self.at
        C = CAPACITY

        def parts(kind, n, i, k):
            p = self.pos(kind, n)
            pe.wait_ge(c.lo_done, at(self.L0 + 2 * (p + 1), i, 12))
            return [w.rearrange("p (k m) -> p k m", k=k) for w in self.parts(p)]

        def up(n, i=None):
            for kind, bank in (("G", 0), ("U", 1)):
                wh, wl = parts(kind, n, i, KC)
                if n > 0:
                    pe.wait_ge(self.sparse_silu if kind == "G" else self.sparse_prod, at(n, i, 2))
                if kind == "G":
                    pe.wait_ge(self.xe_done, at(4 * (n // 2 + 1), i, 4))
                out = c.ps[0:C, bank, 0:WIDE]
                for k in range(KC):
                    xh, xl = (x[:, k, :] for x in self.Xe)
                    pe.matmul(out, xh, wh[:, k, :], start=(k == 0), stop=False)
                    pe.matmul(out, xh, wl[:, k, :], start=False, stop=False)
                    mm = pe.matmul(out, xl, wh[:, k, :], start=False, stop=(k == KC - 1))
                mm.then_inc(c.mm_done, 2)

        def gather(e, i=None):
            pe.wait_ge(self.sel_done, at(nt * (e + 1), i, nt))
            for g in range(4):
                if e > 0 or i is not None:
                    pe.wait_ge(self.sums_done, at(KC + 8 * (e - 2) + 4 + g + 1, i, 8))
                for k in range(4):
                    f = 4 * (g % 2) + k
                    for t in range(nt):
                        mm = pe.matmul(c.ps[:, 4 + g, k * P:(k + 1) * P], self.Htok[g // 2][:, t, f * P:(f + 1) * P],
                                       self.sel[:, t, :], start=(t == 0), stop=(t == nt - 1))
                mm.then_inc(self.gathered, 1)

        def turn(n, i=None):
            pe.wait_ge(self.sparse_prod, at(n + 1, i, 2))
            if n // 2 < EXPERTS - 1:
                pe.wait_ge(self.xe_done, at(4 * (n // 2 + 1) + n % 2 + 1, i, 4))
            else:
                pe.wait_ge(self.sums_done, KC + 8 * (EXPERTS - 2) + 4 + n % 2 + 1)
            for u in range(2):
                tr = pe.transpose(c.ps[:, 4 + n % 2, u * P:(u + 1) * P], c.stat[0:C, n % 2, u * P:(u + 1) * P],
                                  c.s("ident"))
            tr.then_inc(self.prod_turned, 1)

        def down(n, i=None):
            wh, wl = parts("D", n, i, 2)
            pe.wait_ge(self.alo_done, at(n + 1, i, 2))
            for half in range(2):
                out = c.ps[0:C, 2 + half, :]
                F = slice(half * 512, (half + 1) * 512)
                for u in range(2):
                    ah, al = (a[:, u, :] for a in self.aT)
                    pe.matmul(out, ah, wh[:, u, F], start=(n % 2 == 0 and u == 0), stop=False)
                    pe.matmul(out, ah, wl[:, u, F], start=False, stop=False)
                    mm = pe.matmul(out, al, wh[:, u, F], start=False, stop=(n % 2 == 1 and u == 1))
            mm.then_inc(c.mm_done, KC)

        def scatter(e, i=None):
            for j in range(KC):
                if j % 4 == 0:
                    pe.wait_ge(self.yelo_done, at(2 * e + j // 4 + 1, i, 2))
                if j >= 4:
                    pe.wait_ge(self.sums_done, at(KC + 8 * e + j - 3, i, 8))
                out = c.ps[:, 4 + j % 4, 0:tn]
                pe.matmul(out, self.Ye[0][0:C, j * P:(j + 1) * P], self.selT[0:C, 0:tn], start=True, stop=False)
                mm = pe.matmul(out, self.Ye[1][0:C, j * P:(j + 1) * P], self.selT[0:C, 0:tn], start=False, stop=True)
                mm.then_inc(self.scattered, 1)

        for b in range(2 * nt):
            t, half = divmod(b, 2)
            for k in range(4):
                tr = pe.transpose(c.ps[:, b, k * P:(k + 1) * P],
                                  c.H[:, 4 * half + k, self.t0 + t * P:self.t0 + (t + 1) * P], c.s("ident"))
            tr.then_inc(self.tok_turned, 1)
        pe.wait_ge(self.tok_lo, 2 * nt)

        def first(e, i=None, last=False):
            up(2 * e + 1, i)
            if i is not None or e > 0:
                scatter(e - 1, i)
            if not last:
                gather(e + 1, i)
            turn(2 * e, i)
            down(2 * e, i)

        def second(e, i=None):
            up(2 * e + 2, i)
            turn(2 * e + 1, i)
            down(2 * e + 1, i)

        gather(0)
        up(0)
        first(0)
        second(0)
        with pe.Fori(0, EXPERTS - 2) as i:
            first(1, i)
            second(1, i)
        E = EXPERTS - 1
        first(E, last=True)
        turn(2 * E + 1)
        down(2 * E + 1)
        scatter(E)

    def gathered_scalar(self, act):
        c, tn, nt, at = self.c, self.tn, self.nt, self.at
        C = CAPACITY

        def upper(kind, n, i=None):
            p = self.pos(kind, n)
            g = self.g0 + p
            c.arrived(act, g, i)
            if p >= SPLIT_SLOTS:
                act.wait_ge(c.mm_done, at(self.through(p - SPLIT_SLOTS), i, 24))
            for half in range(2):
                W = slice(half * SLOT // 2, (half + 1) * SLOT // 2)
                act.activation(self.parts(p)[0][:, W], c.ring[:, g % SLOTS, W], ACT.Copy).then_inc(c.hi_done, 1)

        def route(e, i=None):
            if i is not None or e >= 1:
                act.wait_ge(self.selT_done, at(e, i, 1))
            number = e if i is None else i + e
            for r in range(2):
                row = c.dram["routes"][bass.ds(number, 1), r, 0:tn].to_broadcast([P, tn])
                act.dma_start(c.route_row[:, r, 0:tn], row).then_inc(c.gate_in[r], 16)

        def silu(n, i=None):
            act.wait_ge(c.mm_done, at(self.through(self.pos("G", n)), i, 24))
            if n > 1:
                act.wait_ge(self.prod_turned, at(n - 1, i, 2))
            act.activation(c.stat[0:C, n % 2, 0:WIDE], c.ps[0:C, 0, 0:WIDE], ACT.Silu).then_inc(self.sparse_silu, 1)

        def tokens(e, i=None):
            for g in range(4):
                act.wait_ge(self.gathered, at(4 * e + g + 1, i, 4))
                x = self.Xe[g // 2][:, 4 * (g % 2):4 * (g % 2) + 4, :]
                act.activation(x, c.ps[:, 4 + g, :].rearrange("p (k s) -> p k s", k=4), ACT.Copy).then_inc(self.xe_done, 1)

        def ahi(n, i=None):
            act.wait_ge(self.prod_turned, at(n + 1, i, 2))
            act.activation(self.aT[0], c.ps[:, 4 + n % 2, 0:WIDE].rearrange("p (k s) -> p k s", k=2), ACT.Copy)\
               .then_inc(self.ahi_done, 1)

        def yehi(e, i=None):
            act.wait_ge(c.mm_done, at(self.through(self.pos("D", 2 * e + 1)), i, 24))
            act.wait_ge(self.selT_done, at(e + 1, i, 1))
            for half in range(2):
                act.activation(self.Ye[0][0:C, half * 512:(half + 1) * 512], c.ps[0:C, 2 + half, :], ACT.Copy,
                               scale=c.slot_gate[0:C, 0:1]).then_inc(self.yehi_done, 1)

        act.wait_ge(c.routes_stored, 16 * self.gates)
        for b in range(2 * nt):
            t, half = divmod(b, 2)
            act.wait_ge(self.tok_turned, b + 1)
            act.activation(self.Htok[0][:, t, half * 512:(half + 1) * 512], c.ps[:, b, :], ACT.Copy).then_inc(self.tok_hi, 1)
        route(0)
        upper("G", 0)
        upper("U", 0)
        tokens(0)
        silu(0)
        upper("G", 1)

        def first(e, i=None, last=False):
            upper("U", 2 * e + 1, i)
            if i is not None or e > 0:
                yehi(e - 1, i)
            silu(2 * e + 1, i)
            upper("D", 2 * e, i)
            if not last:
                tokens(e + 1, i)
            ahi(2 * e, i)
            if not last:
                upper("G", 2 * e + 2, i)

        def second(e, i=None):
            upper("U", 2 * e + 2, i)
            silu(2 * e + 2, i)
            upper("D", 2 * e + 1, i)
            ahi(2 * e + 1, i)
            upper("G", 2 * e + 3, i)
            route(e + 1, i)

        first(0)
        second(0)
        with act.Fori(0, EXPERTS - 2) as i:
            first(1, i)
            second(1, i)
        E = EXPERTS - 1
        first(E, last=True)
        upper("D", 2 * E + 1)
        ahi(2 * E + 1)
        yehi(E)

    def gathered_vector(self, dve):
        c, tn, nt, at = self.c, self.tn, self.nt, self.at
        C = CAPACITY

        def lower(kind, n, i=None):
            p = self.pos(kind, n)
            for half in range(2):
                W = slice(half * SLOT // 2, (half + 1) * SLOT // 2)
                hi, lo = (w[:, W] for w in self.parts(p))
                dve.wait_ge(c.hi_done, at(self.L0 + 2 * p + half + 1, i, 12))
                dve.tensor_tensor(lo, c.ring[:, (self.g0 + p) % SLOTS, W], hi.bitcast(F32), ALU.subtract)\
                   .then_inc(c.lo_done, 1)

        def sel(e, i=None):
            if i is not None or e > 0:
                dve.wait_ge(self.gathered, at(4 * e, i, 4))
            for t in range(nt):
                place = c.place[:, t, e:e + 1] if i is None else c.place[:, t, bass.ds(i + e, 1)]
                dve.tensor_scalar(self.sel[:, t, :], c.s("slots"), place, None, ALU.is_equal)\
                   .then_inc(self.sel_done, 1)

        def selT(e, i=None):
            if i is not None or e > 0:
                dve.wait_ge(self.scattered, at(8 * e, i, 8))
            for r in range(2):
                dve.wait_ge(c.gate_in[r], at(16 * (self.r0 + e + 1), i, 16))
            gates, places = (c.route_row[:, r, 0:tn] for r in range(2))
            dve.tensor_scalar(self.selT[:, 0:tn], places, c.s("slot"), None, ALU.is_equal)
            dve.scalar_tensor_tensor(gates, places, c.s("slot"), gates, ALU.is_equal, ALU.mult)\
               .then_inc(self.gates_summed, 1)
            dve.wait_ge(self.gates_summed, at(e + 1, i, 1))
            dve.reduce_sum(c.slot_gate[:, 0:1], gates, AX_X).then_inc(self.selT_done, 1)

        def product(n, i=None):
            dve.wait_ge(c.mm_done, at(self.through(self.pos("U", n)), i, 24))
            dve.wait_ge(self.sparse_silu, at(n + 1, i, 2))
            act = c.stat[0:C, n % 2, 0:WIDE]
            dve.tensor_tensor(act, act, c.ps[0:C, 1, 0:WIDE], ALU.mult).then_inc(self.sparse_prod, 1)

        def alo(n, i=None):
            dve.wait_ge(self.ahi_done, at(n + 1, i, 2))
            ps = c.ps[:, 4 + n % 2, 0:WIDE].rearrange("p (k s) -> p k s", k=2)
            dve.tensor_tensor(self.aT[1], ps, self.aT[0].bitcast(F32), ALU.subtract).then_inc(self.alo_done, 1)

        def yelo(e, i=None):
            for half in range(2):
                dve.wait_ge(self.yehi_done, at(2 * e + half + 1, i, 2))
                F = slice(half * 512, (half + 1) * 512)
                dve.scalar_tensor_tensor(self.Ye[1][0:C, F], c.ps[0:C, 2 + half, :], c.slot_gate[0:C, 0:1],
                                         self.Ye[0][0:C, F].bitcast(F32), ALU.mult, ALU.subtract)\
                   .then_inc(self.yelo_done, 1)

        def add(e, i=None):
            for j in range(KC):
                dve.wait_ge(self.scattered, at(8 * e + j + 1, i, 8))
                dve.wait_ge(self.sums_done, at(8 * e + j + 1, i, 8))
                acc = c.ACC[:, j, self.t0:self.t0 + tn]
                dve.tensor_tensor(acc, acc, c.ps[:, 4 + j % 4, 0:tn], ALU.add).then_inc(self.sums_done, 1)

        for b in range(2 * nt):
            t, half = divmod(b, 2)
            F = slice(half * 512, (half + 1) * 512)
            dve.wait_ge(self.tok_hi, b + 1)
            dve.tensor_tensor(self.Htok[1][:, t, F], c.ps[:, b, :], self.Htok[0][:, t, F].bitcast(F32), ALU.subtract)\
               .then_inc(self.tok_lo, 1)
        sel(0)
        lower("G", 0)
        lower("U", 0)
        for j in range(KC):
            dve.memset(c.ACC[:, j, self.t0:self.t0 + tn], 0.0).then_inc(self.sums_done, 1)
        lower("G", 1)

        def first(e, i=None, last=False):
            product(2 * e, i)
            lower("U", 2 * e + 1, i)
            if not last:
                sel(e + 1, i)
            if i is not None or e > 0:
                yelo(e - 1, i)
                add(e - 1, i)
            lower("D", 2 * e, i)
            alo(2 * e, i)
            if not last:
                lower("G", 2 * e + 2, i)

        def second(e, i=None):
            product(2 * e + 1, i)
            lower("U", 2 * e + 2, i)
            selT(e, i)
            lower("D", 2 * e + 1, i)
            alo(2 * e + 1, i)
            lower("G", 2 * e + 3, i)

        first(0)
        second(0)
        with dve.Fori(0, EXPERTS - 2) as i:
            first(1, i)
            second(1, i)
        E = EXPERTS - 1
        first(E, last=True)
        product(2 * E + 1)
        selT(E)
        lower("D", 2 * E + 1)
        alo(2 * E + 1)
        yelo(E)
        add(E)


class Lambda(Stage):

    def __init__(self, core, out):
        super().__init__(core)
        self.out = out

    def vector(self, dve):
        c = self.c
        v = c.s("lam").rearrange("p (j d) -> p j d", j=4)
        for j in range(2):
            dve.tensor_tensor(c.stat[:, j, 0:64], v[:, 2 * j, :], v[:, 2 * j + 1, :], ALU.mult).then_inc(self.vector_done, self.dve.mark("prod", j))
            dve.wait_ge(self.vector_done, self.dve.at("prod", j))
            dve.reduce_sum(self.out[:, j:j + 1], c.stat[:, j, 0:64], AX_X).then_inc(self.vector_done, self.dve.mark("sum", j))
        dve.wait_ge(self.scalar_done, self.act.at("exp"))
        dve.tensor_tensor(self.out[:, 2:3], self.out[:, 1:2], self.out[:, 0:1], ALU.subtract).then_inc(self.vector_done, self.dve.mark("d"))
        dve.wait_ge(self.vector_done, self.dve.at("d"))
        dve.tensor_scalar(self.out[:, 3:4], self.out[:, 2:3], -LAM_INIT, None, ALU.add)

    def scalar(self, act):
        c = self.c
        act.wait_ge(self.vector_done, self.dve.at("sum", 1))
        act.activation(self.out[:, 0:2], self.out[:, 0:2], ACT.Exp).then_inc(self.scalar_done, self.act.mark("exp"))


class LogForget(Stage):

    def __init__(self, core, wf, bf, m):
        super().__init__(core)
        self.wf, self.bf, self.m = wf, bf, m

    def tensor(self, pe):
        c, m = self.c, self.m
        for t, (t0, tn) in enumerate(TILES2):
            for k in range(KC):
                mm = pe.matmul(c.ps[0:tn, 0, t * 16:(t + 1) * 16], c.H[:, k, t0:t0 + tn], self.wf[:, k, :],
                               start=(k == 0), stop=(k == KC - 1))
            mm.then_inc(self.tensor_done, self.pe.mark("f", t))
        pe.wait_ge(self.vector_done, self.dve.at("lf", 2))
        for q, (q0, qn) in enumerate(TILES2):
            for s in range(q + 1):
                sn = TILES2[s][1]
                upto = c.s("upto" if s == q else "ones")[0:sn, 0:qn]
                pe.matmul(c.ps[0:qn, 1, q * 16:(q + 1) * 16], upto, m["lf"][0:sn, s, :], start=(s == 0), stop=(s == q))
            for s in range(q + 1):
                sn = TILES2[s][1]
                upto = c.s("upto" if s == q else "ones")[0:sn, 0:qn]
                mm = pe.matmul(c.ps[0:16, 2, q0:q0 + qn], m["lf"][0:sn, s, :], upto, start=(s == 0), stop=(s == q))
            mm.then_inc(self.tensor_done, self.pe.mark("c", q))

    def vector(self, dve):
        c, m = self.c, self.m
        for t, (t0, tn) in enumerate(TILES2):
            z, w = m["z"][0:tn, t, :], m["w"][0:tn, t, :]
            dve.wait_ge(self.tensor_done, self.pe.at("f", 2))
            dve.tensor_tensor(z, c.ps[0:tn, 0, t * 16:(t + 1) * 16], self.bf[0:tn], ALU.add).then_inc(self.vector_done, self.dve.mark("z", t))
            dve.wait_ge(self.vector_done, self.dve.at("z", t))
            dve.scalar_tensor_tensor(w, z, -1.0, z, ALU.mult, ALU.max).then_inc(self.vector_done, self.dve.mark("abs", t))
            dve.wait_ge(self.scalar_done, self.act.at("ln", t))
            dve.scalar_tensor_tensor(m["lf"][0:tn, t, :], z, 0.0, w, ALU.min, ALU.subtract).then_inc(self.vector_done, self.dve.mark("lf", t))

    def scalar(self, act):
        c, m = self.c, self.m
        for t, (t0, tn) in enumerate(TILES2):
            w = m["w"][0:tn, t, :]
            act.wait_ge(self.vector_done, self.dve.at("abs", t))
            act.activation(w, w, ACT.Exp, scale=-1.0).then_inc(self.scalar_done, self.act.mark("e", t))
            act.wait_ge(self.scalar_done, self.act.at("e", t))
            act.activation(w, w, ACT.Ln, bias=1.0).then_inc(self.scalar_done, self.act.mark("ln", t))
        act.wait_ge(self.tensor_done, self.pe.at("c", 2))
        for q, (q0, qn) in enumerate(TILES2):
            act.activation(m["C"][0:qn, q, :], c.ps[0:qn, 1, q * 16:(q + 1) * 16], ACT.Copy)
            act.activation(m["CT"][0:16, q0:q0 + qn], c.ps[0:16, 2, q0:q0 + qn], ACT.Copy, scale=-1.0)


class Multiply(Stage):

    def __init__(self, core, out, factor):
        super().__init__(core)
        self.out, self.factor = out, factor

    def vector(self, dve):
        for k in range(KC):
            dve.tensor_tensor(self.out[:, k, 0:T2], self.out[:, k, 0:T2], self.factor[:, k, 0:T2], ALU.mult)


class Store(Stage):

    def vector(self, dve):
        c = self.c
        for k in range(KC):
            dve.tensor_tensor(c.X[:, k, 0:T2], c.X[:, k, 0:T2], c.ACC[:, k, 0:T2], ALU.add).then_inc(self.vector_done, self.dve.mark("x", k))

    def sync(self, sp):
        c = self.c
        for k in range(KC):
            sp.wait_ge(self.vector_done, self.dve.at("x", k))
            sp.dma_start(c.dram["outT"][k * P:(k + 1) * P, :], c.X[:, k, META:T2]).then_inc(c.stored, 16)
        sp.wait_ge(c.stored, 16 * KC)


class GlaGates(Stage):

    def __init__(self, core, m):
        super().__init__(core)
        self.m = m

    def tensor(self, pe):
        c, m = self.c, self.m
        wa = c.s("gla_wa").rearrange("p (k e) -> p k e", k=KC)
        for k in range(KC):
            mm = pe.matmul(c.ps[0:16, 0, 0:T2], wa[:, k, :], c.H[:, k, 0:T2], start=(k == 0), stop=(k == KC - 1))
        mm.then_inc(self.tensor_done, self.pe.mark("lr"))
        pe.wait_ge(self.scalar_done, self.act.at("lr"))
        for h in range(4):
            mm = pe.matmul(c.ps[:, 1 + h, 0:T2], c.s("gla_w2", 16)[:, h * P:(h + 1) * P], m["lr"][0:16, :],
                           start=True, stop=True)
            mm.then_inc(self.tensor_done, self.pe.mark("z", h))

    def scalar(self, act):
        c, m = self.c, self.m
        act.wait_ge(self.tensor_done, self.pe.at("lr"))
        act.activation(m["lr"][0:16, :], c.ps[0:16, 0, 0:T2], ACT.Copy).then_inc(self.scalar_done, self.act.mark("lr"))
        for h in range(4):
            act.wait_ge(self.tensor_done, self.pe.at("z", h))
            act.activation(m["b"][:, h, :], c.ps[:, 1 + h, 0:T2], ACT.Identity,
                                      bias=c.s("gla_ba")[:, h:h + 1]).then_inc(self.scalar_done, self.act.mark("z", h))
        act.wait_ge(self.vector_done, self.dve.at("abs"))
        act.activation(m["e"], m["e"], ACT.Exp, scale=-1.0).then_inc(self.scalar_done, self.act.mark("e"))
        act.wait_ge(self.scalar_done, self.act.at("e"))
        act.activation(m["e"], m["e"], ACT.Ln, bias=1.0).then_inc(self.scalar_done, self.act.mark("ln"))

    def vector(self, dve):
        c, m = self.c, self.m
        dve.wait_ge(self.scalar_done, self.act.at("z", 3))
        dve.scalar_tensor_tensor(m["e"], m["b"], -1.0, m["b"], ALU.mult, ALU.max).then_inc(self.vector_done, self.dve.mark("abs"))
        dve.memset(m["one"], 1.0).then_inc(self.vector_done, self.dve.mark("one"))
        dve.wait_ge(self.scalar_done, self.act.at("ln"))
        dve.scalar_tensor_tensor(m["g"], m["b"], 0.0, m["e"], ALU.min, ALU.subtract).then_inc(self.vector_done, self.dve.mark("g"))
        dve.wait_ge(self.vector_done, self.dve.at("g"))
        for h in range(4):
            for t0, tn in TILES2:
                dve.tensor_tensor_scan(m["b"][:, h, t0:t0 + tn], m["one"][:, 0:tn], m["g"][:, h, t0:t0 + tn],
                                       0.0, ALU.mult, ALU.add)


class GlaScores(Stage):

    def __init__(self, core, m):
        super().__init__(core)
        self.m = m

    def view(self, x, l):
        if l <= 3:
            return x.rearrange("p h t -> p (h t)").rearrange("p (n w) -> p n w", w=2 << l)
        return x[:, :, META:].rearrange("p h (n w) -> p h n w", w=2 << l)

    def units(self, l):
        for h in range(4):
            for t, (t0, tn) in enumerate(TILES2):
                if tn > (1 << max(l, 0)):
                    yield h, t, t0, tn

    def out(self, l, h, t, tn):
        if t == 0:
            return self.c.ps[0:tn, 6 + l % 2, h * META:h * META + tn]
        return self.c.ps[0:tn, 3 * (l % 2) + t - 1, h * P:h * P + tn]

    def tensor(self, pe):
        c, m = self.c, self.m
        for l in range(-1, LEVELS):
            if l >= 0:
                pe.wait_ge(self.vector_done, self.dve.at("scaled", l))
            if l >= 1:
                pe.wait_ge(self.vector_done, self.dve.at("kept", l - 2))
            q, k = (m["Q"], m["K"]) if l < 0 else (m["q"][l % 2], m["k"][l % 2])
            for h, t, t0, tn in self.units(l):
                mm = pe.matmul(self.out(l, h, t, tn), k[:, h, t0:t0 + tn], q[:, h, t0:t0 + tn], start=True, stop=True)
            mm.then_inc(self.tensor_done, self.pe.mark("pairs", l))

    def scalar(self, act):
        c, m = self.c, self.m
        for l in range(LEVELS):
            d = self.view(m["e"], l)
            act.wait_ge(self.vector_done, self.dve.at("diff", l))
            act.activation(m["e"], m["e"], ACT.Exp, scale=-1.0 / 16.0).then_inc(self.scalar_done, self.act.mark("decay", l))

    def vector(self, dve):
        c, m = self.c, self.m
        dve.memset(m["A"], 0.0)
        dve.memset(m["e"], 0.0).then_inc(self.vector_done, self.dve.mark("zero"))

        def keep(l):
            dve.wait_ge(self.tensor_done, self.pe.at("pairs", l))
            mask = c.s("ident") if l < 0 else c.s("levels").rearrange("p (l t) -> p l t", l=LEVELS)[:, l, :]
            mask = mask.bitcast(U32)
            for t in (1, 2):
                ins = dve.copy_predicated(m["A"][:, t - 1, :, :], mask.unsqueeze(1).to_broadcast([P, 4, P]),
                                          c.ps[:, 3 * (l % 2) + t - 1, :].rearrange("p (h t) -> p h t", h=4))
            if l <= 3:
                ins = dve.copy_predicated(m["A0"][0:META, :, :],
                                          mask[0:META, 0:META].unsqueeze(1).to_broadcast([META, 4, META]),
                                          c.ps[0:META, 6 + l % 2, 0:64].rearrange("p (h t) -> p h t", h=4))
            ins.then_inc(self.vector_done, self.dve.mark("kept", l))

        dve.memset(m["A0"], 0.0).then_inc(self.vector_done, self.dve.mark("zero0"))
        dve.wait_ge(self.vector_done, self.dve.at("zero0"))
        for l in range(LEVELS):
            half = 1 << l
            b, e = self.view(m["b"], l), self.view(m["e"], l)
            if l >= 1:
                dve.wait_ge(self.vector_done, self.dve.at("scaled", l - 1))
            if l <= 3:
                n = b.shape[1]
                ins = dve.tensor_tensor(e, b, b[:, :, half - 1:half].to_broadcast([P, n, 2 * half]), ALU.subtract)
            else:
                n = b.shape[2]
                for h in range(4):
                    ins = dve.tensor_tensor(e[:, h], b[:, h],
                                            b[:, h, :, half - 1:half].to_broadcast([P, n, 2 * half]), ALU.subtract)
            ins.then_inc(self.vector_done, self.dve.mark("raw", l))
            dve.wait_ge(self.vector_done, self.dve.at("raw", l))
            dve.scalar_tensor_tensor(m["e"], m["e"], -1.0, m["e"], ALU.mult, ALU.max).then_inc(self.vector_done, self.dve.mark("diff", l))
            keep(l - 1)
            dve.wait_ge(self.scalar_done, self.act.at("decay", l))
            dve.tensor_tensor(m["q"][l % 2], m["Q"], m["e"], ALU.mult)
            dve.tensor_tensor(m["k"][l % 2], m["K"], m["e"], ALU.mult).then_inc(self.vector_done, self.dve.mark("scaled", l))
            dve.wait_ge(self.vector_done, self.dve.at("kept", l - 1))
        keep(LEVELS - 1)


class GlaOutput(Stage):

    def __init__(self, core, m):
        super().__init__(core)
        self.m = m

    def vector(self, dve):
        c, m = self.c, self.m
        for t, (t0, tn) in enumerate(TILES2):
            b = m["b"][:, :, t0:t0 + tn]
            dve.tensor_tensor(m["e"][:, :, t0:t0 + tn], b[:, :, tn - 1:tn].to_broadcast([P, 4, tn]), b, ALU.subtract)
        dve.tensor_copy(m["last"], m["b"][:, :, T2 - 1]).then_inc(self.vector_done, self.dve.mark("rest"))
        for h in range(4):
            dve.wait_ge(self.scalar_done, self.act.at("inter", h))
            dve.tensor_tensor(m["q"][0][:, h, :], m["Q"][:, h, :], m["q"][1][:, h, :], ALU.mult)
            dve.tensor_tensor(m["k"][0][:, h, :], m["K"][:, h, :], m["e"][:, h, :], ALU.mult).then_inc(self.vector_done, self.dve.mark("scaled", h))
        for t in range(2):
            for h in range(4):
                dve.wait_ge(self.tensor_done, self.pe.at("kv", t, h))
                S = m["S"][:, h, :]
                if t == 0:
                    ins = dve.tensor_copy(S, c.ps[:, 4 + h % 2, 0:256])
                else:
                    dve.wait_ge(self.scalar_done, self.act.at("eb"))
                    dve.wait_ge(self.tensor_done, self.pe.at("o", t, 2 * h + 1))
                    ins = dve.scalar_tensor_tensor(S, S, m["ebl"][:, h:h + 1], c.ps[:, 4 + h % 2, 0:256],
                                                   ALU.mult, ALU.add)
                ins.then_inc(self.vector_done, self.dve.mark("state", t, h))

    def scalar(self, act):
        c, m = self.c, self.m
        act.activation(m["ebl"], m["b"][:, :, META + P - 1], ACT.Exp, scale=1.0 / 16.0).then_inc(self.scalar_done, self.act.mark("eb"))
        act.wait_ge(self.vector_done, self.dve.at("rest"))
        for h in range(4):
            act.activation(m["q"][1][:, h, :], m["b"][:, h, :], ACT.Exp, scale=1.0 / 16.0)
            act.activation(m["e"][:, h, :], m["e"][:, h, :], ACT.Exp, scale=1.0 / 16.0).then_inc(self.scalar_done, self.act.mark("inter", h))
        for t, (t0, tn) in enumerate(TILES2):
            if t < 2:
                for h in range(4):
                    act.wait_ge(self.tensor_done, self.pe.at("turned", t, h))
                    act.activation(m["kT"][0:tn, h, :], c.ps[0:tn, 2 + h % 2, 0:P], ACT.Copy).then_inc(self.scalar_done, self.act.mark("turned", t, h))
            for u in range(8):
                act.wait_ge(self.tensor_done, self.pe.at("o", t, u))
                act.activation(m["OT"][:, u, t0:t0 + tn], c.ps[:, u % 2, 0:tn], ACT.Copy).then_inc(self.scalar_done, self.act.mark("o", t, u))

    def tensor(self, pe):
        c, m = self.c, self.m
        for t, (t0, tn) in enumerate(TILES2):
            if t < 2:
                for h in range(4):
                    if t == 0:
                        pe.wait_ge(self.vector_done, self.dve.at("scaled", h))
                    if 4 * t + h >= 2:
                        pt, ph = divmod(4 * t + h - 2, 4)
                        pe.wait_ge(self.scalar_done, self.act.at("turned", pt, ph))
                    tr = pe.transpose(c.ps[0:tn, 2 + h % 2, 0:P], m["k"][0][:, h, t0:t0 + tn], c.s("ident"))
                    tr.then_inc(self.tensor_done, self.pe.mark("turned", t, h))
            for u in range(8):
                h, half = divmod(u, 2)
                if 8 * t + u >= 2:
                    pt, pu = divmod(8 * t + u - 2, 8)
                    pe.wait_ge(self.scalar_done, self.act.at("o", pt, pu))
                A = m["A0"][0:tn, h, :] if t == 0 else m["A"][0:tn, t - 1, h, :]
                cols = slice(h * 256 + half * P, h * 256 + half * P + P)
                if t > 0:
                    pe.wait_ge(self.vector_done, self.dve.at("state", t - 1, h))
                mm = pe.matmul(c.ps[:, u % 2, 0:tn], m["V"][0:tn, t, cols], A, start=True, stop=(t == 0))
                if t > 0:
                    mm = pe.matmul(c.ps[:, u % 2, 0:tn], m["S"][:, h, half * P:(half + 1) * P],
                                   m["q"][0][:, h, t0:t0 + tn], start=False, stop=True)
                mm.then_inc(self.tensor_done, self.pe.mark("o", t, u))
            if t < 2:
                for h in range(4):
                    if 4 * t + h >= 2:
                        pt, ph = divmod(4 * t + h - 2, 4)
                        pe.wait_ge(self.vector_done, self.dve.at("state", pt, ph))
                    pe.wait_ge(self.scalar_done, self.act.at("turned", t, h))
                    mm = pe.matmul(c.ps[:, 4 + h % 2, 0:256], m["kT"][0:tn, h, :], m["V"][0:tn, t, h * 256:(h + 1) * 256],
                                   start=True, stop=True)
                    mm.then_inc(self.tensor_done, self.pe.mark("kv", t, h))


class Convolve(Stage):

    def __init__(self, core, pre, tmp):
        super().__init__(core)
        self.pre, self.tmp = pre, tmp

    def vector(self, dve):
        c = self.c
        w = c.s("gdn_conv").rearrange("p (j k) -> p j k", j=4)
        N = 24
        for i in range(0, N, 2):
            if i >= 4:
                dve.wait_ge(self.scalar_done, self.act.at(i - 3))
            for j in range(4):
                for u in (i, i + 1):
                    x, t = self.pre[:, u, j:j + T2], self.tmp[:, u % 4, :]
                    if j > 0:
                        dve.wait_ge(self.vector_done, self.dve.at("tap", u, j - 1))
                        ins = dve.scalar_tensor_tensor(t, x, w[:, j, u:u + 1], t, ALU.mult, ALU.add)
                    else:
                        ins = dve.tensor_scalar(t, x, w[:, j, u:u + 1], None, ALU.mult)
                    ins.then_inc(self.vector_done, self.dve.mark("tap", u, j))

    def scalar(self, act):
        c = self.c
        for i in range(24):
            act.wait_ge(self.vector_done, self.dve.at("tap", i, 3))
            act.activation(self.pre[:, i, 3:3 + T2], self.tmp[:, i % 4, :], ACT.Silu).then_inc(self.scalar_done, self.act.mark(i))


class GdnGates(Stage):

    def __init__(self, core, m):
        super().__init__(core)
        self.m = m

    def tensor(self, pe):
        c, m = self.c, self.m
        w = c.s("gdn_wab").rearrange("p (k e) -> p k e", k=KC)
        for t, (t0, tn) in enumerate(TILES2):
            for k in range(KC):
                mm = pe.matmul(c.ps[0:tn, 0, t * 16:(t + 1) * 16], c.H[:, k, t0:t0 + tn], w[:, k, :],
                               start=(k == 0), stop=(k == KC - 1))
            mm.then_inc(self.tensor_done, self.pe.mark("ab", t))
        pe.wait_ge(self.vector_done, self.dve.at("g", 2))
        for t, (t0, tn) in enumerate(TILES2):
            pe.matmul(c.ps[0:tn, 1, t * 8:(t + 1) * 8], c.s("upto")[0:tn, 0:tn], m["g"][0:tn, t, :],
                      start=True, stop=True)
            pe.matmul(c.ps[0:8, 2, t0:t0 + tn], m["g"][0:tn, t, :], c.s("upto")[0:tn, 0:tn], start=True, stop=True)
            mm = pe.matmul(c.ps[0:8, 3, t0:t0 + tn], m["beta"][0:tn, t, :], c.s("ident")[0:tn, 0:tn],
                           start=True, stop=True)
        mm.then_inc(self.tensor_done, self.pe.mark("b"))
        pe.wait_ge(self.scalar_done, self.act.at("rows"))
        for h in range(8):
            if h >= 2:
                pe.wait_ge(self.scalar_done, self.act.at("eb", h - 2))
                pe.wait_ge(self.vector_done, self.dve.at("kb", h - 2))
            row = c.s("ident", 8)[:, h:h + 1].to_broadcast([8, P])
            pe.matmul(c.ps[:, 4 + h % 2, 0:T2], row, m["bT"][0:8, :], start=True, stop=True)
            pe.matmul(c.ps[:, 6 + h % 2, 0:T2], row, m["betaT"][0:8, :], start=True, stop=True).then_inc(self.tensor_done, self.pe.mark("bc", h))

    def vector(self, dve):
        c, m = self.c, self.m
        dve.wait_ge(self.scalar_done, self.act.at("alog"))
        for t, (t0, tn) in enumerate(TILES2):
            a, w = m["a"][0:tn, t, :], m["w"][0:tn, t, :]
            dve.wait_ge(self.tensor_done, self.pe.at("ab", 2))
            dve.tensor_tensor(a, c.ps[0:tn, 0, t * 16:t * 16 + 8], c.s("gdn_dt", tn), ALU.add).then_inc(self.vector_done, self.dve.mark("a", t))
            dve.wait_ge(self.vector_done, self.dve.at("a", t))
            dve.scalar_tensor_tensor(w, a, -1.0, a, ALU.mult, ALU.max).then_inc(self.vector_done, self.dve.mark("abs", t))
            dve.wait_ge(self.scalar_done, self.act.at("ln", t))
            dve.scalar_tensor_tensor(a, a, 0.0, w, ALU.max, ALU.add).then_inc(self.vector_done, self.dve.mark("sp", t))
            dve.wait_ge(self.vector_done, self.dve.at("sp", t))
            dve.scalar_tensor_tensor(m["g"][0:tn, t, :], a, -1.0, m["alog"][0:tn, :], ALU.mult, ALU.mult).then_inc(self.vector_done, self.dve.mark("g", t))
        for h in range(8):
            dve.wait_ge(self.tensor_done, self.pe.at("bc", h))
            dve.wait_ge(self.scalar_done, self.act.at("eb", h))
            dve.tensor_tensor(m["KB"][:, h, :], m["K"][:, h, 3:3 + T2], c.ps[:, 6 + h % 2, 0:T2], ALU.mult).then_inc(self.vector_done, self.dve.mark("kb", h))
            dve.tensor_tensor(m["QE"][:, h, :], m["Q"][:, h, 3:3 + T2], m["EB"][:, h, :], ALU.mult)
            dve.wait_ge(self.vector_done, self.dve.at("kb", h))
            dve.tensor_tensor(m["KBE"][:, h, :], m["KB"][:, h, :], m["EB"][:, h, :], ALU.mult)

    def scalar(self, act):
        c, m = self.c, self.m
        for t, (t0, tn) in enumerate(TILES2):
            act.wait_ge(self.tensor_done, self.pe.at("ab", 2))
            ins = act.activation(m["beta"][0:tn, t, :], c.ps[0:tn, 0, t * 16 + 8:t * 16 + 16], ACT.Sigmoid)
        act.activation(m["alog"], c.s("gdn_alog"), ACT.Exp).then_inc(self.scalar_done, self.act.mark("alog"))
        for t, (t0, tn) in enumerate(TILES2):
            w = m["w"][0:tn, t, :]
            act.wait_ge(self.vector_done, self.dve.at("abs", t))
            act.activation(w, w, ACT.Exp, scale=-1.0).then_inc(self.scalar_done, self.act.mark("e", t))
            act.wait_ge(self.scalar_done, self.act.at("e", t))
            act.activation(w, w, ACT.Ln, bias=1.0).then_inc(self.scalar_done, self.act.mark("ln", t))
        act.wait_ge(self.tensor_done, self.pe.at("b"))
        for t, (t0, tn) in enumerate(TILES2):
            act.activation(m["b"][0:tn, t, :], c.ps[0:tn, 1, t * 8:(t + 1) * 8], ACT.Copy)
        act.activation(m["bT"][0:8, :], c.ps[0:8, 2, 0:T2], ACT.Copy)
        act.activation(m["betaT"][0:8, :], c.ps[0:8, 3, 0:T2], ACT.Copy).then_inc(self.scalar_done, self.act.mark("rows"))
        for h in range(8):
            act.wait_ge(self.tensor_done, self.pe.at("bc", h))
            act.activation(m["BB"][:, h, :], c.ps[:, 4 + h % 2, 0:T2], ACT.Copy)
            act.activation(m["EB"][:, h, :], c.ps[:, 4 + h % 2, 0:T2], ACT.Exp).then_inc(self.scalar_done, self.act.mark("eb", h))


class GdnChunk(Stage):

    def __init__(self, core, m, t):
        super().__init__(core)
        self.m, self.t = m, t
        self.t0, self.tn = TILES2[t]
        self.levels = (self.tn - 1).bit_length()

    def psv(self, bank, n=None):
        return self.c.ps[0:self.tn, bank:bank + 2, :].rearrange("p a (h t) -> p (a h) t", h=4)[:, :, 0:n or self.tn]

    def head(self, bank, h, n=None):
        return self.c.ps[0:self.tn, bank + h // 4, (h % 4) * P:(h % 4) * P + (n or self.tn)]

    def tensor(self, pe):
        c, m, t0, n = self.c, self.m, self.t0, self.tn
        T, T3 = slice(t0, t0 + n), slice(3 + t0, 3 + t0 + n)
        for h in range(8):
            pe.matmul(self.head(0, h), m["K"][:, h, T3], m["KB"][:, h, T], start=True, stop=True)
            mm = pe.matmul(self.head(2, h), m["K"][:, h, T3], m["Q"][:, h, T3], start=True, stop=True)
        mm.then_inc(self.tensor_done, self.pe.mark("kk"))
        for h in range(8):
            pe.transpose(self.head(4, h, P), m["K"][:, h, T3], c.s("ident"))
            mm = pe.transpose(self.head(6, h, P), m["V"][:, h, T3], c.s("ident"))
        mm.then_inc(self.tensor_done, self.pe.mark("turned"))
        for l in range(self.levels):
            pe.wait_ge(self.vector_done, self.dve.at("part", l))
            if l == 0:
                pe.wait_ge(self.scalar_done, self.act.at("vb"))
            else:
                pe.wait_ge(self.vector_done, self.dve.at("X", l - 1))
            for h in range(8):
                mm = pe.matmul(self.head(0, h), m["BT"][0:n, l % 2, h, 0:n], m["Xm"][0:n, h, 0:n], start=True, stop=True)
            mm.then_inc(self.tensor_done, self.pe.mark("BX", l))
            pe.wait_ge(self.scalar_done, self.act.at("BX", l))
            for h in range(8):
                pe.matmul(self.head(2, h), m["XT"][0:n, h, 0:n], m["U"][0:n, h, 0:n], start=True, stop=True)
                mm = pe.matmul(self.head(4, h), m["U"][0:n, h, 0:n], m["XT"][0:n, h, 0:n], start=True, stop=True)
            mm.then_inc(self.tensor_done, self.pe.mark("XBX", l))
        pe.wait_ge(self.vector_done, self.dve.at("X", self.levels - 1))
        for h in range(8):
            mm = pe.matmul(self.head(0, h, P), m["KBE"][:, h, T], m["S"][:, h, :], start=True, stop=True)
        mm.then_inc(self.tensor_done, self.pe.mark("kS"))
        pe.wait_ge(self.vector_done, self.dve.at("r"))
        for h in range(8):
            mm = pe.matmul(self.head(2, h, P), m["XT"][0:n, h, 0:n], m["U"][0:n, h, :], start=True, stop=True)
        mm.then_inc(self.tensor_done, self.pe.mark("vnew"))
        pe.wait_ge(self.scalar_done, self.act.at("vnew"))
        for h in range(8):
            o = c.ps[:, 4 + h // 4, (h % 4) * P:(h % 4) * P + n]
            pe.matmul(o, m["VN"][0:n, h, :], m["AT"][0:n, h, 0:n], start=True, stop=False)
            mm = pe.matmul(o, m["S"][:, h, :], m["QE"][:, h, T], start=False, stop=True)
        mm.then_inc(self.tensor_done, self.pe.mark("o"))
        for h in range(8):
            mm = pe.matmul(c.ps[:, 6 + h // 4, (h % 4) * P:(h % 4 + 1) * P], m["KD"][0:n, h, :], m["VN"][0:n, h, :],
                           start=True, stop=True)
        mm.then_inc(self.tensor_done, self.pe.mark("kv"))

    def vector(self, dve):
        c, m, t0, n = self.c, self.m, self.t0, self.tn
        T = slice(t0, t0 + n)
        if self.t == 0:
            dve.memset(m["S"], 0.0)
        dve.tensor_tensor(m["bl"][0:n, :], m["BB"][0:n, :, t0 + n - 1], m["b"][0:n, self.t, :], ALU.subtract).then_inc(self.vector_done, self.dve.mark("bl"))
        for h in range(8):
            dve.tensor_scalar(m["U"][0:n, h, 0:n], m["BB"][0:n, h, T], m["b"][0:n, self.t, h:h + 1], 0.0,
                                         ALU.subtract, ALU.min).then_inc(self.vector_done, self.dve.mark("diff", h))
        ident = c.s("ident")[0:n, 0:n].unsqueeze(1).to_broadcast([n, 8, n])
        dve.tensor_copy(m["Xm"][0:n, :, 0:n], ident)
        dve.tensor_copy(m["XT"][0:n, :, 0:n], ident)
        dve.wait_ge(self.scalar_done, self.act.at("decay"))
        dve.wait_ge(self.tensor_done, self.pe.at("kk"))
        LT, AT, U = m["LT"][0:n, :, 0:n], m["AT"][0:n, :, 0:n], m["U"][0:n, :, 0:n]
        dve.tensor_tensor(LT, self.psv(0), U, ALU.mult).then_inc(self.vector_done, self.dve.mark("LT"))
        dve.tensor_tensor(AT, self.psv(2), U, ALU.mult).then_inc(self.vector_done, self.dve.mark("AT0"))
        dve.wait_ge(self.vector_done, self.dve.at("AT0"))
        dve.tensor_tensor(AT, AT, c.s("upto")[0:n, 0:n].unsqueeze(1).to_broadcast([n, 8, n]), ALU.mult)\
           .then_inc(self.vector_done, self.dve.mark("AT"))
        levels = c.s("levels").rearrange("p (l t) -> p l t", l=LEVELS)

        def part(l):
            mask = levels[0:n, l, 0:n].unsqueeze(1).to_broadcast([n, 8, n])
            dve.tensor_tensor(m["BT"][0:n, l % 2, :, 0:n], LT, mask, ALU.mult).then_inc(self.vector_done, self.dve.mark("part", l))

        part(0)
        for l in range(self.levels):
            if l + 1 < self.levels:
                part(l + 1)
            dve.wait_ge(self.tensor_done, self.pe.at("XBX", l))
            X, XT = m["Xm"][0:n, :, 0:n], m["XT"][0:n, :, 0:n]
            if l > 0:
                dve.wait_ge(self.vector_done, self.dve.at("X", l - 1))
            dve.tensor_tensor(X, X, self.psv(2), ALU.subtract)
            dve.tensor_tensor(XT, XT, self.psv(4), ALU.subtract).then_inc(self.vector_done, self.dve.mark("X", l))
        dve.wait_ge(self.tensor_done, self.pe.at("kS"))
        dve.wait_ge(self.scalar_done, self.act.at("vb"))
        dve.tensor_tensor(m["U"][0:n, :, :], m["VB"][0:n, :, :], self.psv(0, P), ALU.subtract).then_inc(self.vector_done, self.dve.mark("r"))
        if self.t < 2:
            dve.wait_ge(self.tensor_done, self.pe.at("kv"))
            kv = c.ps[:, 6:8, :].rearrange("p a (h t) -> p (a h) t", h=4)
            for h in range(8):
                dve.scalar_tensor_tensor(m["S"][:, h, :], m["S"][:, h, :], m["EB"][:, h, t0 + n - 1:t0 + n],
                                         kv[:, h, :], ALU.mult, ALU.add)

    def scalar(self, act):
        c, m, t0, n = self.c, self.m, self.t0, self.tn
        U = m["U"][0:n, :, 0:n]
        act.wait_ge(self.vector_done, self.dve.at("bl"))
        act.activation(m["bl"][0:n, :], m["bl"][0:n, :], ACT.Exp).then_inc(self.scalar_done, self.act.mark("bl"))
        act.wait_ge(self.vector_done, self.dve.at("diff", 7))
        act.activation(U, U, ACT.Exp).then_inc(self.scalar_done, self.act.mark("decay"))
        act.wait_ge(self.tensor_done, self.pe.at("turned"))
        act.wait_ge(self.scalar_done, self.act.at("bl"))
        for h in range(8):
            act.activation(m["KD"][0:n, h, :], self.head(4, h, P), ACT.Copy, scale=m["bl"][0:n, h:h + 1])
            ins = act.activation(m["VB"][0:n, h, :], self.head(6, h, P), ACT.Copy, scale=m["beta"][0:n, self.t, h:h + 1])
        ins.then_inc(self.scalar_done, self.act.mark("vb"))
        for l in range(self.levels):
            act.wait_ge(self.tensor_done, self.pe.at("BX", l))
            if l == 0:
                act.wait_ge(self.vector_done, self.dve.at("AT0"))
            else:
                act.wait_ge(self.tensor_done, self.pe.at("XBX", l - 1))
            act.activation(U, self.psv(0), ACT.Copy).then_inc(self.scalar_done, self.act.mark("BX", l))
        act.wait_ge(self.tensor_done, self.pe.at("vnew"))
        act.activation(m["VN"][0:n, :, :], self.psv(2, P), ACT.Copy).then_inc(self.scalar_done, self.act.mark("vnew"))
        act.wait_ge(self.tensor_done, self.pe.at("o"))
        o = c.ps[:, 4:6, :].rearrange("p a (h t) -> p (a h) t", h=4)[:, :, 0:n]
        act.activation(m["OT"][:, :, t0:t0 + n], o, ACT.Copy)


class Zero(Stage):

    def __init__(self, core, dst):
        super().__init__(core)
        self.dst = dst

    def vector(self, dve):
        dve.memset(self.dst, 0.0)


def first_stack(c):
    d = c.dram
    yield Modulation(c, c.carve({"rows": (2 * 6 * D,)})["rows"])

    m = c.carve({"QK": (13, 512), "KD": (2, 512), "V": (4, 640), "OT": (8, 512), "p": (4, 512), "s": (4, 512),
                 "pT": (2, 512), "col": (4, 8), "lam": (4,)})
    QK, KD, V, OT = m["QK"], m["KD"], m["V"], m["OT"]
    w = d["w_in_even"]
    items = feature_items(QK, [0, 1], 0, T1)
    items.append((2, "feature", 0, P, 0, T1, move_to(QK[:, 4, :])))
    items += token_items(V, [2], TILES1, lo=P, n=P, at=0)
    items += feature_items(QK, [3, 4, 5, 6], 0, T1, first=5)
    items += token_items(V, [7, 8], TILES1, at=P)
    yield Project(c, c.H, [columns(w, s * WIDE) for s in range(9)], items, [chunks_of(c.ACC_part), chunks_of(c.H_part)])
    yield Lambda(c, m["lam"])
    yield Rope(c, [QK[:, j, CTX:T1] for j in range(13)], 64, m["s"],
               copies=[(KD[o * 64:(o + 1) * 64, g, :], QK[g * 64:(g + 1) * 64, 4, :]) for g in range(2) for o in range(2)])
    window = c.s("window").rearrange("p (q k) -> p q k", q=2)
    items = []
    for h in range(8):
        r, g = 64 * (h % 2), h // 4
        R = slice(r, r + 64)
        for t, (t0, tn) in enumerate(TILES1):
            keys = CTX if t < 2 else T1
            items.append(dict(
                rows=tn, keys=keys, maps=[[(QK[R, h // 2, t0:t0 + tn], KD[R, g, 0:keys])]], scale=64 ** -0.5,
                masks=[[], [], [(window[:, 0, :], 384, 512)], [(window[:, 1, :], 256, 384)]][t], sink=c.s("sink")[:, h:h + 1],
                values=[(b * P, P, V[:, b, g * 64:(g + 1) * 64]) for b in range(keys // P)],
                out_rows=(r, 64), out=OT[R, h // 2, t0:t0 + tn]))
    for h in range(4):
        for t, (t0, tn) in enumerate(TILES1):
            keys = CTX if t < 2 else T1
            items.append(dict(
                rows=tn, keys=keys, scale=64 ** -0.5, lam=m["lam"][:, 3:4],
                maps=[[(QK[64 * j:64 * j + 64, 5 + h, t0:t0 + tn], QK[64 * j:64 * j + 64, 9 + h, 0:keys])] for j in range(2)],
                values=[(b * P, P, V[:, b, P + h * P:P + (h + 1) * P]) for b in range(keys // P)],
                out_rows=(0, P), out=OT[:, 4 + h, t0:t0 + tn]))
    yield Attention(c, items, m["p"], m["s"], m["pT"], m["col"])
    yield HeadNorm(c, [([OT[:, 4 + h, :]], T1, c.s("ones"), P, [c.s("subln_g")], None) for h in range(4)],
                   SUBLN_EPS, m["s"], m["p"], after=1.0 - LAM_INIT)
    yield Project(c, OT, [columns(d["w_out_even"], s * WIDE) for s in range(4)], feature_items(c.ACC, range(4), 0, T1),
                  m["OT_parts"])
    yield LayerNorm(c, 0, 0, [(0, 0), (1, CTX)], (0, 3))
    yield from experts(c, 0, 0, T1)
    yield LayerNorm(c, 0, 1, [(0, 0), (1, CTX)], (1, 0))

    m = c.carve({"Q": (8, 512), "K": (2, 512), "V": (4, 256), "OT": (8, 512), "p": (4, 512), "s": (4, 512),
                 "pT": (2, 512), "col": (4, 8)})
    Q, K, V, OT = m["Q"], m["K"], m["V"], m["OT"]
    w = d["w_in_odd"]
    yield Project(c, c.H, [columns(w, s * WIDE) for s in range(6)],
                  feature_items(Q, range(4), CTX, SEQ) + feature_items(K, [4], 0, T1) + token_items(V, [5], TILES1),
                  [chunks_of(c.ACC_part), chunks_of(c.H_part)])
    yield HeadNorm(c, [([Q[:, h, CTX:T1]], SEQ, c.s("ones"), P, [c.s("qn_g")], None) for h in range(8)]
                   + [([K[:, h, :]], T1, c.s("ones"), P, [c.s("kn_g")], None) for h in range(2)],
                   QK_EPS, m["s"], m["p"])
    yield Rope(c, [Q[:, h, CTX:T1] for h in range(8)] + [K[:, h, CTX:T1] for h in range(2)], 128, m["s"])
    items = [dict(rows=P, keys=T1, scale=P ** -0.5, maps=[[(Q[:, h, t0:t0 + P], K[:, h // 4, :])]],
                  values=[(b * P, P, V[:, b, (h // 4) * P:(h // 4 + 1) * P]) for b in range(4)],
                  out_rows=(0, P), out=OT[:, h, t0:t0 + P])
             for h in range(8) for t0 in (256, 384)]
    yield Attention(c, items, m["p"], m["s"], m["pT"], m["col"])
    yield Project(c, OT, [columns(d["w_out_odd"], s * WIDE) for s in range(4)], feature_items(c.ACC, range(4), CTX, SEQ),
                  m["OT_parts"])
    yield LayerNorm(c, 1, 0, [(1, CTX)], (1, 3))
    yield from experts(c, 1, CTX, SEQ)
    yield LayerNorm(c, 1, 1, [(1, CTX)], None, shift_to=META)


def experts(c, layer, t0, tn):
    d = c.dram
    nt = tn // P
    m = c.carve({"sc": (4, 16), "sel": (4, 16), "ta": (4, 16), "tb": (4, 16), "g": (4, 16), "b": (nt, 16),
                 "place": (nt, 16), "hi": (16, 2), "lo": (16, 2), "gs": (3, 16), "mx": (4,), "rows": (2, 512)})
    yield Router(c, t0, tn, m)

    def rows(name):
        w = d[name][layer].rearrange("e k m -> (e k) m")

        def src(offset, half):
            return w[bass.ds(offset(D), D), half * WIDE:(half + 1) * WIDE].rearrange("(k p) m -> p k m", p=P)
        return src

    def down(offset, half):
        w = d["w_down"][layer].rearrange("e k m -> (e k) m")
        return w[bass.ds(offset(D_EXPERT) + half * WIDE, WIDE), :].rearrange("(k p) m -> p k m", p=P)

    yield Experts(c, t0, tn, 2 * EXPERTS, rows("w_gate"), rows("w_up"), down, gates=layer + 1)


def swiglu(c, layer):
    d = c.dram
    w, wd = d["w_gate_up_2"][layer], d["w_down_2"][layer]

    def cols(base):
        def src(offset, half):
            return w[:, bass.ds(offset(2 * WIDE) + (base + half * WIDE), WIDE)].rearrange("(k p) m -> p k m", p=P)
        return src

    def down(offset, half):
        return wd[bass.ds(offset(2 * WIDE) + half * WIDE, WIDE), :].rearrange("(k p) m -> p k m", p=P)

    yield FeedForward(c, 0, T2, D_FF // WIDE, cols(0), cols(D_FF), down)


def fox(c, j):
    d = c.dram
    m = c.carve({"Q": (8, T2), "K": (8, T2), "V": (3, 1024), "G": (8, T2), "OT": (8, T2), "z": (3, 16), "w": (3, 16),
                 "lf": (3, 16), "C": (3, 16), "CT": (T2,), "p": (4, 512), "s": (4, 512), "pT": (2, 512), "col": (4, 8)})
    Q, K, V, OT = m["Q"], m["K"], m["V"], m["OT"]
    w = d["fox_w_in"][j]
    gate = [(12 + n // 2, "feature", (n % 2) * P, P, 0, T2,
             (lambda dst: lambda act, ps: act.activation(dst, ps, ACT.Sigmoid))(m["G"][:, n, :])) for n in range(8)]
    yield Project(c, c.H, [columns(w, s * WIDE) for s in range(16)],
                  feature_items(Q, range(4), 0, T2) + feature_items(K, range(4, 8), 0, T2)
                  + token_items(V, range(8, 12), TILES2) + gate, c.H_parts)
    yield LogForget(c, c.s("fox_wf").rearrange("p (j k e) -> p j k e", j=2, k=KC)[:, j], c.s("fox_bf")[:, j * 16:(j + 1) * 16], m)
    yield HeadNorm(c, [([Q[:, n, :]], T2, c.s("ones64"), 64, [c.s("fox_qg")[:, j:j + 1]], None) for n in range(8)],
                   NORM_EPS, m["s"], m["p"], after=64 ** -0.5)
    yield HeadNorm(c, [([K[:, n, :]], T2, c.s("ones64"), 64, [c.s("fox_kg")[:, j:j + 1]], None) for n in range(8)],
                   NORM_EPS, m["s"], m["p"])
    items = []
    for h in range(16):
        r = 64 * (h % 2)
        R = slice(r, r + 64)
        for t, (t0, tn) in enumerate(TILES2):
            keys = t0 + tn
            minus_c = (c.s("ident", 16)[:, h:h + 1].to_broadcast([16, tn]), m["CT"][0:16, 0:keys])
            items.append(dict(
                rows=tn, keys=keys, scale=1.0, maps=[[(Q[R, h // 2, t0:t0 + tn], K[R, h // 2, 0:keys]), minus_c]],
                qbias=m["C"][0:tn, t, h:h + 1], masks=[(c.s("causal")[0:tn, 0:tn], t0, keys)],
                values=[(TILES2[b][0], TILES2[b][1], V[0:TILES2[b][1], b, h * 64:(h + 1) * 64]) for b in range(t + 1)],
                out_rows=(r, 64), out=OT[R, h // 2, t0:t0 + tn]))
    yield Attention(c, items, m["p"], m["s"], m["pT"], m["col"])
    yield Multiply(c, OT, m["G"])
    yield Project(c, OT, [columns(d["fox_w_out"][j], s * WIDE) for s in range(4)], feature_items(c.ACC, range(4), 0, T2),
                  m["OT_parts"])


def silu_items(dst, slots):
    return [(s, "feature", m * P, P, 0, T2, (lambda x: lambda act, ps: act.activation(x, ps, ACT.Silu))(dst[:, 2 * n + m, :]))
            for n, s in enumerate(slots) for m in range(2)]


def gla(c):
    d = c.dram
    m = c.carve({"Q": (4, T2), "K": (4, T2), "V": (3, 1024), "R": (8, T2), "OT": (8, T2), "b": (4, T2), "e": (4, T2),
                 "g": (4, T2), "q0": (4, T2), "k0": (4, T2), "q1": (4, T2), "k1": (4, T2), "one": (P,), "lr": (T2,),
                 "A0": (4, META), "S": (4, 256), "kT": (4, P), "ebl": (4,), "last": (4,), "A": (8, P),
                 })
    m["q"], m["k"] = [m["q0"], m["q1"]], [m["k0"], m["k1"]]
    m["A"] = m["A"].rearrange("p (a h) t -> p a h t", a=2)
    w = d["gla_w_in"]
    yield Project(c, c.H, [columns(w, s * WIDE) for s in range(12)],
                  feature_items(m["Q"], [0, 1], 0, T2, scale=P ** -0.5) + feature_items(m["K"], [2, 3], 0, T2)
                  + token_items(m["V"], range(4, 8), TILES2) + silu_items(m["R"], range(8, 12)), c.H_parts)
    yield GlaGates(c, m)
    yield GlaScores(c, m)
    yield GlaOutput(c, m)
    OT = m["OT"]
    og = c.s("gla_og")
    yield HeadNorm(c, [([OT[:, 2 * h, :], OT[:, 2 * h + 1, :]], T2, c.s("ones"), 256, [og[:, 0:1], og[:, 1:2]], None)
                       for h in range(4)], NORM_EPS, m["e"], m["g"])
    yield Multiply(c, OT, m["R"])
    yield Project(c, OT, [columns(d["gla_w_out"], s * WIDE) for s in range(4)], feature_items(c.ACC, range(4), 0, T2),
                  m["OT_parts"])


def gdn(c):
    d = c.dram
    m = c.carve({"pre": (24, 3 + T2), "G": (8, T2), "OT": (8, T2), "BB": (8, T2), "KB": (8, T2),
                 "a": (3, 8), "w": (3, 8), "g": (3, 8), "b": (3, 8), "beta": (3, 8), "bT": (T2,), "betaT": (T2,),
                 "alog": (8,), "bl": (8,)}, reserve=6 * 1024)
    m["Q"], m["K"], m["V"] = (m["pre"][:, 8 * j:8 * j + 8, :] for j in range(3))
    m["QE"], m["EB"], m["KBE"] = m["OT"], c.ACC[:, :, 0:T2], c.H[:, :, 0:T2]
    m["Xm"], m["LT"], m["XT"] = (x[:, :, T2:T2 + P] for x in (c.X, c.H, c.ACC))
    m["VB"], m["KD"], m["U"], m["AT"] = (c.ext[:, j] for j in range(4))
    m["VN"], m["BT"] = m["VB"], c.ext[:, 4:6]
    m["S"] = c.stat[:].rearrange("p a (h t) -> p (a h) t", h=4)
    w = d["gdn_w_in"]
    items = [(n // 2, "feature", (n % 2) * P, P, 0, T2, move_to(m["pre"][:, n, 3:3 + T2])) for n in range(24)]
    yield Zero(c, m["pre"][:, :, 0:3])
    yield Project(c, c.H, [columns(w, s * WIDE) for s in range(16)], items + silu_items(m["G"], range(12, 16)),
                  c.H_parts)
    tmp = c.ext[:, 0:2].rearrange("p a h t -> p (a h t)")[:, 0:4 * T2].rearrange("p (i t) -> p i t", i=4)
    yield Convolve(c, m["pre"], tmp)
    tmp2 = c.ext[:, 2:4].rearrange("p a h t -> p (a h t)")[:, 0:4 * T2].rearrange("p (i t) -> p i t", i=4)
    for j, after in ((0, P ** -0.5), (1, 1.0)):
        yield HeadNorm(c, [([m["pre"][:, 8 * j + h, 3:3 + T2]], T2, c.s("ones"), 1.0, None, after) for h in range(8)],
                       NORM_EPS, tmp, tmp2)
    yield GdnGates(c, m)
    for t in range(3):
        yield GdnChunk(c, m, t)
    OT = m["OT"]
    yield HeadNorm(c, [([OT[:, h, :]], T2, c.s("ones"), P, [c.s("gdn_og")], None) for h in range(8)],
                   NORM_EPS, tmp, tmp2)
    yield Multiply(c, OT, m["G"])
    yield Project(c, OT, [columns(d["gdn_w_out"], s * WIDE) for s in range(4)], feature_items(c.ACC, range(4), 0, T2),
                  m["OT_parts"])


def second_stack(c):
    for i, mixer in enumerate((lambda: fox(c, 0), lambda: gla(c), lambda: gdn(c), lambda: fox(c, 1))):
        yield RmsNorm(c, c.s("norm_mix")[:, i * 8:(i + 1) * 8], add=(i > 0))
        yield from mixer()
        yield RmsNorm(c, c.s("norm_ffn")[:, i * 8:(i + 1) * 8], add=True)
        yield from swiglu(c, i)
    yield Store(c)


def build(nc, dram, values, limit=None):
    with ExitStack() as ctx:
        core = Core(nc, ctx, dram, values)
        stages = list(first_stack(core)) + list(second_stack(core))
        if limit:
            stages = stages[:limit]
        block = ctx.enter_context(nc.Block())

        def run(eng, part):
            for n, stage in enumerate(stages):
                if n:
                    eng.wait_ge(core.stage_done, 3 * n)
                part(stage, eng)
                eng.drain().then_inc(core.stage_done, 1)

        @block.sync
        def _(sp):
            for stage in stages:
                stage.sync(sp)

        @block.tensor
        def _(pe):
            run(pe, lambda stage, eng: stage.tensor(eng))

        @block.scalar
        def _(act):
            run(act, lambda stage, eng: stage.scalar(eng))

        @block.vector
        def _(dve):
            run(dve, lambda stage, eng: stage.vector(eng))
        return stages


WEIGHTS = {"w_mod": "w_mod", "w_in_even": "w_in_even", "w_out_even": "w_out_even", "w_in_odd": "w_in_odd",
           "w_out_odd": "w_out_odd", "w_gate": "w_gate", "w_up": "w_up", "w_down": "w_down",
           "w_gate_up_2": "w_gate_up_2", "w_down_2": "w_down_2", "fox_w_in": "fox_w_in_2", "fox_w_out": "fox_w_out_2",
           "gla_w_in": "gla_w_in_2", "gla_w_out": "gla_w_out_2", "gdn_w_in": "gdn_w_in_2", "gdn_w_out": "gdn_w_out_2"}
ONE_LAYER = ("w_in_even", "w_out_even", "w_in_odd", "w_out_odd", "gla_w_in", "gla_w_out", "gdn_w_in", "gdn_w_out")


def lay_out(inputs):
    x = {k: np.asarray(v) for k, v in inputs.items()}
    arrays = {}
    for name, key in WEIGHTS.items():
        a = x[key]
        arrays[name] = np.ascontiguousarray(a[0] if name in ONE_LAYER else a)

    def chunked(a):
        a = a.reshape(a.shape[:-1] + (-1, P))
        return np.moveaxis(a, -1, 0).reshape(P, -1)

    def features(a):
        return a.reshape(-1, P, a.shape[-1]).transpose(1, 0, 2).reshape(P, -1)

    def rows(a):
        return np.broadcast_to(a.reshape(1, -1), (P, a.size))

    tokens = np.concatenate([x["ctx"][0], x["x"][0]], 0)
    arrays["xT"] = np.ascontiguousarray(tokens.T.reshape(KC, P, T1).transpose(1, 0, 2))
    w2 = np.zeros((P, 512), np.float32)
    w2[:16] = x["gla_w_alpha2_2"][0]
    small = {
        "cond": features(np.stack([x["c_ctx"], x["c"][0]], 1)), "b_mod": chunked(x["b_mod"]),
        "ln_g": chunked(x["ln_g"]), "ln_b": chunked(x["ln_b"]), "norm_mix": chunked(x["norm_mix_2"]),
        "norm_ffn": chunked(x["norm_ffn_2"]), "meta": features(x["meta_tokens_2"].T),
        "w_router": features(x["w_router"]), "b_router": rows(x["b_router"]), "sink": rows(x["sink_logits"]),
        "lam": rows(np.concatenate([x["lam_q1"], x["lam_k1"], x["lam_q2"], x["lam_k2"]])),
        "subln_g": x["subln_g"].T, "qn_g": x["q_norm_g"].T, "kn_g": x["k_norm_g"].T,
        "fox_wf": np.concatenate([features(x["fox_w_in_2"][j][:, 4 * D:]) for j in range(2)], 1),
        "fox_bf": rows(x["fox_b_f_2"]), "fox_qg": np.tile(x["fox_q_gain_2"].T, (2, 1)),
        "fox_kg": np.tile(x["fox_k_gain_2"].T, (2, 1)),
        "gla_wa": features(x["gla_w_in_2"][0][:, 3072:]), "gla_w2": w2, "gla_ba": chunked(x["gla_b_alpha_2"]),
        "gla_og": chunked(x["gla_o_gain_2"]),
        "gdn_wab": features(x["gdn_w_in_2"][0][:, 4096:]), "gdn_conv": chunked(x["gdn_conv_w_2"]),
        "gdn_alog": rows(x["gdn_a_log_2"]), "gdn_dt": rows(x["gdn_dt_bias_2"]), "gdn_og": x["gdn_o_gain_2"].T,
    }
    small.update(shape_constants())
    parts = []
    for name, cols in SMALL_COLS:
        assert small[name].shape == (P, cols), (name, small[name].shape)
        parts.append(small[name])
    arrays["small"] = np.concatenate(parts, 1)
    return arrays


def program(nc, arrays, numbers, limit=None):
    dram = {name: nc.dram_tensor(f"in_{name}", a.shape, F32, kind="ExternalInput").ap() for name, a in arrays.items()}
    dram["routes"] = nc.dram_tensor("routes", (EXPERTS, 2, T1), F32, kind="Internal").ap()
    dram["outT"] = nc.dram_tensor("out_xT", (D, SEQ), F32, kind="ExternalOutput").ap()
    build(nc, dram, numbers, limit)


def kernel(**inputs):
    import concourse.bacc as bacc
    from concourse.bass_utils import run_bass_kernel_spmd as run

    arrays = lay_out(inputs)
    numbers = {}
    for _ in range(2):
        nc = bacc.Bacc("TRN2", target_bir_lowering=False, num_devices=1)
        program(nc, arrays, numbers)
    r = run(nc, [{f"in_{name}": a for name, a in arrays.items()}], core_ids=[0])
    return np.ascontiguousarray(r.results[0]["out_xT"].T)[None]
```
